# Optimizing a Trainium2 kernel written in Bass

```python
import math
import jax
import jax.numpy as jnp
from jax import lax
import numpy as np

D_MODEL = 1024
BATCH = 1
SEQ = 128
DEPTH = 2
DEC_BATCH = 1
DEC_SEQ = 1024
PAST_LEN = 128

GRID_W = 64
N_BRANCH = 3
NA_HEADS = 8
NA_HEAD_DIM = 64
NA_WIDTH = NA_HEADS * NA_HEAD_DIM
NA_WIN_ROWS = 8
NA_WIN_COLS = 16
FNET_GROUPS = 4
FNET_GROUP_DIM = 128
FNET_WIDTH = FNET_GROUPS * FNET_GROUP_DIM
DIFF_HEADS = 4
DIFF_QK_DIM = 64
DIFF_V_DIM = 2 * DIFF_QK_DIM
DIFF_WIDTH = DIFF_HEADS * DIFF_V_DIM
BRANCH_WIDTH = 512
IN_WIDTH = 4 * NA_WIDTH + 2 * FNET_WIDTH + 4 * DIFF_WIDTH + N_BRANCH * D_MODEL
ROPE_BASE = 10000.0
EPS = 1e-6
Q_BLOCK = 128
NEG_INF = -1e30

kernel_name = "hybrid_diffusion_na_fnet_diffattn_step"

F32 = jnp.float32

def rmsnorm(x, g):
    xf = x.astype(F32)
    y = xf * lax.rsqrt(jnp.mean(xf * xf, axis=-1, keepdims=True) + EPS)
    return (y * g.astype(F32)).astype(x.dtype)

def adaln(cvec, w_mod, b_mod):
    mod = jax.nn.silu(cvec) @ w_mod + b_mod
    mod = mod.reshape(-1, 1, 3 * D_MODEL)
    return jnp.split(mod, 3, axis=-1)

def split_projection(p):
    sizes = [NA_WIDTH] * 4 + [FNET_WIDTH] * 2 + [DIFF_WIDTH] * 4 + [N_BRANCH * D_MODEL]
    offs = [int(o) for o in np.cumsum(sizes)[:-1]]
    return jnp.split(p, offs, axis=-1)

def to_heads(x, n_heads):
    B, T, _ = x.shape
    return x.reshape(B, T, n_heads, -1).transpose(0, 2, 1, 3)

def from_heads(x):
    B, H, T, d = x.shape
    return x.transpose(0, 2, 1, 3).reshape(B, T, H * d)

def diff_qk_heads(x):
    B, T, _ = x.shape
    return x.reshape(B, T, DIFF_HEADS, 2, DIFF_QK_DIM).transpose(0, 2, 1, 3, 4)

def axial_rope_tables(T, dtype):
    t = jnp.arange(T)
    row = (t // GRID_W).astype(F32)
    col = (t % GRID_W).astype(F32)
    half = DIFF_QK_DIM // 2
    inv = ROPE_BASE ** (-jnp.arange(0, half, 2, dtype=F32) / half)
    ang_r = row[:, None] * inv
    ang_c = col[:, None] * inv
    return tuple(a.astype(dtype) for a in (jnp.cos(ang_r), jnp.sin(ang_r), jnp.cos(ang_c), jnp.sin(ang_c)))

def rope_1d(x, cos, sin):
    x1, x2 = jnp.split(x, 2, axis=-1)
    return jnp.concatenate([x1 * cos - x2 * sin, x2 * cos + x1 * sin], axis=-1)

def apply_axial_rope(x, tables):
    cr, sr, cc, sc = (a[:, None, :] for a in tables)
    xr, xc = jnp.split(x, 2, axis=-1)
    return jnp.concatenate([rope_1d(xr, cr, sr), rope_1d(xc, cc, sc)], axis=-1)

def map_query_blocks(fn, q):
    B, H, T = q.shape[:3]
    nb = T // Q_BLOCK
    qb = jnp.moveaxis(q.reshape(B, H, nb, Q_BLOCK, *q.shape[3:]), 2, 0)
    o = lax.map(fn, qb)
    o = jnp.moveaxis(o, 0, 2)
    return o.reshape(B, H, T, o.shape[-1])

def softmax_attention(q, k, v):
    scale = q.shape[-1] ** -0.5

    def block(qb):
        s = jnp.einsum('bhqd,bhkd->bhqk', qb, k).astype(F32) * scale
        p = jax.nn.softmax(s, axis=-1).astype(v.dtype)
        return jnp.einsum('bhqk,bhkd->bhqd', p, v)

    return map_query_blocks(block, q)

def neighbourhood_attention(q, k, v, k_ctx, v_ctx, rpb):
    B, H, T, dh = q.shape
    rows = T // GRID_W
    wr = min(NA_WIN_ROWS, rows)
    wc = NA_WIN_COLS
    scale = dh ** -0.5
    r = jnp.arange(rows)
    row_start = jnp.clip(r - wr // 2, 0, rows - wr)
    key_rows = row_start[:, None] + jnp.arange(wr)[None, :]
    c = jnp.arange(GRID_W)
    col_start = jnp.clip(c - wc // 2, 0, GRID_W - wc)
    col_ok = (c[None, :] >= col_start[:, None]) & (c[None, :] < col_start[:, None] + wc)
    dr_idx = key_rows - r[:, None] + NA_WIN_ROWS - 1
    dc_idx = jnp.clip(c[None, :] - c[:, None] + wc - 1, 0, 2 * wc - 2)
    bias = rpb[:, dr_idx[:, None, :, None], dc_idx[None, :, None, :]].astype(F32)

    qg = q.reshape(B, H, rows, GRID_W, dh)
    kg = k.reshape(B, H, rows, GRID_W, dh)[:, :, key_rows]
    vg = v.reshape(B, H, rows, GRID_W, dh)[:, :, key_rows]
    s_loc = jnp.einsum('bhrqd,bhriwd->bhrqiw', qg, kg).astype(F32) * scale + bias[None]
    s_loc = jnp.where(col_ok[None, None, None, :, None, :], s_loc, NEG_INF)
    s_loc = s_loc.reshape(B, H, rows, GRID_W, wr * GRID_W)
    s_ctx = jnp.einsum('bhrqd,bhnd->bhrqn', qg, k_ctx).astype(F32) * scale
    p = jax.nn.softmax(jnp.concatenate([s_loc, s_ctx], axis=-1), axis=-1).astype(v.dtype)
    p_loc = p[..., :wr * GRID_W].reshape(B, H, rows, GRID_W, wr, GRID_W)
    p_ctx = p[..., wr * GRID_W:]
    o = jnp.einsum('bhrqiw,bhriwd->bhrqd', p_loc, vg) + jnp.einsum('bhrqn,bhnd->bhrqd', p_ctx, v_ctx)
    return o.reshape(B, H, T, dh)

def diff_lambda(lq1, lk1, lq2, lk2, lam_init):
    return (jnp.exp(jnp.sum(lq1.astype(F32) * lk1.astype(F32)))
            - jnp.exp(jnp.sum(lq2.astype(F32) * lk2.astype(F32))) + lam_init)

def diff_attention(q, k, v, lam, subln_g, lam_init):
    scale = DIFF_QK_DIM ** -0.5

    def block(qb):
        s = jnp.einsum('bhqmd,bhkmd->bhmqk', qb, k).astype(F32) * scale
        p = jax.nn.softmax(s, axis=-1)
        a = (p[:, :, 0] - lam * p[:, :, 1]).astype(v.dtype)
        return jnp.einsum('bhqk,bhkd->bhqd', a, v)

    o = map_query_blocks(block, q)
    return rmsnorm(o, subln_g) * (1.0 - lam_init)

def fourier_mix(u, w_f):
    B, T, _ = u.shape
    ug = u.astype(F32).reshape(B, T, FNET_GROUPS, FNET_GROUP_DIM)
    f = jnp.fft.fftn(ug, axes=(1, 3), norm="ortho").real.astype(u.dtype).reshape(B, T, FNET_WIDTH)
    return f @ w_f

def merge_branches(gate_logits, outs, zs, w_branch_l, w_out_l):
    g = jax.nn.sigmoid(gate_logits)
    y = 0.0
    for b in range(N_BRANCH):
        gb = g[..., b * D_MODEL:(b + 1) * D_MODEL]
        y = y + gb * ((outs[b] * jax.nn.silu(zs[b])) @ w_branch_l[b])
    return y @ w_out_l

def mixer_input(x, cvec, norm_g, w_mod, b_mod, w_in):
    shift, scale, gate = adaln(cvec, w_mod, b_mod)
    h = rmsnorm(x, norm_g) * (1.0 + scale) + shift
    return gate, split_projection(h @ w_in)

def setup_inputs(seed: int = 0) -> dict:
    key = jax.random.key(seed)
    ks = jax.random.split(key, 24)
    n = jax.random.normal
    D = D_MODEL
    return {
        "x_prompt": n(ks[0], (BATCH, SEQ, D), F32),
        "x_sample": n(ks[1], (DEC_BATCH, DEC_SEQ, D), F32),
        "cache_na_k": n(ks[2], (DEC_BATCH, DEPTH, NA_HEADS, PAST_LEN, NA_HEAD_DIM), F32),
        "cache_na_v": n(ks[3], (DEC_BATCH, DEPTH, NA_HEADS, PAST_LEN, NA_HEAD_DIM), F32),
        "cache_diff_k": n(ks[4], (DEC_BATCH, DEPTH, DIFF_HEADS, PAST_LEN, 2 * DIFF_QK_DIM), F32),
        "cache_diff_v": n(ks[5], (DEC_BATCH, DEPTH, DIFF_HEADS, PAST_LEN, DIFF_V_DIM), F32),
        "c": n(ks[6], (DEC_BATCH, D), F32),
        "c_ctx": n(ks[7], (D,), F32),
        "norm_g": 1.0 + 0.02 * n(ks[8], (DEPTH, D), F32),
        "w_mod": 0.5 * D ** -0.5 * n(ks[9], (DEPTH, D, 3 * D), F32),
        "b_mod": 0.01 * n(ks[10], (DEPTH, 3 * D), F32),
        "w_in": D ** -0.5 * n(ks[11], (DEPTH, D, IN_WIDTH), F32),
        "na_rpb": 0.1 * n(ks[12], (DEPTH, NA_HEADS, 2 * NA_WIN_ROWS - 1, 2 * NA_WIN_COLS - 1), F32),
        "fnet_w": FNET_WIDTH ** -0.5 * n(ks[13], (DEPTH, FNET_WIDTH, FNET_WIDTH), F32),
        "diff_lq1": 0.1 * n(ks[14], (DEPTH, DIFF_QK_DIM), F32),
        "diff_lk1": 0.1 * n(ks[15], (DEPTH, DIFF_QK_DIM), F32),
        "diff_lq2": 0.1 * n(ks[16], (DEPTH, DIFF_QK_DIM), F32),
        "diff_lk2": 0.1 * n(ks[17], (DEPTH, DIFF_QK_DIM), F32),
        "diff_subln_g": 1.0 + 0.02 * n(ks[18], (DEPTH, DIFF_V_DIM), F32),
        "w_branch": BRANCH_WIDTH ** -0.5 * n(ks[19], (DEPTH, N_BRANCH, BRANCH_WIDTH, D), F32),
        "w_out": D ** -0.5 * n(ks[20], (DEPTH, D, D), F32),
        "final_g": 1.0 + 0.02 * n(ks[21], (D,), F32),
    }

def reference(x_prompt, x_sample, cache_na_k, cache_na_v, cache_diff_k, cache_diff_v, c, c_ctx,
              norm_g, w_mod, b_mod, w_in, na_rpb, fnet_w, diff_lq1, diff_lk1, diff_lq2, diff_lk2,
              diff_subln_g, w_branch, w_out, final_g):
    xp = x_prompt
    Bp, N = xp.shape[0], xp.shape[1]
    na_ks, na_vs, d_ks, d_vs = [], [], [], []
    for l in range(DEPTH):
        lam_init = 0.8 - 0.6 * math.exp(-0.3 * l)
        lam = diff_lambda(diff_lq1[l], diff_lk1[l], diff_lq2[l], diff_lk2[l], lam_init)
        gate, (na_q, na_k, na_v, na_z, f_u, f_z, d_q, d_k, d_v, d_z, g) = mixer_input(
            xp, c_ctx, norm_g[l], w_mod[l], b_mod[l], w_in[l])
        qa, ka, va = to_heads(na_q, NA_HEADS), to_heads(na_k, NA_HEADS), to_heads(na_v, NA_HEADS)
        o_na = from_heads(softmax_attention(qa, ka, va))
        o_f = fourier_mix(f_u, fnet_w[l])
        qd, kd, vd = diff_qk_heads(d_q), diff_qk_heads(d_k), to_heads(d_v, DIFF_HEADS)
        o_d = from_heads(diff_attention(qd, kd, vd, lam, diff_subln_g[l], lam_init))
        y = merge_branches(g, (o_na, o_f, o_d), (na_z, f_z, d_z), w_branch[l], w_out[l])
        xp = xp + gate * y
        na_ks.append(ka)
        na_vs.append(va)
        d_ks.append(kd.reshape(Bp, DIFF_HEADS, N, 2 * DIFF_QK_DIM))
        d_vs.append(vd)
    y_prompt = rmsnorm(xp, final_g)
    new_na_k = jnp.stack(na_ks, axis=1)
    new_na_v = jnp.stack(na_vs, axis=1)
    new_diff_k = jnp.stack(d_ks, axis=1)
    new_diff_v = jnp.stack(d_vs, axis=1)

    xs = x_sample
    Bs, T = xs.shape[0], xs.shape[1]
    Nc = cache_diff_k.shape[3]
    tables = axial_rope_tables(T, xs.dtype)
    for l in range(DEPTH):
        lam_init = 0.8 - 0.6 * math.exp(-0.3 * l)
        lam = diff_lambda(diff_lq1[l], diff_lk1[l], diff_lq2[l], diff_lk2[l], lam_init)
        gate, (na_q, na_k, na_v, na_z, f_u, f_z, d_q, d_k, d_v, d_z, g) = mixer_input(
            xs, c, norm_g[l], w_mod[l], b_mod[l], w_in[l])
        qa, ka, va = to_heads(na_q, NA_HEADS), to_heads(na_k, NA_HEADS), to_heads(na_v, NA_HEADS)
        o_na = from_heads(neighbourhood_attention(qa, ka, va, cache_na_k[:, l], cache_na_v[:, l], na_rpb[l]))
        o_f = fourier_mix(f_u, fnet_w[l])
        qd = apply_axial_rope(diff_qk_heads(d_q), tables)
        kd = apply_axial_rope(diff_qk_heads(d_k), tables)
        vd = to_heads(d_v, DIFF_HEADS)
        k_ctx = cache_diff_k[:, l].reshape(Bs, DIFF_HEADS, Nc, 2, DIFF_QK_DIM)
        k_all = jnp.concatenate([kd, k_ctx], axis=2)
        v_all = jnp.concatenate([vd, cache_diff_v[:, l]], axis=2)
        o_d = from_heads(diff_attention(qd, k_all, v_all, lam, diff_subln_g[l], lam_init))
        y = merge_branches(g, (o_na, o_f, o_d), (na_z, f_z, d_z), w_branch[l], w_out[l])
        xs = xs + gate * y
    y_sample = rmsnorm(xs, final_g)
    return (y_prompt, y_sample, new_na_k, new_na_v, new_diff_k, new_diff_v)


_drawn_inputs = setup_inputs


def setup_inputs(seed=0):
    import zlib

    import numpy as np

    out = dict(_drawn_inputs(seed))
    spreads = {}
    factors = {'cache_na_k': 6.031,
     'cache_na_v': 5.075,
     'cache_diff_k': 4.796,
     'cache_diff_v': 4.496,
     'norm_g': 2.93,
     'b_mod': 4.14,
     'na_rpb': 39.32,
     'diff_lq1': 4.379,
     'diff_lk1': 5.297,
     'diff_lq2': 4.386,
     'diff_lk2': 6.101,
     'diff_subln_g': 8.0,
     'final_g': 7.519}
    for name, (base, spread) in spreads.items():
        noise = np.random.default_rng([zlib.crc32(name.encode()), seed]).standard_normal(out[name].shape)
        drawn = base * np.exp(spread * noise) if base else spread * noise
        out[name] = jnp.asarray(drawn.astype(out[name].dtype))
    for name, factor in factors.items():
        out[name] = (out[name] * factor).astype(out[name].dtype)
    return out
```

```python
import math
from collections import namedtuple

import numpy as np

import concourse.bass as bass
from concourse import mybir

F32 = mybir.dt.float32
F32R = mybir.dt.float32r
ALU = mybir.AluOpType
ACT = mybir.ActivationFunctionType
AX = mybir.AxisListType

P = 128
DEPTH = 2
D = 1024
KT = D // P
TL = 1024
TC = 128
T = TL + TC
TILES = T // P
LT = TL // P
CH = 384
NC = T // CH
PAST = 128
GW = 64
WIN = 8
HEADS = 4
BW = 512
BK = BW // P
EPS = 1e-6

MODS = 3 * KT
NA0, FN0, DF0 = 0, 16, 28
MG0 = DF0 + 16
OUT0 = MG0 + 2 * 3 * KT
SPLITS = OUT0 + KT
CHUNKS = MODS + SPLITS
ROUTES = (["act", "act", "act", "dve"] * HEADS + ["act"] * HEADS + ["dve", "dve"] * HEADS
          + ["act", "act", "act", "dve"] * HEADS + ["act", "dve"] * (3 * KT) + ["dve"] * KT)

S_MIN, S_MAX = -6, 7
I_MIN, I_MAX = -4, 4
NS = S_MAX - S_MIN + 1
NI = I_MAX - I_MIN + 1
PADW = 2 * GW - 1


def window(t):
    rows = TL // GW
    lo = min(max(2 * t - WIN // 2, 0), rows - WIN)
    hi = min(max(2 * t + 1 - WIN // 2, 0), rows - WIN) + WIN
    n = hi - lo
    e = (lo - 2 * t - S_MIN) if n == WIN else NS + (lo - 2 * t - I_MIN)
    return lo, n, e


def na_tiles(t):
    if t == LT:
        return [(0, P, LT)]
    lo, n, _ = window(t)
    nk = n * GW
    tiles = [(P * j, P * j + P, lo // 2 + j) for j in range(4)] + [(nk, nk + PAST, TILES)]
    return tiles + ([(512, nk, lo // 2 + 4)] if nk > 512 else [])


def chunk_k(i):
    fnet = FN0 + HEADS <= i < DF0 and (i - FN0 - HEADS) % 2
    branch = MG0 <= i < OUT0 and (i - MG0) % 2
    return BK if fnet or branch else KT


def build(nc, x_prompt, x_sample, cache_na_k, cache_na_v, cache_diff_k, cache_diff_v, cvec, norm_g, w_mod,
          b_mod, w_in, rpb, fnet_w, lams, subln_g, w_branch, w_out, final_g, na_mask, rope, dft_c, dft_x, dft_t,
          y_prompt, y_sample, new_na_k, new_na_v, new_diff_k, new_diff_v, xs_dram, outs_dram):
    base = (nc.sbuf_base + 31) // 32 * 32
    TB = T * 4

    class Place:

        def __init__(self, at):
            self.at = at

        def __call__(self, name, shape, dtype=F32):
            size = int(np.prod(shape[1:])) * 4
            t = nc.alloc_sbuf_tensor_at(name, shape, dtype, offset=self.at)
            self.at += (size + 31) // 32 * 32
            return t

    keep = Place(base)
    hhi = keep("hhi", [P, KT, T], F32R)
    hlo = keep("hlo", [P, KT, T], F32R)
    wraw = keep("wraw", [P, 2, KT, P])
    whi = keep("whi", [P, 2, KT, P], F32R)
    wlo = keep("wlo", [P, 2, KT, P], F32R)
    ident = keep("ident", [P, P])
    ones = keep("ones", [P, P])
    eps = keep("eps", [P, 1])
    csil = keep("csil", [P, KT, 2])
    gcol = keep("gcol", [P, DEPTH, KT])
    bcol = keep("bcol", [P, DEPTH, MODS])
    subg = keep("subg", [P, DEPTH])
    modr = keep("modr", [P, MODS, 2])
    mul_a = keep("mul_a", [P, KT, 2])
    mul_g = keep("mul_g", [P, KT, 2])
    neglam = keep("neglam", [P, DEPTH])
    lprod = keep("lprod", [P, DEPTH, 2])
    lexp = keep("lexp", [P, DEPTH, 2])
    cth = keep("cth", [P, KT, 2])
    craw = keep("craw", [P, KT, 2])
    y0 = keep.at
    arena0 = y0 + KT * TB

    pl = Place(y0)
    ysum = pl("ysum", [P, KT, T])
    assert pl.at == arena0
    xT = pl("xT", [P, KT, T])
    sq = pl("sq", [P, 2, T])
    rstd = pl("rstd", [P, T])
    tn = pl("tn", [P, 2, T])
    un = pl("un", [P, 2, T])
    assert pl.at <= nc.sbuf_usable_end

    pl = Place(y0)
    xtok = pl("xtok", [P, TILES, D])

    pl = Place(y0)
    qa = pl("qa", [P, T])
    qb = pl("qb", [P, T])
    kT = pl("kT", [P, T + PAST])
    vt = pl("vt", [P, TILES + 1, P])
    ck = pl("ck", [P, P])
    kout = pl("kout", [P, P])
    vT = pl("vT", [P, T])
    th = pl("th", [P, T])
    zs = pl("zs", [P, T])
    obuf = pl("obuf", [P, T])
    stat = pl("stat", [P, 2, 8])
    na_at = pl.at
    bias = pl("bias", [P, 2, NS + NI, GW])
    mask = pl("mask", [P, NS + NI, GW])
    sn = pl("sn", [P, 2, 704])
    pT = pl("pT", [P, 2, 6, P])
    assert pl.at <= nc.sbuf_usable_end
    pl = Place(na_at)
    cosT = pl("cosT", [P, TL])
    sinT = pl("sinT", [P, TL])
    xi = pl("xi", [P, T])
    xr = pl("xr", [P, T])
    xc = pl("xc", [P, T])
    e1 = pl("e1", [P, 3, T])
    e2 = pl("e2", [P, 2, T])
    aT = pl("aT", [P, 2, LT + 1, 2 * P])
    assert pl.at <= nc.sbuf_usable_end

    HK = TL // 4
    pl = Place(y0)
    uT = pl("uT", [P, 2, T])
    fth = pl("fth", [P, T])
    fzs = pl("fzs", [P, T])
    fout = pl("fout", [P, T])
    tab_c = pl("tab_c", [P, 2, P])
    tab_x = pl("tab_x", [P, 2, P])
    tab_t = pl("tab_t", [P, 4, 4, HK + 2])
    xcs = pl("xcs", [P, 4, 2, P])
    xsum = pl("xsum", [P, 4, 2, P])
    xdif = pl("xdif", [P, 4, 2, P])
    xctx = pl("xctx", [P, 2, P])
    qsb = pl("qsb", [P, 2, HK + 2])
    ft = pl("ft", [P, T])
    fhi = pl("fhi", [P, HEADS, T], F32R)
    flo = pl("flo", [P, HEADS, T], F32R)
    assert pl.at <= nc.sbuf_usable_end

    pl = Place(arena0)
    oraw = pl("oraw", [P, BK, T])
    ohi = pl("ohi", [P, BK, T], F32R)
    olo = pl("olo", [P, BK, T], F32R)
    gth = pl("gth", [P, 2, T])
    assert pl.at <= nc.sbuf_usable_end
    pl = Place(arena0 + KT * TB)
    xold = pl("xold", [P, 2, T])

    pl = Place(y0)
    fg = pl("fg", [P, D])
    yb = pl("yb", [P, 2, D])
    junk = pl("junk", [P, D])
    fss = pl("fss", [P, 2, 4])
    pl = Place(y0)
    lamraw = nc.alloc_sbuf_tensor_at("lamraw", [P, DEPTH, 4, 64], F32, offset=base)
    lammul = nc.alloc_sbuf_tensor_at("lammul", [P, DEPTH, 2, 64], F32, offset=base + DEPTH * 4 * 64 * 4)

    ps = nc.alloc_psum_tensor("ps", [P, 8, 512], F32)
    flat = ps[:].rearrange("p b n -> p (b n)")

    def group(g):
        return ps[:, 3 * g:3 * g + NC, 0:CH]

    def by_chunk(ap):
        return ap.rearrange("p (c n) -> p c n", n=CH)

    names = """bar setup_load setup_done xtok_ready xtok_used w_load0 w_load1 w_hi w_lo w_used mod_used mod_ready
        sq_ready ss_used ss_done rstd_ready t_ready u_ready hi_ready h_ready job_done act_evac dve_evac
        th_ready load tables masked tr_ready tr_used rot_in rot_shuf rot_mul rope_done store
        na_s na_b na_e na_p na_pt na_ptc na_pv na_o df_s df_m df_e df_p df_pt df_ptc df_pv df_o f_store
        u_pair pair_copied folded x_done q_done q_copied f_done f_hi f_lo f_ctx
        sqo_ready sso_done rso_ready o_load o_hi o_lo g_ready m_ready y_added x_load0 x_load1 x_new
        fin_tr fin_sq fin_rs fin_y fin_st0 fin_st1""".split()

    S = namedtuple("Semaphores", names)(*[nc.alloc_semaphore(n) for n in names])
    w_load = (S.w_load0, S.w_load1)
    barriers = {}

    def barrier(eng):
        barriers[eng] = barriers.get(eng, 0) + 1
        eng.drain().then_inc(S.bar, 1)
        eng.wait_ge(S.bar, 5 * barriers[eng])

    evacs = {"act": S.act_evac, "dve": S.dve_evac}

    def evacuated(s):
        l, i = divmod(s, SPLITS)
        who = ROUTES[i]
        return evacs[who], l * ROUTES.count(who) + ROUTES[:i + 1].count(who)

    with nc.Block() as block:

        @block.sync
        def _(sp):
            done = {"w": 0, "load": 0, "store": 0, "o": 0}

            def weights_to(c_end):
                while done["w"] < min(c_end, DEPTH * CHUNKS):
                    c = done["w"]
                    if c >= 2:
                        l, i = divmod(c - 2, CHUNKS)
                        if i < MODS:
                            sp.wait_ge(S.mod_used, l * MODS + i + 1)
                        else:
                            sp.wait_ge(S.w_lo, l * SPLITS + i - MODS + 1)
                    l, i = divmod(c, CHUNKS)
                    src, kt = weight(l, i)
                    sp.dma_start(wraw[:, c % 2, 0:kt, :], src).then_inc(w_load[c % 2], 16)
                    done["w"] += 1

            def weight(l, i):
                if i < MODS:
                    return cols(w_mod[l], i), KT
                i -= MODS
                if i < FN0:
                    p, r = divmod(i, 4)
                    return cols(w_in[l], 4 * r + p), KT
                if i < FN0 + HEADS:
                    return cols(w_in[l], 16 + i - FN0), KT
                if i < DF0:
                    m, r = divmod(i - FN0 - HEADS, 2)
                    return (cols(fnet_w[l], m), BK) if r else (cols(w_in[l], 20 + m), KT)
                if i < MG0:
                    h, r = divmod(i - DF0, 4)
                    return cols(w_in[l], 24 + 4 * r + h), KT
                if i < OUT0:
                    bm, r = divmod(i - MG0, 2)
                    b, m = divmod(bm, KT)
                    return (cols(w_branch[l, b], m), BK) if r else (cols(w_in[l], 40 + bm), KT)
                return cols(w_out[l], i - OUT0), KT

            def cols(w, m):
                return w.rearrange("(k p) n -> p k n", p=P)[:, :, m * P:(m + 1) * P]

            def load(out, src):
                sp.dma_start(out, src).then_inc(S.load, 16)
                done["load"] += 1

            def store(out, src):
                sp.dma_start(out, src).then_inc(S.store, 16)
                done["store"] += 1

            for out, src in ((craw[:], cvec), (gcol[:], norm_g), (bcol[:], b_mod), (subg[:], subln_g)):
                sp.dma_start(out, src).then_inc(S.setup_load, 16)
            sp.dma_start(lamraw[:], lams.rearrange("(o a) b c -> o a b c", o=1).broadcast_to([P, DEPTH, 4, 64])
                         ).then_inc(S.setup_load, 16)
            sp.dma_start(xtok[:, 0:LT, :], x_sample[0].rearrange("(t p) d -> p t d", p=P)).then_inc(S.xtok_ready, 16)
            sp.dma_start(xtok[:, LT, :], x_prompt[0]).then_inc(S.xtok_ready, 16)
            weights_to(2)
            barrier(sp)
            for l in range(DEPTH):
                c0 = l * CHUNKS + MODS
                store(xs_dram.rearrange("k p t -> p k t"), xT[:])
                weights_to(c0 + 4)
                sp.wait_ge(S.store, 16 * done["store"])
                barrier(sp)
                for p in range(HEADS):
                    if p == 0:
                        load(mask[:], na_mask)
                    for e in range(2):
                        for u in range(2):
                            for lo, n, at in ((S_MIN, NS, 0), (I_MIN, NI, NS)):
                                r0 = lo - u + WIN - 1
                                load(bias[GW * u:GW * u + GW, e, at:at + n, :], rpb[l, 2 * p + e, :, r0:r0 + n, :])
                    load(ck[:].rearrange("p (h d) -> p h d", h=2),
                         cache_na_k[0, l, 2 * p:2 * p + 2].rearrange("h n d -> n h d"))
                    load(vt[:, TILES, :].rearrange("p (h d) -> p h d", h=2),
                         cache_na_v[0, l, 2 * p:2 * p + 2].rearrange("h n d -> n h d"))
                    weights_to(c0 + NA0 + 4 * p + 4 + 4)
                    barrier(sp)
                    store(new_na_k[0, l, 2 * p:2 * p + 2].rearrange("h n d -> n h d"),
                          kout[:].rearrange("p (h d) -> p h d", h=2))
                    store(new_na_v[0, l, 2 * p:2 * p + 2].rearrange("h n d -> n h d"),
                          vt[:, LT, :].rearrange("p (h d) -> p h d", h=2))
                    sp.wait_ge(S.na_o, 3 * (l * HEADS + p) + 3)
                    store(outs_dram[0, p], obuf[:])
                    sp.wait_ge(S.store, 16 * done["store"])
                    barrier(sp)
                load(tab_c[:], dft_c)
                load(tab_x[:], dft_x)
                load(tab_t[:], dft_t)
                weights_to(c0 + FN0 + HEADS + 3)
                for m in range(HEADS):
                    weights_to(c0 + FN0 + HEADS + 2 * m + 2 + 3)
                    sp.wait_ge(*evacuated(l * SPLITS + FN0 + HEADS + 2 * m + 1))
                    sp.dma_start(outs_dram[1, m], fout[:]).then_inc(S.f_store, 16)
                    sp.wait_ge(S.f_store, 16 * (l * HEADS + m + 1))
                barrier(sp)
                for h in range(HEADS):
                    if h == 0:
                        load(cosT[:], rope[0])
                        load(sinT[:], rope[1])
                    load(ck[:], cache_diff_k[0, l, h])
                    load(vt[:, TILES, :], cache_diff_v[0, l, h])
                    weights_to(c0 + DF0 + 4 * h + 4 + 4)
                    sp.wait_ge(S.store, 16 * done["store"])
                    barrier(sp)
                    store(new_diff_k[0, l, h], kout[:])
                    store(new_diff_v[0, l, h], vt[:, LT, :])
                    sp.wait_ge(S.store, 16 * done["store"])
                    barrier(sp)
                    barrier(sp)
                    store(outs_dram[2, h], obuf[:])
                sp.wait_ge(S.store, 16 * done["store"])
                for b in range(3):
                    sp.dma_start(oraw[:], outs_dram[b].rearrange("k p t -> p k t")).then_inc(S.o_load, 16)
                    weights_to(c0 + MG0 + 2 * KT * (b + 1) + 3)
                    barrier(sp)
                for m in range(KT):
                    if m >= 2:
                        sp.wait_ge(*evacuated(l * SPLITS + OUT0 + m - 2))
                    sp.dma_start(xold[:, m % 2, :], xs_dram[m]).then_inc((S.x_load0, S.x_load1)[m % 2], 16)
                    weights_to(min(c0 + OUT0 + m + 4, (l + 1) * CHUNKS + 2))
                weights_to((l + 1) * CHUNKS + 2)
                barrier(sp)
            sp.dma_start(fg[:], final_g.rearrange("(o d) -> o d", o=1).broadcast_to([P, D])).then_inc(S.load, 16)
            done["load"] += 1
            for t in range(TILES):
                sp.wait_ge(S.fin_y, t + 1)
                out = y_sample[0, t * P:(t + 1) * P, :] if t < LT else y_prompt[0]
                sp.dma_start(out, yb[:, t % 2, :]).then_inc((S.fin_st0, S.fin_st1)[t % 2], 16)
            sp.wait_ge(S.fin_st0, 16 * 5)
            sp.wait_ge(S.fin_st1, 16 * 4)

        NA_LOADS = [1 + 8 + 2] + [8 + 2] * 3
        DF_LOADS = [4, 2, 2, 2]
        LAYER_LOADS = sum(NA_LOADS) + 3 + sum(DF_LOADS)

        def na_loaded(l, p):
            return 16 * (l * LAYER_LOADS + sum(NA_LOADS[:p + 1]))

        def fn_loaded(l):
            return 16 * (l * LAYER_LOADS + sum(NA_LOADS) + 3)

        def df_loaded(l, h):
            return fn_loaded(l) + 16 * sum(DF_LOADS[:h + 1])

        @block.tensor
        def _(pe):
            mm = nc.tensor.matmul

            def job(s, kt, mhi, mlo):
                l, i = divmod(s, SPLITS)
                pe.wait_ge(S.w_lo, s + 1)
                if s >= 2:
                    pe.wait_ge(*evacuated(s - 2))
                for k in range(kt):
                    for a, b in ((whi, mhi), (whi, mlo), (wlo, mhi)):
                        for n in range(NC):
                            x = mm(ps[:, 3 * (s % 2) + n, 0:CH], a[:, s % 2, k, :], b[:, k, n * CH:(n + 1) * CH],
                                   start=(k == 0 and a is whi and b is mhi), stop=(k == kt - 1 and a is wlo))
                x.then_inc(S.job_done, 1)

            def transposed(bank, srcs):
                for j, src in enumerate(srcs):
                    x = nc.tensor.transpose(ps[:, bank, j * P:(j + 1) * P], src, ident[:])
                return x

            def keys_values(n):
                transposed(6, [ck[:], kT[:, TL + PAST:]]).then_inc(S.tr_ready, 1)
                transposed(7, [vT[:, t * P:(t + 1) * P] for t in range(4)]).then_inc(S.tr_ready, 1)
                pe.wait_ge(S.tr_used, 4 * n + 1)
                transposed(6, [vT[:, t * P:(t + 1) * P] for t in range(4, 8)]).then_inc(S.tr_ready, 1)
                pe.wait_ge(S.tr_used, 4 * n + 2)
                transposed(7, [vT[:, LT * P:]]).then_inc(S.tr_ready, 1)

            pe.wait_ge(S.setup_done, 1)
            pe.wait_ge(S.xtok_ready, 32)
            for g in range(2 * TILES):
                t, half = divmod(g, 2)
                if g >= 2:
                    pe.wait_ge(S.xtok_used, g - 1)
                transposed(g % 2, [xtok[:, t, (4 * half + j) * P:(4 * half + j + 1) * P] for j in range(4)]
                           ).then_inc(S.tr_ready, 1)
            barrier(pe)
            for l in range(DEPTH):
                for i in range(MODS):
                    c = l * CHUNKS + i
                    pe.wait_ge(w_load[c % 2], 16 * (c // 2 + 1))
                    for k in range(KT):
                        x = mm(ps[:, 7, 2 * i:2 * i + 2], wraw[:, c % 2, k, :], csil[:, k, :],
                               start=(k == 0), stop=(k == KT - 1))
                    x.then_inc(S.mod_used, 1)
                for m in range(KT):
                    pe.wait_ge(S.sq_ready, l * KT + m + 1)
                    for n in range(NC):
                        x = mm(ps[:, n, 0:CH], ones[:], sq[:, m % 2, n * CH:(n + 1) * CH],
                               start=(m == 0), stop=(m == KT - 1))
                    x.then_inc(S.ss_used, 1)
                pe.wait_ge(S.h_ready, KT * (2 * l + 1))
                barrier(pe)
                for p in range(HEADS):
                    s0 = l * SPLITS + NA0 + 4 * p
                    for r in range(4):
                        job(s0 + r, KT, hhi, hlo)
                    pe.wait_ge(S.load, na_loaded(l, p))
                    pe.wait_ge(*evacuated(s0 + 2))
                    keys_values(l * 2 * HEADS + p)
                    barrier(pe)

                    units = [(t, e) for t in range(TILES) for e in range(2)]
                    u0 = (l * HEADS + p) * len(units)
                    g0 = 3 * (l * HEADS + p)

                    def scores(i):
                        t, e = units[i]
                        q = (qa, qb)[e][:, t * P:(t + 1) * P]
                        bank = 3 * (i % 2)
                        if i >= 2:
                            pe.wait_ge(S.na_b, u0 + i - 1)
                        if t == LT:
                            x = mm(ps[:, bank, 0:P], q, kT[:, TL + PAST:], start=True, stop=True)
                        else:
                            lo, n, _ = window(t)
                            k0, nk = lo * GW, n * GW
                            x = mm(ps[:, bank, :], q, kT[:, k0:k0 + 512], start=True, stop=True)
                            if nk > 512:
                                x = mm(ps[:, bank + 1, 0:nk - 512], q, kT[:, k0 + 512:k0 + nk], start=True, stop=True)
                            x = mm(ps[:, bank + 1, nk - 512:nk - 512 + PAST], q, kT[:, TL:TL + PAST],
                                   start=True, stop=True)
                        x.then_inc(S.na_s, 1)

                    def probs_t(i):
                        t, e = units[i]
                        pe.wait_ge(S.na_p, u0 + i + 1)
                        if i >= 1:
                            pe.wait_ge(S.na_ptc, u0 + i)
                        for j, (c0, c1, _) in enumerate(na_tiles(t)):
                            x = nc.tensor.transpose(ps[0:c1 - c0, 6 + j // 4, (j % 4) * P:(j % 4) * P + P],
                                                    sn[:, i % 2, c0:c1], ident[:])
                        x.then_inc(S.na_pt, 1)

                    def values(i):
                        t, e = units[i]
                        tg = t // 4
                        pe.wait_ge(S.na_ptc, u0 + i + 1)
                        if t % 4 == 0 and e == 0 and tg >= 2:
                            pe.wait_ge(S.na_o, g0 + tg - 1)
                        tiles = na_tiles(t)
                        for j, (c0, c1, vtile) in enumerate(tiles):
                            kk = c1 - c0
                            x = mm(ps[64 * e:64 * e + 64, 2 + 3 * (tg % 2), (t % 4) * P:(t % 4 + 1) * P],
                                   vt[0:kk, vtile, 64 * e:64 * e + 64], pT[0:kk, i % 2, j, :],
                                   start=(j == 0), stop=(j == len(tiles) - 1))
                        x.then_inc(S.na_pv, 1)

                    scores(0)
                    for i in range(len(units)):
                        if i + 1 < len(units):
                            scores(i + 1)
                        if i >= 1:
                            values(i - 1)
                        probs_t(i)
                    values(len(units) - 1)
                    barrier(pe)

                s0 = l * SPLITS + FN0
                pe.wait_ge(S.load, fn_loaded(l))
                job(s0, KT, hhi, hlo)
                for g in range(HEADS):
                    n = l * HEADS + g
                    if g + 1 < HEADS:
                        if g >= 1:
                            pe.wait_ge(S.q_done, 2 * n)
                            pe.wait_ge(S.f_ctx, n)
                        job(s0 + g + 1, KT, hhi, hlo)
                    pe.wait_ge(*evacuated(s0 + g))
                    if g >= 1:
                        pe.wait_ge(S.q_done, 2 * n)
                        pe.wait_ge(S.f_ctx, n)
                    for j in range(5):
                        if j >= 2:
                            pe.wait_ge(S.folded, n * 5 + j - 1)
                        for i, t in enumerate((j, j + 4) if j < 4 else (8,)):
                            x = mm(ps[:, 6 + j % 2, 256 * i:256 * i + 256], uT[:, g % 2, t * P:(t + 1) * P],
                                   tab_c[:].rearrange("p a b -> p (a b)"), start=True, stop=True)
                        x.then_inc(S.u_pair, 1)
                    pe.wait_ge(S.folded, n * 5 + 5)
                    for i, bank in enumerate((3 * (g % 2), 3 * (g % 2) + 1, 3 * (g % 2) + 2, 6)):
                        x_in, part = ((xsum, 0), (xsum, 1), (xdif, 0), (xdif, 1))[i]
                        width = (HK + 1) if i < 2 else HK
                        for j in range(4):
                            x = mm(ps[:, bank, 0:width], x_in[:, j, part, :], tab_t[:, j, i, 0:width],
                                   start=(j == 0), stop=(j == 3))
                        x.then_inc(S.x_done, 1)
                    for i in range(2):
                        x = mm(ps[:, 7, 0:P], xctx[:, i, :], tab_x[:, i, :], start=(i == 0), stop=(i == 1))
                    x.then_inc(S.x_done, 1)
                pe.wait_ge(S.q_done, 2 * (l + 1) * HEADS)
                pe.wait_ge(S.f_ctx, (l + 1) * HEADS)
                for m in range(HEADS):
                    job(s0 + HEADS + 2 * m, KT, hhi, hlo)
                    if m == 0:
                        pe.wait_ge(S.f_lo, (l + 1) * HEADS)
                    job(s0 + HEADS + 2 * m + 1, BK, fhi, flo)
                barrier(pe)

                for h in range(HEADS):
                    s0 = l * SPLITS + DF0 + 4 * h
                    for r in range(4):
                        job(s0 + r, KT, hhi, hlo)
                    pe.wait_ge(S.load, df_loaded(l, h))
                    pe.wait_ge(*evacuated(s0 + 2))
                    pe.wait_ge(S.rope_done, 2 * (l * HEADS + h) + 2)
                    keys_values(l * 2 * HEADS + HEADS + h)
                    barrier(pe)
                    n9 = (l * HEADS + h) * TILES
                    g0 = (l * HEADS + h) * (3 * LT + 1)
                    o0 = (l * HEADS + h) * 5

                    def scores(t, m):
                        q = (qa, qb)[m][:, t * P:(t + 1) * P]
                        if t >= 1:
                            pe.wait_ge(S.df_e, 2 * (n9 + t - 1) + m + 1)
                        if t == LT:
                            x = mm(ps[:, 3 * m, 0:P], q, kT[:, TL + PAST:], start=True, stop=True)
                        else:
                            for b, (k0, k1) in enumerate(((0, 512), (512, 1024), (1024, 1152))):
                                x = mm(ps[:, 3 * m + b, 0:k1 - k0], q, kT[:, k0:k1], start=True, stop=True)
                        x.then_inc(S.df_s, 1)

                    def probs_t(t, g):
                        if g == 0:
                            pe.wait_ge(S.df_p, n9 + t + 1)
                        elif t == LT:
                            return
                        if t or g:
                            pe.wait_ge(S.df_ptc, g0 + 3 * t + g)
                        for j in range(3 if t < LT else 1):
                            kt = 3 * g + j
                            x = nc.tensor.transpose(ps[:, 6, j * P:(j + 1) * P],
                                                    e1[:, t % 3, kt * P:(kt + 1) * P], ident[:])
                        x.then_inc(S.df_pt, 1)

                    def values(pair):
                        last = 3 * 2 * (pair + 1) if pair < 4 else 3 * LT + 1
                        pe.wait_ge(S.df_ptc, g0 + last)
                        if pair >= 1:
                            pe.wait_ge(S.df_o, o0 + pair)
                        w = 2 * P if pair < 4 else P
                        tiles = [*range(LT), TILES] if pair < 4 else [LT]
                        for j, vtile in enumerate(tiles):
                            x = mm(ps[:, 7, 0:w], vt[:, vtile, :], aT[:, pair % 2, j, 0:w],
                                   start=(j == 0), stop=(j == len(tiles) - 1))
                        x.then_inc(S.df_pv, 1)

                    scores(0, 0)
                    scores(0, 1)
                    for t in range(TILES + 1):
                        for g in range(3):
                            if t >= 1:
                                probs_t(t - 1, g)
                            if t + 1 < TILES and g < 2:
                                scores(t + 1, g)
                        if t % 2 == 0 and t >= 2:
                            values(t // 2 - 1)
                    values(4)
                    barrier(pe)
                    n = l * HEADS + h
                    pe.wait_ge(S.sqo_ready, n + 1)
                    for c in range(NC):
                        x = mm(ps[:, c, 0:CH], ones[:], xi[:, c * CH:(c + 1) * CH], start=True, stop=True)
                    x.then_inc(S.sso_done, 1)
                    barrier(pe)

                for b in range(3):
                    for m in range(KT):
                        s = l * SPLITS + MG0 + 2 * (b * KT + m)
                        job(s, KT, hhi, hlo)
                        if m == 0:
                            pe.wait_ge(S.o_lo, l * 3 + b + 1)
                        job(s + 1, BK, ohi, olo)
                    barrier(pe)
                pe.wait_ge(S.h_ready, KT * (2 * l + 2))
                for m in range(KT):
                    job(l * SPLITS + OUT0 + m, KT, hhi, hlo)
                barrier(pe)
            for t in range(TILES):
                if t >= 2:
                    pe.wait_ge(S.fin_y, t - 1)
                for half in range(2):
                    x = transposed(2 * (t % 2) + half, [xT[:, 4 * half + j, t * P:(t + 1) * P] for j in range(4)])
                x.then_inc(S.fin_tr, 1)

        @block.scalar
        def _(act):
            fn = nc.scalar.activation
            split = [0]

            def split_to(s_end):
                while split[0] < s_end:
                    s = split[0]
                    l, i = divmod(s, SPLITS)
                    c = l * CHUNKS + MODS + i
                    kt = chunk_k(i)
                    act.wait_ge(w_load[c % 2], 16 * (c // 2 + 1))
                    if s >= 2:
                        act.wait_ge(S.job_done, s - 1)
                    fn(whi[:, s % 2, 0:kt, :], wraw[:, c % 2, 0:kt, :], ACT.Copy).then_inc(S.w_hi, 1)
                    split[0] += 1

            def token_rows(n):
                n = 2 * TILES + 4 * n
                act.wait_ge(S.tr_ready, n + 1)
                fn(kT[:, TL:TL + PAST], ps[:, 6, 0:P], ACT.Copy)
                fn(kout[:], ps[:, 6, P:2 * P], ACT.Copy).then_inc(S.tr_used, 1)
                act.wait_ge(S.tr_ready, n + 2)
                fn(vt[:, 0:4, :], ps[:, 7, :].rearrange("p (t n) -> p t n", t=4), ACT.Copy).then_inc(S.tr_used, 1)
                act.wait_ge(S.tr_ready, n + 3)
                fn(vt[:, 4:8, :], ps[:, 6, :].rearrange("p (t n) -> p t n", t=4), ACT.Copy).then_inc(S.tr_used, 1)
                act.wait_ge(S.tr_ready, n + 4)
                fn(vt[:, LT, :], ps[:, 7, 0:P], ACT.Copy).then_inc(S.tr_used, 1)

            act.wait_ge(S.setup_load, 16 * 5)
            fn(cth[:], craw[:], ACT.Tanh, scale=0.5).then_inc(S.th_ready, 1)
            act.wait_ge(S.setup_done, 2)
            fn(lexp[:], lprod[:], ACT.Exp).then_inc(S.th_ready, 1)
            barrier(act)
            for l in range(DEPTH):
                for m in range(KT):
                    n = l * KT + m
                    if m >= 2:
                        act.wait_ge(S.ss_used, n - 1)
                    fn(sq[:, m % 2, :], xT[:, m, :], ACT.Square).then_inc(S.sq_ready, 1)
                act.wait_ge(S.ss_used, l * KT + KT)
                fn(by_chunk(rstd[:]), group(0), ACT.Ln, bias=eps[:, 0:1], scale=1.0 / D)
                act.drain()
                fn(rstd[:], rstd[:], ACT.Exp, scale=-0.5).then_inc(S.rstd_ready, 1)
                act.wait_ge(S.mod_ready, l + 1)
                for m in range(KT):
                    n = l * KT + m
                    act.wait_ge(S.t_ready, n + 1)
                    if m >= 2:
                        act.wait_ge(S.h_ready, KT * 2 * l + m - 1)
                    for j, (a, b) in enumerate(((0, TL), (TL, T))):
                        fn(un[:, m % 2, a:b], tn[:, m % 2, a:b], ACT.Identity, bias=modr[:, m, j:j + 1],
                           scale=mul_a[:, m, j:j + 1])
                    act.drain()
                    fn(hhi[:, m, :], un[:, m % 2, :], ACT.Copy).then_inc(S.hi_ready, 1)
                split_to(l * SPLITS + 2)
                barrier(act)
                for p in range(HEADS):
                    s0 = l * SPLITS + NA0 + 4 * p
                    for r in range(4):
                        s = s0 + r
                        split_to(s + 2)
                        g = group(s % 2)
                        act.wait_ge(S.job_done, s + 1)
                        if r == 0:
                            fn(by_chunk(qa[0:64, :]), g[0:64], ACT.Copy, scale=0.125)
                            fn(by_chunk(qb[64:128, :]), g[64:128], ACT.Copy, scale=0.125).then_inc(S.act_evac, 1)
                        if r == 1:
                            fn(by_chunk(kT[:, 0:2 * CH]), g[:, 0:2], ACT.Copy)
                            fn(kT[:, 2 * CH:TL], g[:, 2, 0:TL - 2 * CH], ACT.Copy)
                            fn(kT[:, TL + PAST:], g[:, 2, TL - 2 * CH:], ACT.Copy).then_inc(S.act_evac, 1)
                        if r == 2:
                            fn(by_chunk(vT[:]), g, ACT.Copy).then_inc(S.act_evac, 1)
                        if r == 3:
                            fn(by_chunk(th[:]), g, ACT.Tanh, scale=0.5).then_inc(S.th_ready, 1)
                    token_rows(l * 2 * HEADS + p)
                    split_to(s0 + 6)
                    barrier(act)
                    units = [(t, e) for t in range(TILES) for e in range(2)]
                    u0 = (l * HEADS + p) * len(units)

                    def exps(i):
                        t, e = units[i]
                        nk = P if t == LT else window(t)[1] * GW + PAST
                        act.wait_ge(S.na_b, u0 + i + 1)
                        fn(sn[:, i % 2, 0:nk], sn[:, i % 2, 0:nk], ACT.Exp, bias=stat[:, i % 2, 2:3],
                           accum_out=stat[:, i % 2, 3:4]).then_inc(S.na_e, 1)

                    def copies(i):
                        t, e = units[i]
                        act.wait_ge(S.na_pt, u0 + i + 1)
                        if i >= 2:
                            act.wait_ge(S.na_pv, u0 + i - 1)
                        tiles = na_tiles(t)
                        full = [x for x in tiles if x[1] - x[0] == P]
                        n4 = min(len(full), 4)
                        last = fn(pT[:, i % 2, 0:n4, :], ps[:, 6, 0:n4 * P].rearrange("p (t n) -> p t n", n=P), ACT.Copy)
                        if len(full) > 4:
                            last = fn(pT[:, i % 2, 4, :], ps[:, 7, 0:P], ACT.Copy)
                        if len(tiles) > len(full):
                            last = fn(pT[0:64, i % 2, 5, :], ps[0:64, 7, P:2 * P], ACT.Copy)
                        last.then_inc(S.na_ptc, 1)

                    exps(0)
                    for i in range(len(units)):
                        if i + 1 < len(units):
                            exps(i + 1)
                        copies(i)
                    barrier(act)

                s0 = l * SPLITS + FN0
                for g in range(HEADS):
                    n = l * HEADS + g
                    if g == 0:
                        split_to(s0 + 2)
                        act.wait_ge(S.job_done, s0 + 1)
                        fn(by_chunk(uT[:, 0, :]), group(s0 % 2), ACT.Copy).then_inc(S.act_evac, 1)
                    if g + 1 < HEADS:
                        split_to(s0 + g + 3)
                        act.wait_ge(S.job_done, s0 + g + 2)
                        fn(by_chunk(uT[:, (g + 1) % 2, :]), group((s0 + g + 1) % 2), ACT.Copy).then_inc(S.act_evac, 1)
                    for j in range(4):
                        act.wait_ge(S.u_pair, 5 * n + j + 1)
                        fn(xcs[:, j].rearrange("p a b -> p (a b)"), ps[:, 6 + j % 2, 0:256], ACT.Copy
                           ).then_inc(S.pair_copied, 1)
                    for i in range(2):
                        act.wait_ge(S.x_done, 5 * n + 2 * i + 2)
                        w = (HK + 1) if i == 0 else HK
                        if g:
                            act.wait_ge(S.q_done, 2 * (n - 1) + i + 1)
                        fn(qsb[:, i, 0:w], ps[:, 3 * (g % 2) + 1 if i == 0 else 6, 0:w], ACT.Copy).then_inc(S.q_copied, 1)
                    act.wait_ge(S.x_done, 5 * n + 5)
                    if g:
                        act.wait_ge(S.f_lo, n)
                    fn(ft[:, TL:], ps[:, 7, 0:P], ACT.Copy).then_inc(S.f_ctx, 1)
                    act.drain()
                    act.wait_ge(S.q_done, 2 * n + 2)
                    fn(fhi[:, g, :], ft[:], ACT.Copy).then_inc(S.f_hi, 1)
                for m in range(HEADS):
                    s = s0 + HEADS + 2 * m
                    split_to(s + 2)
                    act.wait_ge(S.job_done, s + 1)
                    if m:
                        act.wait_ge(*evacuated(s - 1))
                    fn(by_chunk(fth[:]), group(s % 2), ACT.Tanh, scale=0.5).then_inc(S.th_ready, 1)
                    split_to(s + 3)
                split_to(s0 + 3 * HEADS + 2)
                barrier(act)

                for h in range(HEADS):
                    s0 = l * SPLITS + DF0 + 4 * h
                    for r in range(4):
                        s = s0 + r
                        split_to(s + 2)
                        g = group(s % 2)
                        act.wait_ge(S.job_done, s + 1)
                        if r == 0:
                            fn(by_chunk(xi[:]), g, ACT.Copy, scale=0.125).then_inc(S.act_evac, 1)
                        if r == 1:
                            act.wait_ge(S.rope_done, 2 * (l * HEADS + h) + 1)
                            fn(by_chunk(xi[:]), g, ACT.Copy).then_inc(S.act_evac, 1)
                        if r == 2:
                            fn(by_chunk(vT[:]), g, ACT.Copy).then_inc(S.act_evac, 1)
                        if r == 3:
                            fn(by_chunk(th[:]), g, ACT.Tanh, scale=0.5).then_inc(S.th_ready, 1)
                    token_rows(l * 2 * HEADS + HEADS + h)
                    split_to(min(s0 + 6, (l + 1) * SPLITS))
                    barrier(act)
                    n9 = (l * HEADS + h) * TILES
                    g0 = (l * HEADS + h) * (3 * LT + 1)

                    def exps(t, m):
                        nk = TC if t == LT else TL + PAST
                        e = (e1, e2)[m]
                        act.wait_ge(S.df_m, 2 * (n9 + t) + m + 1)
                        if t >= 3 and m == 0:
                            act.wait_ge(S.df_pt, g0 + 3 * (t - 2))
                        fn(e[:, t % (3 - m), 0:nk], flat[:, 1536 * m:1536 * m + nk], ACT.Exp,
                           bias=stat[:, t % 2, m:m + 1], accum_out=stat[:, t % 2, 2 + m:3 + m]).then_inc(S.df_e, 1)

                    def copies(t, g):
                        if t == LT and g:
                            return
                        if g == 0 and t % 2 == 0 and t >= 4:
                            act.wait_ge(S.df_pv, (l * HEADS + h) * 5 + t // 2 - 1)
                        act.wait_ge(S.df_pt, g0 + 3 * t + g + 1)
                        w = 3 if t < LT else 1
                        fn(aT[:, (t // 2) % 2, 3 * g:3 * g + w, (t % 2) * P:(t % 2 + 1) * P],
                           ps[:, 6, 0:w * P].rearrange("p (t n) -> p t n", n=P), ACT.Copy).then_inc(S.df_ptc, 1)

                    exps(0, 0)
                    exps(0, 1)
                    for t in range(TILES + 1):
                        for g in range(3):
                            if t >= 1:
                                copies(t - 1, g)
                            if t + 1 < TILES and g < 2:
                                exps(t + 1, g)
                    barrier(act)
                    n = l * HEADS + h
                    fn(xi[:], obuf[:], ACT.Square).then_inc(S.sqo_ready, 1)
                    act.wait_ge(S.sso_done, n + 1)
                    fn(by_chunk(xr[:]), group(0), ACT.Ln, bias=eps[:, 0:1], scale=1.0 / P)
                    act.drain()
                    fn(xr[:], xr[:], ACT.Exp, scale=-0.5).then_inc(S.rso_ready, 1)
                    barrier(act)

                for b in range(3):
                    n = l * 3 + b
                    act.wait_ge(S.o_load, 16 * (n + 1))
                    fn(ohi[:], oraw[:], ACT.Copy).then_inc(S.o_hi, 1)
                    for m in range(KT):
                        s = l * SPLITS + MG0 + 2 * (b * KT + m)
                        split_to(s + 2)
                        act.wait_ge(S.job_done, s + 1)
                        if m >= 2:
                            act.wait_ge(*(evacuated(s - 3) if b == 0 else (S.y_added, (2 * l + b - 1) * KT + m - 1)))
                        fn(by_chunk(gth[:, m % 2, :]), group(s % 2), ACT.Tanh, scale=0.5).then_inc(S.act_evac, 1)
                        split_to(s + 3)
                    split_to(l * SPLITS + MG0 + 2 * KT * (b + 1) + 2)
                    barrier(act)
                for m in range(KT):
                    fn(hhi[:, m, :], ysum[:, m, :], ACT.Copy).then_inc(S.hi_ready, 1)
                for m in range(KT):
                    split_to(min(l * SPLITS + OUT0 + m + 2, (l + 1) * SPLITS))
                barrier(act)
            for t in range(TILES):
                act.wait_ge(S.fin_tr, t + 1)
                if t >= 2:
                    act.wait_ge(S.fin_y, t - 1)
                act.drain()
                fn(junk[:], flat[:, 1024 * (t % 2):1024 * (t % 2) + D], ACT.Square,
                   accum_out=fss[:, t % 2, 0:1])
                act.drain()
                fn(fss[:, t % 2, 1:2], fss[:, t % 2, 0:1], ACT.Ln, bias=eps[:, 0:1], scale=1.0 / D)
                act.drain()
                fn(fss[:, t % 2, 2:3], fss[:, t % 2, 1:2], ACT.Exp, scale=-0.5).then_inc(S.fin_rs, 1)

        @block.vector
        def _(dve):
            v = nc.vector
            ths = [2]
            dve.wait_ge(S.setup_load, 16 * 5)
            v.memset(ones[:], 1.0)
            v.memset(eps[:], EPS)
            v.tensor_tensor(lammul[:], lamraw[:, :, 0:4:2, :], lamraw[:, :, 1:4:2, :], ALU.mult)
            dve.drain()
            dve.wait_ge(S.setup_done, 1)
            v.tensor_reduce(lprod[:], lammul[:], AX.X, ALU.add).then_inc(S.setup_done, 1)
            dve.wait_ge(S.th_ready, 2)
            v.scalar_tensor_tensor(out=cth[:], in0=cth[:], scalar=1.0, in1=craw[:], op0=ALU.add, op1=ALU.mult)
            v.tensor_tensor(neglam[:], lexp[:, :, 1], lexp[:, :, 0], ALU.subtract)
            dve.drain()
            v.tensor_scalar(csil[:], cth[:], 0.5, None, ALU.mult)
            for l in range(DEPTH):
                lam_init = 0.8 - 0.6 * math.exp(-0.3 * l)
                v.tensor_scalar(neglam[:, l:l + 1], neglam[:, l:l + 1], -lam_init, None, ALU.add)
                v.tensor_scalar(subg[:, l:l + 1], subg[:, l:l + 1], 1.0 - lam_init, None, ALU.mult)
            for g in range(2 * TILES):
                t, half = divmod(g, 2)
                dve.wait_ge(S.tr_ready, g + 1)
                v.tensor_copy(xT[:, 4 * half:4 * half + 4, t * P:(t + 1) * P],
                              ps[:, g % 2, :].rearrange("p (k n) -> p k n", k=4)).then_inc(S.xtok_used, 1)
            barrier(dve)
            for l in range(DEPTH):
                dve.wait_ge(S.mod_used, (l + 1) * MODS)
                for j in range(2):
                    v.tensor_tensor(modr[:, :, j], ps[:, 7, j:2 * MODS:2], bcol[:, l, :], ALU.add)
                dve.drain()
                for j in range(2):
                    v.scalar_tensor_tensor(out=mul_a[:, :, j], in0=modr[:, KT:2 * KT, j], scalar=1.0, in1=gcol[:, l, :],
                                           op0=ALU.add, op1=ALU.mult)
                v.tensor_scalar(mul_g[:], modr[:, 2 * KT:, :], 0.25, None, ALU.mult).then_inc(S.mod_ready, 1)
                dve.wait_ge(S.rstd_ready, l + 1)
                for m in range(KT):
                    n = l * KT + m
                    if m >= 2:
                        dve.wait_ge(S.hi_ready, KT * 2 * l + m - 1)
                    v.tensor_tensor(tn[:, m % 2, :], xT[:, m, :], rstd[:], ALU.mult).then_inc(S.t_ready, 1)
                barrier(dve)

                def silu_gate(s, tanh, out):
                    ths[0] += 1
                    dve.wait_ge(S.th_ready, ths[0])
                    v.scalar_tensor_tensor(out=by_chunk(out[:]), in0=by_chunk(tanh[:]), scalar=1.0, in1=group(s % 2),
                                           op0=ALU.add, op1=ALU.mult).then_inc(S.dve_evac, 1)

                for p in range(HEADS):
                    if p == 0:
                        v.memset(qa[64:128, :], 0.0)
                        v.memset(qb[0:64, :], 0.0)
                    silu_gate(l * SPLITS + NA0 + 4 * p + 3, th, zs)
                    barrier(dve)
                    units = [(t, e) for t in range(TILES) for e in range(2)]
                    u0 = (l * HEADS + p) * len(units)

                    def biased(i):
                        t, e = units[i]
                        st = stat[:, i % 2]
                        c0 = 1536 * (i % 2)
                        dve.wait_ge(S.na_s, u0 + i + 1)
                        if i >= 2:
                            dve.wait_ge(S.na_pt, u0 + i - 1)
                        if t == LT:
                            v.tensor_copy(sn[:, i % 2, 0:P], flat[:, c0:c0 + P])
                            v.tensor_reduce(st[:, 0:1], flat[:, c0:c0 + P], AX.X, ALU.max)
                            dve.drain()
                            v.tensor_scalar(st[:, 2:3], st[:, 0:1], -1.0, None, ALU.mult).then_inc(S.na_b, 1)
                            return
                        _, n, at = window(t)
                        nk = n * GW
                        v.tensor_tensor_reduce(out=sn[:, i % 2, 0:nk], in0=flat[:, c0:c0 + nk],
                                               in1=bias[:, e, at:at + n, :].rearrange("p a b -> p (a b)"), scale=1.0,
                                               scalar=-3.0e38, op0=ALU.add, op1=ALU.max, accum_out=st[:, 0:1])
                        v.tensor_scalar(sn[:, i % 2, nk:nk + PAST], flat[:, c0 + nk:c0 + nk + PAST], 1.0, None,
                                        ALU.mult, ALU.max, accum_out=st[:, 1:2])
                        dve.drain()
                        v.tensor_scalar(st[:, 2:3], st[:, 0:1], st[:, 1:2], -1.0, ALU.max, ALU.mult
                                        ).then_inc(S.na_b, 1)

                    def normed(i):
                        t, e = units[i]
                        st = stat[:, i % 2]
                        nk = P if t == LT else window(t)[1] * GW + PAST
                        dve.wait_ge(S.na_e, u0 + i + 1)
                        v.reciprocal(st[:, 4:5], st[:, 3:4])
                        dve.drain()
                        v.tensor_scalar(sn[:, i % 2, 0:nk], sn[:, i % 2, 0:nk], st[:, 4:5], None, ALU.mult
                                        ).then_inc(S.na_p, 1)

                    def gated(tg):
                        w = 512 if tg < 2 else P
                        last = min(8 * (tg + 1), len(units))
                        dve.wait_ge(S.na_pv, u0 + last)
                        v.tensor_tensor(obuf[:, 512 * tg:512 * tg + w], ps[:, 2 + 3 * (tg % 2), 0:w],
                                        zs[:, 512 * tg:512 * tg + w], ALU.mult).then_inc(S.na_o, 1)

                    dve.wait_ge(S.masked, l * HEADS + p + 1)
                    biased(0)
                    for i in range(len(units)):
                        if i + 1 < len(units):
                            biased(i + 1)
                        normed(i)
                        if i in (9, 17):
                            gated(i // 8 - 1)
                    gated(2)
                    barrier(dve)

                for g in range(HEADS):
                    n = l * HEADS + g
                    for j in range(5):
                        if j < 4:
                            dve.wait_ge(S.pair_copied, 4 * n + j + 1)
                            hi = ps[:, 6 + j % 2, 256:512]
                            lo = xcs[:, j].rearrange("p a b -> p (a b)")
                            v.tensor_tensor(xsum[:, j].rearrange("p a b -> p (a b)"), lo, hi, ALU.add)
                            v.tensor_tensor(xdif[:, j].rearrange("p a b -> p (a b)"), lo, hi, ALU.subtract
                                            ).then_inc(S.folded, 1)
                        else:
                            dve.wait_ge(S.u_pair, 5 * n + 5)
                            v.tensor_copy(xctx[:].rearrange("p a b -> p (a b)"), ps[:, 6, 0:256]).then_inc(S.folded, 1)
                    if g:
                        dve.wait_ge(S.f_lo, n)
                    for i in range(2):
                        bank = 3 * (g % 2) + 2 * i
                        first = 1 if i == 0 else 0
                        w = (HK + 1) if i == 0 else HK
                        dve.wait_ge(S.q_copied, 2 * n + i + 1)
                        v.tensor_tensor(ft[:, i:i + 2 * w - 1:2], ps[:, bank, 0:w], qsb[:, i, 0:w], ALU.subtract)
                        v.tensor_tensor(ft[:, TL - 2 * first - i:TL // 2:-2], ps[:, bank, first:HK], qsb[:, i, first:HK], ALU.add).then_inc(S.q_done, 1)
                for m in range(HEADS):
                    s = l * SPLITS + FN0 + HEADS + 2 * m
                    silu_gate(s, fth, fzs)
                    dve.drain()
                    dve.wait_ge(S.job_done, s + 2)
                    if m:
                        dve.wait_ge(S.f_store, 16 * (l * HEADS + m))
                    v.tensor_tensor(by_chunk(fout[:]), group((s + 1) % 2), by_chunk(fzs[:]), ALU.mult
                                    ).then_inc(S.dve_evac, 1)
                barrier(dve)

                for h in range(HEADS):
                    n = l * HEADS + h
                    s0 = l * SPLITS + DF0 + 4 * h
                    if h == 0:
                        v.memset(qa[64:128, :], 0.0)
                        v.memset(qb[0:64, :], 0.0)
                    dve.wait_ge(S.load, df_loaded(l, h))
                    for r in range(2):
                        dve.wait_ge(*evacuated(s0 + r))
                        v.stream_shuffle(xr[:, 0:TL], xi[:, 0:TL], [(i + 16) % 32 for i in range(32)])
                        dve.drain()
                        v.tensor_tensor(xr[:, 0:TL], xr[:, 0:TL], sinT[:], ALU.mult)
                        v.tensor_tensor(xc[:, 0:TL], xi[:, 0:TL], cosT[:], ALU.mult)
                        dve.drain()
                        if r == 0:
                            v.tensor_copy(qa[0:64, TL:], xi[0:64, TL:])
                            v.tensor_copy(qb[64:128, TL:], xi[64:128, TL:])
                            v.tensor_tensor(qa[0:64, 0:TL], xc[0:64, 0:TL], xr[0:64, 0:TL], ALU.add)
                            v.tensor_tensor(qb[64:128, 0:TL], xc[64:128, 0:TL], xr[64:128, 0:TL], ALU.add
                                            ).then_inc(S.rope_done, 1)
                        else:
                            v.tensor_copy(kT[:, TL + PAST:], xi[:, TL:])
                            v.tensor_tensor(kT[:, 0:TL], xc[:, 0:TL], xr[:, 0:TL], ALU.add).then_inc(S.rope_done, 1)
                        dve.drain()
                    silu_gate(s0 + 3, th, zs)
                    barrier(dve)
                    n9 = n * TILES

                    def maxes(t):
                        for m in range(2):
                            nk = TC if t == LT else TL + PAST
                            dve.wait_ge(S.df_s, 2 * (n9 + t) + m + 1)
                            v.tensor_reduce(stat[:, t % 2, m:m + 1], flat[:, 1536 * m:1536 * m + nk], AX.X, ALU.max,
                                            negate=True).then_inc(S.df_m, 1)

                    def combined(t):
                        st = stat[:, t % 2]
                        nk = TC if t == LT else TL + PAST
                        dve.wait_ge(S.df_e, 2 * (n9 + t) + 2)
                        v.reciprocal(st[:, 4:6], st[:, 2:4])
                        dve.drain()
                        v.tensor_scalar(e2[:, t % 2, 0:nk], e2[:, t % 2, 0:nk], st[:, 5:6], neglam[:, l:l + 1],
                                        ALU.mult, ALU.mult)
                        dve.drain()
                        v.scalar_tensor_tensor(out=e1[:, t % 3, 0:nk], in0=e1[:, t % 3, 0:nk], scalar=st[:, 4:5],
                                               in1=e2[:, t % 2, 0:nk], op0=ALU.mult, op1=ALU.add).then_inc(S.df_p, 1)

                    def out_pair(pair):
                        w = 2 * P if pair < 4 else P
                        dve.wait_ge(S.df_pv, 5 * n + pair + 1)
                        v.tensor_copy(obuf[:, 2 * P * pair:2 * P * pair + w], ps[:, 7, 0:w]
                                      ).then_inc(S.df_o, 1)

                    maxes(0)
                    for t in range(TILES):
                        if t + 1 < TILES:
                            maxes(t + 1)
                        combined(t)
                        if t % 2 and t >= 3:
                            out_pair(t // 2 - 1)
                    out_pair(3)
                    out_pair(4)
                    barrier(dve)
                    dve.wait_ge(S.rso_ready, n + 1)
                    v.scalar_tensor_tensor(out=xc[:], in0=obuf[:], scalar=subg[:, l:l + 1], in1=xr[:],
                                           op0=ALU.mult, op1=ALU.mult)
                    dve.drain()
                    v.tensor_tensor(obuf[:], xc[:], zs[:], ALU.mult)
                    barrier(dve)

                for b in range(3):
                    for m in range(KT):
                        s = l * SPLITS + MG0 + 2 * (b * KT + m)
                        dve.wait_ge(*evacuated(s))
                        dve.wait_ge(S.job_done, s + 2)
                        out = ysum[:, m, :] if b == 0 else gth[:, m % 2, :]
                        x = v.scalar_tensor_tensor(out=by_chunk(out), in0=by_chunk(gth[:, m % 2, :]), scalar=1.0,
                                                   in1=group((s + 1) % 2), op0=ALU.add, op1=ALU.mult)
                        x.then_inc(S.dve_evac, 1)
                    barrier(dve)
                for m in range(KT):
                    s = l * SPLITS + OUT0 + m
                    n = l * KT + m
                    dve.wait_ge(S.job_done, s + 1)
                    dve.wait_ge((S.x_load0, S.x_load1)[m % 2], 16 * (l * (KT // 2) + m // 2 + 1))
                    g = group(s % 2)
                    for src, lo, hi, j in ((g[:, 0:2], 0, 2 * CH, 0), (g[:, 2, 0:TL - 2 * CH], 2 * CH, TL, 0),
                                           (g[:, 2, TL - 2 * CH:], TL, T, 1)):
                        o, r = xT[:, m, lo:hi], xold[:, m % 2, lo:hi]
                        if lo == 0:
                            o, r = by_chunk(o), by_chunk(r)
                        x = v.scalar_tensor_tensor(out=o, in0=src, scalar=mul_g[:, m, j:j + 1], in1=r,
                                                   op0=ALU.mult, op1=ALU.add)
                    x.then_inc(S.dve_evac, 1)
                barrier(dve)
            dve.wait_ge(S.load, 16 * (DEPTH * LAYER_LOADS + 1))
            for t in range(TILES):
                dve.wait_ge(S.fin_rs, t + 1)
                if t >= 2:
                    dve.wait_ge((S.fin_st0, S.fin_st1)[t % 2], 16 * (t // 2))
                v.scalar_tensor_tensor(out=yb[:, t % 2, :], in0=flat[:, 1024 * (t % 2):1024 * (t % 2) + D],
                                       scalar=fss[:, t % 2, 2:3], in1=fg[:], op0=ALU.mult, op1=ALU.mult
                                       ).then_inc(S.fin_y, 1)

        @block.gpsimd
        def _(pool):
            g_ = nc.gpsimd
            split = [0]

            def split_to(s_end):
                while split[0] < s_end:
                    s = split[0]
                    l, i = divmod(s, SPLITS)
                    c = l * CHUNKS + MODS + i
                    kt = chunk_k(i)
                    pool.wait_ge(S.w_hi, s + 1)
                    g_.tensor_tensor(wlo[:, s % 2, 0:kt, :], wraw[:, c % 2, 0:kt, :],
                                     whi[:, s % 2, 0:kt, :].bitcast(F32), ALU.subtract).then_inc(S.w_lo, 1)
                    split[0] += 1

            g_.memset(ident[:], 0.0)
            pool.drain()
            g_.affine_select(out=ident[:], in_=ident[:], compare_op=ALU.not_equal, fill=1.0, base=0,
                             pattern=[[-1, P]], channel_multiplier=1).then_inc(S.setup_done, 1)
            barrier(pool)
            for l in range(DEPTH):
                for m in range(KT):
                    pool.wait_ge(S.hi_ready, KT * 2 * l + m + 1)
                    g_.tensor_tensor(hlo[:, m, :], un[:, m % 2, :], hhi[:, m, :].bitcast(F32), ALU.subtract
                                     ).then_inc(S.h_ready, 1)
                split_to(l * SPLITS + 2)
                barrier(pool)
                for p in range(HEADS):
                    pool.wait_ge(S.load, na_loaded(l, p))
                    for e in range(2):
                        x = g_.tensor_tensor(bias[:, e], bias[:, e], mask[:], ALU.add)
                    x.then_inc(S.masked, 1)
                    split_to(l * SPLITS + NA0 + 4 * p + 6)
                    barrier(pool)
                    barrier(pool)
                s0 = l * SPLITS + FN0
                for g in range(HEADS):
                    split_to(s0 + min(g, 2) + 3)
                    n = l * HEADS + g
                    pool.wait_ge(S.f_hi, n + 1)
                    g_.tensor_tensor(flo[:, g, :], ft[:], fhi[:, g, :].bitcast(F32), ALU.subtract
                                     ).then_inc(S.f_lo, 1)
                split_to(s0 + 3 * HEADS + 2)
                barrier(pool)
                for h in range(HEADS):
                    split_to(l * SPLITS + DF0 + 4 * h + 6)
                    barrier(pool)
                    barrier(pool)
                    barrier(pool)
                for b in range(3):
                    n = l * 3 + b
                    pool.wait_ge(S.o_hi, n + 1)
                    g_.tensor_tensor(olo[:], oraw[:], ohi[:].bitcast(F32), ALU.subtract).then_inc(S.o_lo, 1)
                    for m in range(KT):
                        s = l * SPLITS + MG0 + 2 * (b * KT + m)
                        split_to(s + 3)
                        if b:
                            pool.wait_ge(*evacuated(s + 1))
                            g_.tensor_tensor(ysum[:, m, :], ysum[:, m, :], gth[:, m % 2, :], ALU.add
                                             ).then_inc(S.y_added, 1)
                    split_to(min(l * SPLITS + MG0 + 2 * KT * (b + 1) + 2, (l + 1) * SPLITS))
                    barrier(pool)
                for m in range(KT):
                    pool.wait_ge(S.hi_ready, KT * (2 * l + 1) + m + 1)
                    g_.tensor_tensor(hlo[:, m, :], ysum[:, m, :], hhi[:, m, :].bitcast(F32), ALU.subtract
                                     ).then_inc(S.h_ready, 1)
                split_to((l + 1) * SPLITS)
                barrier(pool)


def dft_tables():
    c = np.arange(P)
    ang = 2 * np.pi * (np.outer(c, c) % P) / P
    chan = np.stack([np.cos(ang), np.sin(ang)], 1) / np.sqrt(P)
    ctx = np.stack([np.cos(ang), -np.sin(ang)], 1) / np.sqrt(P)
    tok = np.zeros((4, P, 4, TL // 4 + 2))
    t = np.arange(TL // 2)
    for i in range(4):
        odd = i // 2
        k = 2 * np.arange(TL // 4 + 1 - odd) + odd
        ang = 2 * np.pi * (np.outer(t, k) % TL) / TL
        tok[:, :, i, :len(k)] = ((np.sin if i % 2 else np.cos)(ang) / np.sqrt(TL)).reshape(4, P, len(k))
    return [np.ascontiguousarray(a, np.float32) for a in (chan, ctx, tok.transpose(1, 0, 2, 3))]


def rope_tables():
    t = np.arange(TL)
    inv = (np.float32(10000.0) ** (-np.arange(0, 32, 2, dtype=np.float32) / np.float32(32))).astype(np.float32)
    d = np.arange(P) % 64
    where = np.where((d < 32)[:, None], (t // GW)[None], (t % GW)[None]).astype(np.float32)
    ang = where * inv[d % 16][:, None]
    sign = np.where(d % 32 < 16, -1.0, 1.0)[:, None]
    return np.stack([np.cos(ang), np.sin(ang) * sign]).astype(np.float32)


def window_mask():
    c = np.arange(GW)
    start = np.clip(c - 8, 0, GW - 16)
    out = (c[None] < start[:, None]) | (c[None] >= start[:, None] + 16)
    m = np.zeros((2, GW, NS + NI, GW), bool) | out[None, :, None, :]
    m[0, :, NS + I_MAX - I_MIN] = True
    m[1, :, NS] = True
    return np.where(m, np.float32(-1e30), np.float32(0)).reshape(P, NS + NI, GW)


def kernel(x_prompt, x_sample, cache_na_k, cache_na_v, cache_diff_k, cache_diff_v, c, c_ctx, norm_g, w_mod, b_mod,
           w_in, na_rpb, fnet_w, diff_lq1, diff_lk1, diff_lq2, diff_lk2, diff_subln_g, w_branch, w_out, final_g):
    import concourse.bacc as bacc
    from concourse.bass_utils import run_bass_kernel_spmd

    arr = np.asarray
    padded = np.zeros((DEPTH, 8, 15, PADW), np.float32)
    padded[..., GW - 16:GW + 15] = arr(na_rpb)
    rpb = np.stack([padded[..., GW - 1 - q:2 * GW - 1 - q] for q in range(GW)], 2)
    tables = dft_tables()
    ins = {
        "x_prompt": arr(x_prompt), "x_sample": arr(x_sample), "cache_na_k": arr(cache_na_k),
        "cache_na_v": arr(cache_na_v), "cache_diff_k": arr(cache_diff_k), "cache_diff_v": arr(cache_diff_v),
        "cvec": np.stack([arr(c)[0].reshape(KT, P).T, arr(c_ctx).reshape(KT, P).T], -1),
        "norm_g": arr(norm_g).reshape(DEPTH, KT, P).transpose(2, 0, 1),
        "w_mod": arr(w_mod), "b_mod": arr(b_mod).reshape(DEPTH, MODS, P).transpose(2, 0, 1), "w_in": arr(w_in),
        "rpb": rpb, "fnet_w": arr(fnet_w),
        "lams": np.stack([arr(diff_lq1), arr(diff_lk1), arr(diff_lq2), arr(diff_lk2)], 1),
        "subln_g": arr(diff_subln_g).T, "w_branch": arr(w_branch), "w_out": arr(w_out), "final_g": arr(final_g),
        "na_mask": window_mask(), "rope": rope_tables(), "dft_c": tables[0], "dft_x": tables[1], "dft_t": tables[2],
    }
    ins = {k: np.ascontiguousarray(v) for k, v in ins.items()}
    outs = {
        "y_prompt": (1, TC, D), "y_sample": (1, TL, D), "new_na_k": (1, DEPTH, 8, TC, 64),
        "new_na_v": (1, DEPTH, 8, TC, 64), "new_diff_k": (1, DEPTH, HEADS, TC, P), "new_diff_v": (1, DEPTH, HEADS, TC, P),
    }
    nc = bacc.Bacc("TRN2", target_bir_lowering=False, num_devices=1)
    args = [nc.dram_tensor(n, a.shape, F32, kind="ExternalInput").ap() for n, a in ins.items()]
    args += [nc.dram_tensor(n, s, F32, kind="ExternalOutput").ap() for n, s in outs.items()]
    args.append(nc.dram_tensor("xs_dram", (KT, P, T), F32, kind="Internal").ap())
    args.append(nc.dram_tensor("outs_dram", (3, BK, P, T), F32, kind="Internal").ap())
    build(nc, *args)
    r = run_bass_kernel_spmd(nc, [ins], core_ids=[0]).results[0]
    return tuple(r[n] for n in outs)
```

```python
import math
from collections import namedtuple

import numpy as np

import concourse.bass as bass
from concourse import mybir

F32 = mybir.dt.float32
F32R = mybir.dt.float32r
ALU = mybir.AluOpType
ACT = mybir.ActivationFunctionType
AX = mybir.AxisListType

P = 128
DEPTH = 2
D = 1024
KT = D // P
TL = 1024
TC = 128
T = TL + TC
TILES = T // P
LT = TL // P
CH = 384
NC = T // CH
PAST = 128
GW = 64
NA_BATCHES = 4 * LT + 2
WIN = 8
HEADS = 4
BW = 512
BK = BW // P
EPS = 1e-6

MODS = 3 * KT
ROUTE = {"z": "dve", "q": "act", "k": "act", "v": "act", "u": "act", "w": "dve", "b": "dve", "o": "dve"}
FILL = 3


def plan():
    out = [("m", 0, "", i) for i in range(MODS)]
    for l in range(DEPTH):
        for ph in ("na", "fn", "df"):
            if ph == "fn":
                out += [("u", l, ph, g) for g in range(HEADS)]
                out += [(r, l, ph, m) for m in range(HEADS) for r in "zw"]
                continue
            for p in range(HEADS):
                out += [(r, l, ph, p) for r in "qkzv"]
                at = FILL * (p + (HEADS if ph == "df" else 0))
                out += [("g", l, "", at + i) for i in range(FILL)]
        for i in range(3 * KT):
            out.append(("b", l, "", i))
            if l + 1 < DEPTH:
                out.append(("m", l + 1, "", i))
        out += [("o", l, "", m) for m in range(KT)]
    return out


STREAM = plan()
CHUNK = {c: i for i, c in enumerate(STREAM)}
SPLIT = [c for c in STREAM if c[0] != "m"]
SPLIT_NO = {c: i for i, c in enumerate(SPLIT)}
JOBS = [c for c in SPLIT if c[0] != "g"]
JOB_NO = {c: i for i, c in enumerate(JOBS)}


def chunk_k(c):
    return BK if c[0] in "wb" else KT


S_MIN, S_MAX = -6, 7
I_MIN, I_MAX = -4, 4
NS = S_MAX - S_MIN + 1
NI = I_MAX - I_MIN + 1
PADW = 2 * GW - 1


def window(t):
    rows = TL // GW
    lo = min(max(2 * t - WIN // 2, 0), rows - WIN)
    hi = min(max(2 * t + 1 - WIN // 2, 0), rows - WIN) + WIN
    n = hi - lo
    e = (lo - 2 * t - S_MIN) if n == WIN else NS + (lo - 2 * t - I_MIN)
    return lo, n, e


def na_tiles(t):
    if t == LT:
        return [(0, P, LT)]
    lo, n, _ = window(t)
    nk = n * GW
    tiles = [(P * j, P * j + P, lo // 2 + j) for j in range(4)] + [(nk, nk + PAST, TILES)]
    return tiles + ([(512, nk, lo // 2 + 4)] if nk > 512 else [])


def build(nc, x_prompt, x_sample, cache_na_k, cache_na_v, cache_diff_k, cache_diff_v, cvec, norm_g, w_mod,
          b_mod, w_in, rpb, fnet_w, lams, subln_g, w_branch, w_out, final_g, na_mask, rope, dft_c, dft_x, dft_t,
          y_prompt, y_sample, new_na_k, new_na_v, new_diff_k, new_diff_v, xs_dram, outs_dram, gates_dram):
    base = (nc.sbuf_base + 31) // 32 * 32
    TB = T * 4

    class Place:

        def __init__(self, at):
            self.at = at

        def __call__(self, name, shape, dtype=F32):
            size = int(np.prod(shape[1:])) * 4
            t = nc.alloc_sbuf_tensor_at(name, shape, dtype, offset=self.at)
            self.at += (size + 31) // 32 * 32
            return t

    keep = Place(base)
    hhi = keep("hhi", [P, KT, T], F32R)
    hlo = keep("hlo", [P, KT, T], F32R)
    wraw = keep("wraw", [P, 2, KT, P])
    whi = keep("whi", [P, 2, KT, P], F32R)
    wlo = keep("wlo", [P, 2, KT, P], F32R)
    ident = keep("ident", [P, P])
    ones = keep("ones", [P, P])
    eps = keep("eps", [P, 1])
    csil = keep("csil", [P, KT, 2])
    gcol = keep("gcol", [P, DEPTH, KT])
    bcol = keep("bcol", [P, DEPTH, MODS])
    subg = keep("subg", [P, DEPTH])
    modr = keep("modr", [P, MODS, 2])
    mul_a = keep("mul_a", [P, KT, 2])
    mul_g = keep("mul_g", [P, KT, 2])
    neglam = keep("neglam", [P, DEPTH])
    lprod = keep("lprod", [P, DEPTH, 2])
    lexp = keep("lexp", [P, DEPTH, 2])
    cth = keep("cth", [P, KT, 2])
    craw = keep("craw", [P, KT, 2])
    y0 = keep.at
    arena0 = y0 + KT * TB

    TK = T + PAST
    pl = Place(y0)
    ysum = pl("ysum", [P, KT, T])
    assert pl.at == arena0
    xT = pl("xT", [P, KT, T])
    sqs = pl("sqs", [P, T])
    sq = pl("sq", [P, 2, T])
    rstd = pl("rstd", [P, T])
    tn = pl("tn", [P, 2, T])
    assert pl.at <= nc.sbuf_usable_end

    pl = Place(y0)
    xtok = pl("xtok", [P, TILES, D])

    pl = Place(y0)
    qq = pl("qq", [P, 2, T], F32R)
    kkh = pl("kkh", [P, 2, TK], F32R)
    kkl = pl("kkl", [P, 2, TK], F32R)
    vhi = pl("vhi", [P, TILES + 1, P], F32R)
    vlo = pl("vlo", [P, TILES + 1, P], F32R)
    vraw = pl("vraw", [P, P])
    vout = pl("vout", [P, P])
    ck = pl("ck", [P, P])
    kout = pl("kout", [P, P])
    gst = pl("gst", [P, T])
    zs = pl("zs", [P, T])
    obuf = pl("obuf", [P, T])
    stat = pl("stat", [P, 2, 8])
    na_at = pl.at
    xi = pl("xi", [P, TK])
    xh = pl("xh", [P, TK], F32R)
    xl = pl("xl", [P, TK], F32R)
    bias = pl("bias", [P, 2, NS + NI, GW])
    mask = pl("mask", [P, NS + NI, GW])
    sn = pl("sn", [P, 2, 704])
    pth = pl("pth", [P, 6, 2, P], F32R)
    ptl = pl("ptl", [P, 6, 2, P], F32R)
    vT = pl("vT", [P, T])
    assert pl.at <= nc.sbuf_usable_end, pl.at - nc.sbuf_usable_end
    pl = Place(na_at)
    e1 = pl("e1", [P, 3, TK])
    e2 = pl("e2", [P, 2, TK])
    aTh = pl("aTh", [P, LT + 1, 2 * P], F32R)
    aTl = pl("aTl", [P, LT + 1, 2 * P], F32R)
    cosT = pl("cosT", [P, TL])
    sinT = pl("sinT", [P, TL])
    assert pl.at <= nc.sbuf_usable_end, pl.at - nc.sbuf_usable_end
    pl = Place(na_at)
    xi_d = pl("xi_d", [P, TK])
    xh_d = pl("xh_d", [P, TK], F32R)
    xl_d = pl("xl_d", [P, TK], F32R)
    xr = pl("xr", [P, TK])
    xc = pl("xc", [P, TK])
    vT_d = pl("vT_d", [P, T])
    sqo = nc.alloc_sbuf_tensor_at("sqo", [P, T], F32, offset=pl.at)
    rso = nc.alloc_sbuf_tensor_at("rso", [P, T], F32, offset=pl.at + TB)

    HK = TL // 4
    pl = Place(y0)
    uT = pl("uT", [P, 2, T])
    fth = pl("fth", [P, T])
    fzs = pl("fzs", [P, T])
    fout = pl("fout", [P, T])
    tab_c = pl("tab_c", [P, 2, P])
    tab_x = pl("tab_x", [P, 2, P])
    tab_t = pl("tab_t", [P, 4, 4, HK + 2])
    xcs = pl("xcs", [P, 4, 2, P])
    xsum = pl("xsum", [P, 4, 2, P])
    xdif = pl("xdif", [P, 4, 2, P])
    xctx = pl("xctx", [P, 2, P])
    qsb = pl("qsb", [P, 2, HK + 2])
    ft = pl("ft", [P, T])
    fhi = pl("fhi", [P, HEADS, T], F32R)
    flo = pl("flo", [P, HEADS, T], F32R)
    assert pl.at <= nc.sbuf_usable_end

    HB = BK * TB
    omh = [nc.alloc_sbuf_tensor_at(f"omh{b}", [P, BK, T], F32R, offset=a)
           for b, a in enumerate((base, base + 2 * HB, arena0))]
    oml = [nc.alloc_sbuf_tensor_at(f"oml{b}", [P, BK, T], F32R, offset=a + HB)
           for b, a in enumerate((base, base + 2 * HB, arena0))]
    pl = Place(arena0 + KT * TB)
    pl.at += 3 * TB
    oraw = pl("oraw", [P, 2, T])
    gth = pl("gth", [P, 3, T])
    assert pl.at <= nc.sbuf_usable_end, pl.at - nc.sbuf_usable_end
    xold = nc.alloc_sbuf_tensor_at("xold", [P, 2, T], F32, offset=arena0 + KT * TB + 3 * TB)

    pl = Place(y0)
    fg = pl("fg", [P, D])
    yb = pl("yb", [P, 2, D])
    junk = pl("junk", [P, D])
    fss = pl("fss", [P, 2, 4])
    pl = Place(y0)
    lamraw = nc.alloc_sbuf_tensor_at("lamraw", [P, DEPTH, 4, 64], F32, offset=base)
    lammul = nc.alloc_sbuf_tensor_at("lammul", [P, DEPTH, 2, 64], F32, offset=base + DEPTH * 4 * 64 * 4)

    ps = nc.alloc_psum_tensor("ps", [P, 8, 512], F32)
    flat = ps[:].rearrange("p b n -> p (b n)")

    def group(g):
        return ps[:, 3 * g:3 * g + NC, 0:CH]

    def by_chunk(ap):
        return ap.rearrange("p (c n) -> p c n", n=CH)

    names = """bar setup_load setup_done xtok_ready xtok_used w_load0 w_load1 w_hi w_lo w_used mod_used mod_ready
        sq_ready sq_added ss_done rstd_ready csil_ready cth_ready lprod_ready xtok_done t_ready hi_ready h_ready act_evac dve_evac th_ready masked kv_load mask_load bias_load tab_load rope_load fg_load v_out xh_ready
        ck_done ck_used kc_done kc_used v_done v_hi v_lo vc_hi vc_lo x_split xs_copied q_placed k_placed
        rope_done store k_store o_store fil_done fil_evac g_store
        na_s na_b na_e na_r na_p na_pt na_pth na_ptc na_pv na_o df_s df_m df_e df_p df_pt df_pth df_ptc df_pv df_o
        f_store u_pair pair_copied folded x_done q_done q_copied f_hi f_lo f_ctx
        sqo_ready sso_done sso_read rso_ready out_ready o_load0 o_load1 o_hi o_lo g_load0 g_load1 g_load2 y_added
        x_load0 x_load1 y_hi y_lo fin_tr fin_rs fin_y fin_st0 fin_st1""".split()
    S = namedtuple("Semaphores", names)(*[nc.alloc_semaphore(n) for n in names])
    w_load, o_load, x_load = (S.w_load0, S.w_load1), (S.o_load0, S.o_load1), (S.x_load0, S.x_load1)
    g_load = (S.g_load0, S.g_load1, S.g_load2)
    barriers = {}

    def barrier(eng):
        barriers[eng] = barriers.get(eng, 0) + 1
        eng.drain().then_inc(S.bar, 1)
        eng.wait_ge(S.bar, 5 * barriers[eng])

    evacs = {"act": S.act_evac, "dve": S.dve_evac}

    def evacuated(*c):
        who = ROUTE[c[0]]
        return evacs[who], sum(ROUTE[x[0]] == who for x in JOBS[:JOB_NO[c] + 1])

    def gate_used(l, i):
        if i < KT:
            return evacuated("b", l, "", i)
        return S.y_added, l * 2 * KT + i - KT + 1

    def na_batches(t, e):
        if t == LT:
            return [(4 * LT + e, e, 0, 1, 6 + e)]
        count = len(na_tiles(t))
        return [(4 * t + 2 * e, e, 0, 3, 6), (4 * t + 2 * e + 1, e, 3, count - 3, 7)]

    def na_copies(t, e, first, count, bank, to):
        n = count if first + count < 6 else count - 1
        out = [(to[:, first:first + n, e, :], ps[:, bank, 0:n * P].rearrange("p (t n) -> p t n", n=P))]
        if n < count:
            out.append((to[0:64, 5, e, :], ps[0:64, bank, n * P:n * P + P]))
        return out

    def loaded_no(n):
        return w_load[n % 2], 16 * (n // 2 + 1)

    with nc.Block() as block:

        @block.sync
        def _(sp):
            issued = [0]

            def weights_to(n_end):
                while issued[0] < min(n_end, len(STREAM)):
                    n = issued[0]
                    if n >= 2:
                        before = STREAM[n - 2]
                        if before[0] == "m":
                            sp.wait_ge(S.mod_used, before[1] * MODS + before[3] + 1)
                        else:
                            sp.wait_ge(S.w_lo, SPLIT_NO[before] + 1)
                    c = STREAM[n]
                    src = weight(*c).rearrange("(k p) n -> p k n", p=P)
                    sp.dma_start(wraw[:, n % 2, 0:chunk_k(c), :], src).then_inc(w_load[n % 2], 16)
                    issued[0] += 1

            def weight(kind, l, ph, i):
                def cols(w, m):
                    return w[:, m * P:(m + 1) * P]

                if kind == "m":
                    return cols(w_mod[l], i)
                if kind == "g":
                    return cols(w_in[l], 40 + i)
                if kind == "b":
                    return cols(w_branch[l, i // KT], i % KT)
                if kind == "o":
                    return cols(w_out[l], i)
                if kind == "w":
                    return cols(fnet_w[l], i)
                first = {"na": {"q": 0, "k": 4, "v": 8, "z": 12}, "fn": {"u": 16, "z": 20},
                         "df": {"q": 24, "k": 28, "v": 32, "z": 36}}
                return cols(w_in[l], first[ph][kind] + i)

            def place(n, h, lo, l, ph, p):
                sp.wait_ge(S.x_split, 2 * n + 1)
                for e in range(2):
                    for r, x in enumerate((h, lo)):
                        sp.dma_start(qq[64 * r:64 * r + 64, e, :].bitcast(F32),
                                     x[64 * e:64 * e + 64, 0:T].bitcast(F32)).then_inc(S.q_placed, 16)
                weights_to(CHUNK["z", l, ph, p] + 3)
                sp.wait_ge(S.x_split, 2 * n + 2)
                for x, kk in ((h, kkh), (lo, kkl)):
                    for e in range(2):
                        for r in range(2):
                            sp.dma_start(kk[64 * r:64 * r + 64, e, :].bitcast(F32),
                                         x[64 * e:64 * e + 64, :].bitcast(F32)).then_inc(S.k_placed, 16)
                weights_to(CHUNK["v", l, ph, p] + 3)

            def gate_stores(l, ph, p):
                first = FILL * (p + (HEADS if ph == "df" else 0))
                for i in range(first, first + FILL):
                    weights_to(CHUNK["g", l, "", i] + 4)
                    n = l * 3 * KT + i
                    sp.wait_ge(S.fil_evac, 3 * (n + 1))
                    sp.dma_start(gates_dram[i], gst[:]).then_inc(S.g_store, 16)
                    sp.wait_ge(S.g_store, 16 * (n + 1))

            for out, src in ((craw[:], cvec), (gcol[:], norm_g), (bcol[:], b_mod), (subg[:], subln_g)):
                sp.dma_start(out, src).then_inc(S.setup_load, 16)
            sp.dma_start(lamraw[:], lams.rearrange("(o a) b c -> o a b c", o=1).broadcast_to([P, DEPTH, 4, 64])
                         ).then_inc(S.setup_load, 16)
            sp.dma_start(xtok[:, 0:LT, :], x_sample[0].rearrange("(t p) d -> p t d", p=P)).then_inc(S.xtok_ready, 16)
            sp.dma_start(xtok[:, LT, :], x_prompt[0]).then_inc(S.xtok_ready, 16)
            weights_to(MODS + 2)
            barrier(sp)
            for l in range(DEPTH):
                sp.dma_start(xs_dram.rearrange("k p t -> p k t"), xT[:]).then_inc(S.store, 16)
                weights_to(CHUNK["q", l, "na", 0] + 2)
                sp.wait_ge(S.store, 16 * (l + 1))
                sp.wait_ge(S.h_ready, KT * (l + 1))
                for p in range(HEADS):
                    n, u = 2 * HEADS * l + p, l * HEADS + p
                    if p:
                        sp.wait_ge(S.ck_done, n)
                        sp.wait_ge(S.vc_lo, n)
                        sp.wait_ge(S.na_b, u * 2 * TILES)
                    sp.dma_start(ck[:].rearrange("p (h d) -> p h d", h=2),
                                 cache_na_k[0, l, 2 * p:2 * p + 2].rearrange("h n d -> n h d")).then_inc(S.kv_load, 16)
                    sp.dma_start(vraw[:].rearrange("p (h d) -> p h d", h=2),
                                 cache_na_v[0, l, 2 * p:2 * p + 2].rearrange("h n d -> n h d")).then_inc(S.kv_load, 16)
                    weights_to(CHUNK["k", l, "na", p] + 2)
                    if p == 0:
                        sp.dma_start(mask[:], na_mask).then_inc(S.mask_load, 16)
                    for e in range(2):
                        for r in range(2):
                            for lo, m, at in ((S_MIN, NS, 0), (I_MIN, NI, NS)):
                                r0 = lo - r + WIN - 1
                                sp.dma_start(bias[GW * r:GW * r + GW, e, at:at + m, :],
                                             rpb[l, 2 * p + e, :, r0:r0 + m, :]).then_inc(S.bias_load, 16)
                    place(n, xh, xl, l, "na", p)
                    sp.wait_ge(S.v_out, n + 1)
                    sp.dma_start(new_na_k[0, l, 2 * p:2 * p + 2].rearrange("h n d -> n h d"),
                                 kout[:].rearrange("p (h d) -> p h d", h=2)).then_inc(S.k_store, 16)
                    sp.dma_start(new_na_v[0, l, 2 * p:2 * p + 2].rearrange("h n d -> n h d"),
                                 vout[:].rearrange("p (h d) -> p h d", h=2)).then_inc(S.k_store, 16)
                    gate_stores(l, "na", p)
                    sp.wait_ge(S.na_o, TILES * (u + 1))
                    sp.dma_start(outs_dram[0, p], obuf[:]).then_inc(S.o_store, 16)
                    sp.wait_ge(S.o_store, 16 * (n + 1))
                    sp.wait_ge(S.k_store, 32 * (n + 1))
                barrier(sp)
                for out, src in ((tab_c[:], dft_c), (tab_x[:], dft_x), (tab_t[:], dft_t)):
                    sp.dma_start(out, src).then_inc(S.tab_load, 16)
                for m in range(HEADS):
                    weights_to(CHUNK["w", l, "fn", m] + 4)
                    sp.wait_ge(*evacuated("w", l, "fn", m))
                    sp.dma_start(outs_dram[1, m], fout[:]).then_inc(S.f_store, 16)
                    sp.wait_ge(S.f_store, 16 * (l * HEADS + m + 1))
                barrier(sp)
                sp.dma_start(cosT[:], rope[0]).then_inc(S.rope_load, 16)
                sp.dma_start(sinT[:], rope[1]).then_inc(S.rope_load, 16)
                for h in range(HEADS):
                    n, u = 2 * HEADS * l + HEADS + h, l * HEADS + h
                    if h:
                        sp.wait_ge(S.ck_done, n)
                        sp.wait_ge(S.vc_lo, n)
                    sp.dma_start(ck[:], cache_diff_k[0, l, h]).then_inc(S.kv_load, 16)
                    sp.dma_start(vraw[:], cache_diff_v[0, l, h]).then_inc(S.kv_load, 16)
                    weights_to(CHUNK["k", l, "df", h] + 2)
                    if h:
                        sp.wait_ge(S.out_ready, u)
                        sp.dma_start(outs_dram[2, h - 1], obuf[:]).then_inc(S.o_store, 16)
                    place(n, xh_d, xl_d, l, "df", h)
                    sp.wait_ge(S.v_out, n + 1)
                    sp.dma_start(new_diff_k[0, l, h], kout[:]).then_inc(S.k_store, 16)
                    sp.dma_start(new_diff_v[0, l, h], vout[:]).then_inc(S.k_store, 16)
                    gate_stores(l, "df", h)
                    sp.wait_ge(S.o_store, 16 * n)
                    sp.wait_ge(S.k_store, 32 * (n + 1))
                sp.wait_ge(S.out_ready, (l + 1) * HEADS)
                sp.dma_start(outs_dram[2, HEADS - 1], obuf[:]).then_inc(S.o_store, 16)
                sp.wait_ge(S.o_store, 16 * 2 * HEADS * (l + 1))
                barrier(sp)

                def gate_load(i):
                    n = l * 3 * KT + i
                    if i >= 3:
                        sp.wait_ge(*gate_used(l, i - 3))
                    sp.dma_start(gth[:, i % 3, :], gates_dram[i]).then_inc(g_load[n % 3], 16)

                for i in range(3 * BK):
                    n = l * 3 * BK + i
                    if i >= 2:
                        sp.wait_ge(S.o_lo, n - 1)
                    sp.dma_start(oraw[:, i % 2, :], outs_dram[i // BK, i % BK]).then_inc(o_load[i % 2], 16)
                    if i % BK == BK - 1:
                        gate_load(i // BK)
                for i in range(3 * KT):
                    weights_to(CHUNK["b", l, "", i] + 4)
                    if 1 <= i < 3 * KT - 2:
                        gate_load(i + 2)
                    if i == 2 * KT:
                        sp.wait_ge(S.o_lo, 3 * BK * (l + 1))
                        for m in range(2):
                            sp.dma_start(xold[:, m, :], xs_dram[m]).then_inc(x_load[m], 16)
                for m in range(KT):
                    weights_to(CHUNK["o", l, "", m] + 3)
                    if m >= 2:
                        sp.wait_ge(*evacuated("o", l, "", m - 2))
                        sp.dma_start(xold[:, m % 2, :], xs_dram[m]).then_inc(x_load[m % 2], 16)
                barrier(sp)
            sp.dma_start(fg[:], final_g.rearrange("(o d) -> o d", o=1).broadcast_to([P, D])).then_inc(S.fg_load, 16)
            for t in range(TILES):
                sp.wait_ge(S.fin_y, t + 1)
                out = y_sample[0, t * P:(t + 1) * P, :] if t < LT else y_prompt[0]
                sp.dma_start(out, yb[:, t % 2, :]).then_inc((S.fin_st0, S.fin_st1)[t % 2], 16)
            sp.wait_ge(S.fin_st0, 16 * ((TILES + 1) // 2))
            sp.wait_ge(S.fin_st1, 16 * (TILES // 2))

        @block.tensor
        def _(pe):
            mm = nc.tensor.matmul

            def job(c, mhi, mlo, rows_ready=None):
                s, j, kt = SPLIT_NO[c], JOB_NO[c], chunk_k(c)
                pe.wait_ge(S.w_lo, s + 1)
                if j >= 2:
                    pe.wait_ge(*evacuated(*JOBS[j - 2]))
                for k in range(kt):
                    if rows_ready is not None:
                        pe.wait_ge(rows_ready[0], rows_ready[1] + k + 1)
                    for a, b in ((whi, mhi), (whi, mlo), (wlo, mhi)):
                        for n in range(NC):
                            x = mm(ps[:, 3 * (j % 2) + n, 0:CH], a[:, s % 2, k, :], b[:, k, n * CH:(n + 1) * CH],
                                   start=(k == 0 and a is whi and b is mhi), stop=(k == kt - 1 and a is wlo))
                x.then_inc(S.w_used, 1)

            def filler(l, ph, p, i, bank):
                g, n = divmod(i, NC)
                c = ("g", l, "", FILL * (p + (HEADS if ph == "df" else 0)) + g)
                s, at = SPLIT_NO[c], 3 * (l * 3 * KT + c[3]) + n
                if n == 0:
                    pe.wait_ge(S.w_lo, s + 1)
                if at:
                    pe.wait_ge(S.fil_evac, at)
                for k in range(KT):
                    for a, b in ((whi, hhi), (whi, hlo), (wlo, hhi)):
                        x = mm(ps[:, bank, 0:CH], a[:, s % 2, k, :], b[:, k, n * CH:(n + 1) * CH],
                               start=(k == 0 and a is whi and b is hhi), stop=(k == KT - 1 and a is wlo))
                x.then_inc(S.w_used if n == NC - 1 else S.fil_done, 1)

            def transposed(bank, srcs):
                for j, src in enumerate(srcs):
                    x = nc.tensor.transpose(ps[:, bank, j * P:(j + 1) * P], src, ident[:])
                return x

            def cached_keys(n):
                pe.wait_ge(S.kv_load, 32 * (n + 1))
                transposed(6, [ck[:]]).then_inc(S.ck_done, 1)

            def new_keys(n, x):
                pe.wait_ge(S.ck_used, n + 1)
                pe.wait_ge(S.x_split, 2 * n + 2)
                transposed(6, [x[:, TL + PAST:]]).then_inc(S.kc_done, 1)

            def values_to_rows(n, l, ph, p, vt):
                pe.wait_ge(*evacuated("v", l, ph, p))
                transposed(7, [vt[:, t * P:(t + 1) * P] for t in range(4)]).then_inc(S.v_done, 1)
                pe.wait_ge(S.kc_used, n + 1)
                transposed(6, [vt[:, t * P:(t + 1) * P] for t in range(4, 8)]).then_inc(S.v_done, 1)
                pe.wait_ge(S.v_lo, 3 * n + 1)
                transposed(7, [vt[:, LT * P:]]).then_inc(S.v_done, 1)

            def score(out, e, t, k0, k1):
                q = qq[:, e, t * P:(t + 1) * P]
                mm(out, q, kkh[:, e, k0:k1], start=True, stop=False)
                return mm(out, q, kkl[:, e, k0:k1], start=False, stop=True)

            pe.wait_ge(S.setup_done, 1)
            pe.wait_ge(S.xtok_ready, 32)
            for g in range(2 * TILES):
                t, half = divmod(g, 2)
                if g >= 2:
                    pe.wait_ge(S.xtok_used, g - 1)
                transposed(g % 2, [xtok[:, t, (4 * half + j) * P:(4 * half + j + 1) * P] for j in range(4)]
                           ).then_inc(S.xtok_done, 1)

            def modulation(l, i):
                n = CHUNK["m", l, "", i]
                pe.wait_ge(*loaded_no(n))
                for k in range(KT):
                    x = mm(ps[:, 7, 2 * i:2 * i + 2], wraw[:, n % 2, k, :], csil[:, k, :],
                           start=(k == 0), stop=(k == KT - 1))
                x.then_inc(S.mod_used, 1)

            pe.wait_ge(S.csil_ready, 1)
            for i in range(MODS):
                modulation(0, i)
            barrier(pe)
            for l in range(DEPTH):
                pe.wait_ge(S.sq_added, (KT - 1) * (l + 1))
                for n in range(NC):
                    x = mm(ps[:, n, 0:CH], ones[:], sqs[:, n * CH:(n + 1) * CH], start=True, stop=True)
                x.then_inc(S.ss_done, 1)

                for p in range(HEADS):
                    n, u = 2 * HEADS * l + p, l * HEADS + p
                    u0, b0 = u * 2 * TILES, u * NA_BATCHES
                    if p:
                        pe.wait_ge(S.na_b, u0)
                        pe.wait_ge(S.fil_evac, 3 * (l * 3 * KT + FILL * p))
                    job(("q", l, "na", p), hhi, hlo, (S.h_ready, KT * l) if p == 0 else None)
                    if p:
                        pe.wait_ge(S.na_o, TILES * u)
                    cached_keys(n)
                    for r in "kzv":
                        job((r, l, "na", p), hhi, hlo)
                    new_keys(n, xi)
                    values_to_rows(n, l, "na", p, vT)

                    def scores(t, e):
                        if t >= 1:
                            pe.wait_ge(S.na_b, u0 + 2 * (t - 1) + e + 1)
                        bank = 3 * e
                        if t == LT:
                            x = score(ps[:, bank, 0:P], e, t, TL + PAST, TK)
                        else:
                            lo, rows, _ = window(t)
                            k0, nk = lo * GW, rows * GW
                            score(ps[:, bank, :], e, t, k0, k0 + 512)
                            if nk > 512:
                                score(ps[:, bank + 1, 0:nk - 512], e, t, k0 + 512, k0 + nk)
                            x = score(ps[:, bank + 1, nk - 512:nk - 512 + PAST], e, t, TL, TL + PAST)
                        x.then_inc(S.na_s, 1)

                    def probs_t(t, e):
                        pe.wait_ge(S.na_p, u0 + 2 * t + e + 1)
                        for k, _, first, count, bank in na_batches(t, e):
                            if k >= 2:
                                pe.wait_ge(S.na_ptc, b0 + k - 1)
                            for j in range(count):
                                c0, c1, _ = na_tiles(t)[first + j]
                                x = nc.tensor.transpose(ps[0:c1 - c0, bank, j * P:(j + 1) * P], sn[:, e, c0:c1], ident[:])
                            x.then_inc(S.na_pt, 1)

                    def values(t):
                        pe.wait_ge(S.na_ptc, b0 + na_batches(t, 1)[-1][0] + 1)
                        if t:
                            pe.wait_ge(S.na_o, TILES * u + t)
                        tiles = na_tiles(t)
                        for j, (c0, c1, vtile) in enumerate(tiles):
                            kk = c1 - c0
                            for a, b in ((vhi, pth), (vlo, pth), (vhi, ptl)):
                                x = mm(ps[:, 5, 0:2 * P], a[0:kk, vtile, :], b[0:kk, j], start=(j == 0 and a is vhi and b is pth),
                                       stop=(j == len(tiles) - 1 and b is ptl))
                        x.then_inc(S.na_pv, 1)

                    pe.wait_ge(S.q_placed, 64 * (n + 1))
                    pe.wait_ge(S.k_placed, 128 * (n + 1))
                    pe.wait_ge(S.vc_lo, n + 1)
                    scores(0, 0)
                    scores(0, 1)
                    pe.wait_ge(S.v_lo, 3 * n + 3)
                    for t in range(TILES):
                        probs_t(t, 0)
                        if t + 1 < TILES:
                            scores(t + 1, 0)
                            scores(t + 1, 1)
                        probs_t(t, 1)
                        filler(l, "na", p, t, 2)
                        values(t)
                barrier(pe)

                pe.wait_ge(S.tab_load, 48 * (l + 1))
                job(("u", l, "fn", 0), hhi, hlo)
                for g in range(HEADS):
                    n = l * HEADS + g
                    if g >= 1:
                        pe.wait_ge(S.q_done, 2 * n)
                        pe.wait_ge(S.f_ctx, n)
                    if g + 1 < HEADS:
                        job(("u", l, "fn", g + 1), hhi, hlo)
                    pe.wait_ge(*evacuated("u", l, "fn", g))
                    for j in range(5):
                        if j >= 2:
                            pe.wait_ge(S.folded, n * 5 + j - 1)
                        for i, t in enumerate((j, j + 4) if j < 4 else (8,)):
                            x = mm(ps[:, 6 + j % 2, 256 * i:256 * i + 256], uT[:, g % 2, t * P:(t + 1) * P],
                                   tab_c[:].rearrange("p a b -> p (a b)"), start=True, stop=True)
                        x.then_inc(S.u_pair, 1)
                    pe.wait_ge(S.folded, n * 5 + 5)
                    for i, bank in enumerate((3 * (g % 2), 3 * (g % 2) + 1, 3 * (g % 2) + 2, 6)):
                        x_in, part = ((xsum, 0), (xsum, 1), (xdif, 0), (xdif, 1))[i]
                        width = (HK + 1) if i < 2 else HK
                        for j in range(4):
                            x = mm(ps[:, bank, 0:width], x_in[:, j, part, :], tab_t[:, j, i, 0:width],
                                   start=(j == 0), stop=(j == 3))
                        x.then_inc(S.x_done, 1)
                    for i in range(2):
                        x = mm(ps[:, 7, 0:P], xctx[:, i, :], tab_x[:, i, :], start=(i == 0), stop=(i == 1))
                    x.then_inc(S.x_done, 1)
                pe.wait_ge(S.q_done, 2 * (l + 1) * HEADS)
                pe.wait_ge(S.f_ctx, (l + 1) * HEADS)
                for m in range(HEADS):
                    job(("z", l, "fn", m), hhi, hlo)
                    if m == 0:
                        pe.wait_ge(S.f_lo, (l + 1) * HEADS)
                    job(("w", l, "fn", m), fhi, flo)
                barrier(pe)

                def square_sums(n, chunks):
                    pe.wait_ge(S.sqo_ready, n + 1)
                    for c in chunks:
                        if c == 2:
                            pe.wait_ge(S.sso_read, NC * n + 1)
                        mm(ps[:, 6 + c % 2, 0:CH], ones[:], sqo[:, c * CH:(c + 1) * CH], start=True, stop=True
                           ).then_inc(S.sso_done, 1)

                for h in range(HEADS):
                    n, u = 2 * HEADS * l + HEADS + h, l * HEADS + h
                    n9, g0, o0 = u * TILES, u * (3 * LT + 1), u * 5
                    if h:
                        pe.wait_ge(S.df_e, 2 * n9)
                        pe.wait_ge(S.fil_evac, 3 * (l * 3 * KT + FILL * (HEADS + h)))
                    job(("q", l, "df", h), hhi, hlo)
                    if h:
                        square_sums(u - 1, (0, 1, 2))
                        pe.wait_ge(S.sso_read, NC * u)
                    cached_keys(n)
                    for r in "kzv":
                        job((r, l, "df", h), hhi, hlo)
                    new_keys(n, xi_d)
                    values_to_rows(n, l, "df", h, vT_d)

                    def scores(t, m):
                        if t >= 1:
                            pe.wait_ge(S.df_e, 2 * (n9 + t - 1) + m + 1)
                        if t == LT:
                            x = score(ps[:, 3 * m, 0:P], m, t, TL + PAST, TK)
                        else:
                            for b, (k0, k1) in enumerate(((0, 512), (512, 1024), (1024, 1152))):
                                x = score(ps[:, 3 * m + b, 0:k1 - k0], m, t, k0, k1)
                        x.then_inc(S.df_s, 1)

                    def probs_t(t, g):
                        if g == 0:
                            pe.wait_ge(S.df_p, n9 + t + 1)
                        elif t == LT:
                            return
                        if t or g:
                            pe.wait_ge(S.df_ptc, g0 + 3 * t + g)
                        for j in range(3 if t < LT else 1):
                            kt = 3 * g + j
                            x = nc.tensor.transpose(ps[:, 6, j * P:(j + 1) * P],
                                                    e1[:, t % 3, kt * P:(kt + 1) * P], ident[:])
                        x.then_inc(S.df_pt, 1)

                    def values(pair, fillers):
                        last = 3 * 2 * (pair + 1) if pair < 4 else 3 * LT + 1
                        pe.wait_ge(S.df_ptc, g0 + last)
                        pe.wait_ge(S.fil_evac, 3 * (l * 3 * KT + FILL * (HEADS + h)) + fillers)
                        if pair:
                            pe.wait_ge(S.df_o, o0 + pair)
                        w = 2 * P if pair < 4 else P
                        tiles = [*range(LT), TILES] if pair < 4 else [LT]
                        for j, vtile in enumerate(tiles):
                            for a, b in ((vhi, aTh), (vlo, aTh), (vhi, aTl)):
                                x = mm(ps[:, 7, 0:w], a[:, vtile, :], b[:, j, 0:w],
                                       start=(j == 0 and a is vhi and b is aTh),
                                       stop=(j == len(tiles) - 1 and b is aTl))
                        x.then_inc(S.df_pv, 1)

                    pe.wait_ge(S.q_placed, 64 * (n + 1))
                    pe.wait_ge(S.k_placed, 128 * (n + 1))
                    pe.wait_ge(S.vc_lo, n + 1)
                    scores(0, 0)
                    scores(0, 1)
                    pe.wait_ge(S.v_lo, 3 * n + 3)
                    for t in range(TILES + 1):
                        for g in range(3):
                            if t >= 1:
                                probs_t(t - 1, g)
                            if t + 1 < TILES and g < 2:
                                scores(t + 1, g)
                        if t < TILES:
                            if t >= 3:
                                pe.wait_ge(S.df_o, o0 + (t - 1) // 2)
                            filler(l, "df", h, t, 7)
                        if t % 2 == 0 and t >= 2:
                            values(t // 2 - 1, t + 1)
                    values(4, TILES)
                square_sums((l + 1) * HEADS - 1, (0, 1, 2))
                barrier(pe)

                for i in range(3 * KT):
                    b = i // KT
                    job(("b", l, "", i), omh[b], oml[b], (S.o_lo, 3 * BK * l + b * BK) if i % KT == 0 else None)
                    if l + 1 < DEPTH:
                        modulation(l + 1, i)
                for m in range(KT):
                    job(("o", l, "", m), hhi, hlo, (S.y_lo, KT * l) if m == 0 else None)
                barrier(pe)
            for t in range(TILES):
                if t >= 2:
                    pe.wait_ge(S.fin_y, t - 1)
                for half in range(2):
                    x = transposed(2 * (t % 2) + half, [xT[:, 4 * half + j, t * P:(t + 1) * P] for j in range(4)])
                x.then_inc(S.fin_tr, 1)

        @block.scalar
        def _(act):
            fn = nc.scalar.activation
            split = [0]

            def split_to(s_end):
                while split[0] < min(s_end, len(SPLIT)):
                    s = split[0]
                    n, kt = CHUNK[SPLIT[s]], chunk_k(SPLIT[s])
                    act.wait_ge(*loaded_no(n))
                    if s >= 2:
                        act.wait_ge(S.w_used, s - 1)
                    fn(whi[:, s % 2, 0:kt, :], wraw[:, n % 2, 0:kt, :], ACT.Copy).then_inc(S.w_hi, 1)
                    split[0] += 1

            def projected(*c):
                split_to(SPLIT_NO[c] + 2)
                act.wait_ge(S.w_used, SPLIT_NO[c] + 1)
                return group(JOB_NO[c] % 2)

            def filled(l, ph, p, i, bank):
                g, n = divmod(i, NC)
                c = ("g", l, "", FILL * (p + (HEADS if ph == "df" else 0)) + g)
                at = l * 3 * KT + c[3]
                if n == 0:
                    split_to(SPLIT_NO[c] + 2)
                    if at:
                        act.wait_ge(S.g_store, 16 * at)
                    act.wait_ge(*evacuated("z", l, ph, p))
                if n == NC - 1:
                    act.wait_ge(S.w_used, SPLIT_NO[c] + 1)
                else:
                    act.wait_ge(S.fil_done, (NC - 1) * at + n + 1)
                fn(gst[:, n * CH:(n + 1) * CH], ps[:, bank, 0:CH], ACT.Tanh, scale=0.5).then_inc(S.fil_evac, 1)

            def keys_out(g, outs):
                for out in outs:
                    fn(by_chunk(out[:, 0:2 * CH]), g[:, 0:2], ACT.Copy)
                    fn(out[:, 2 * CH:TL], g[:, 2, 0:TL - 2 * CH], ACT.Copy)
                    x = fn(out[:, TL + PAST:], g[:, 2, TL - 2 * CH:], ACT.Copy)
                return x

            def cached_keys(n, outs):
                act.wait_ge(S.ck_done, n + 1)
                for out in outs:
                    x = fn(out[:, TL:TL + PAST], ps[:, 6, 0:P], ACT.Copy)
                x.then_inc(S.ck_used, 1)

            def gate_tanh(l, ph, p):
                g = projected("z", l, ph, p)
                at = l * 3 * KT + FILL * (p + (HEADS if ph == "df" else 0))
                if at:
                    act.wait_ge(S.g_store, 16 * at)
                fn(by_chunk(gst[:]), g, ACT.Tanh, scale=0.5).then_inc(S.th_ready, 1)

            def rows(n, l, ph, p, vt):
                g = projected("v", l, ph, p)
                fn(by_chunk(vt[:]), g, ACT.Copy).then_inc(S.act_evac, 1)
                act.wait_ge(S.kv_load, 32 * (n + 1))
                fn(vhi[:, TILES, :], vraw[:], ACT.Copy).then_inc(S.vc_hi, 1)
                act.wait_ge(S.kc_done, n + 1)
                if n:
                    act.wait_ge(S.k_store, 32 * n)
                fn(kout[:], ps[:, 6, 0:P], ACT.Copy).then_inc(S.kc_used, 1)
                for i, (bank, a, b) in enumerate(((7, 0, 4), (6, 4, 8), (7, 8, 9))):
                    act.wait_ge(S.v_done, 3 * n + i + 1)
                    src = ps[:, bank, 0:(b - a) * P].rearrange("p (t n) -> p t n", n=P)
                    if i == 2:
                        fn(vout[:], ps[:, bank, 0:P], ACT.Copy).then_inc(S.v_out, 1)
                    fn(vhi[:, a:b, :], src, ACT.Copy).then_inc(S.v_hi, 1)
                split_to(SPLIT_NO["v", l, ph, p] + 3)

            def squares(i, m):
                if m == 0:
                    fn(sqs[:], xT[:, 0, :], ACT.Square).then_inc(S.sq_ready, 1)
                    return
                if m >= 3:
                    act.wait_ge(S.sq_added, (KT - 1) * i + m - 2)
                fn(sq[:, m % 2, :], xT[:, m, :], ACT.Square).then_inc(S.sq_ready, 1)

            act.wait_ge(S.setup_load, 16 * 5)
            fn(cth[:], craw[:], ACT.Tanh, scale=0.5).then_inc(S.cth_ready, 1)
            act.wait_ge(S.lprod_ready, 1)
            fn(lexp[:], lprod[:], ACT.Exp).then_inc(S.cth_ready, 1)
            act.wait_ge(S.xtok_used, 2 * TILES)
            for m in range(KT):
                squares(0, m)
            split_to(2)
            barrier(act)
            for l in range(DEPTH):
                act.wait_ge(S.ss_done, l + 1)
                fn(by_chunk(rstd[:]), group(0), ACT.Ln, bias=eps[:, 0:1], scale=1.0 / D)
                act.drain()
                fn(rstd[:], rstd[:], ACT.Exp, scale=-0.5).then_inc(S.rstd_ready, 1)
                act.wait_ge(S.mod_ready, l + 1)
                for m in range(KT):
                    act.wait_ge(S.t_ready, l * KT + m + 1)
                    for j, (a, b) in enumerate(((0, TL), (TL, T))):
                        x = fn(hhi[:, m, a:b], tn[:, m % 2, a:b], ACT.Identity, bias=modr[:, m, j:j + 1])
                    x.then_inc(S.hi_ready, 1)
                for p in range(HEADS):
                    n, u = 2 * HEADS * l + p, l * HEADS + p
                    g = projected("q", l, "na", p)
                    if p == 0:
                        act.wait_ge(S.store, 16 * (l + 1))
                    fn(by_chunk(xi[:, 0:T]), g, ACT.Copy, scale=0.125)
                    fn(by_chunk(xh[:, 0:T]), g, ACT.Copy, scale=0.125).then_inc(S.act_evac, 1)
                    g = projected("k", l, "na", p)
                    act.wait_ge(S.x_split, 2 * n + 1)
                    act.wait_ge(S.q_placed, 64 * (n + 1))
                    cached_keys(n, (xi, xh))
                    keys_out(g, (xi, xh)).then_inc(S.act_evac, 1)
                    gate_tanh(l, "na", p)
                    rows(n, l, "na", p, vT)
                    u0, b0 = u * 2 * TILES, u * NA_BATCHES

                    def exps(t, e):
                        nk = P if t == LT else window(t)[1] * GW + PAST
                        act.wait_ge(S.na_b, u0 + 2 * t + e + 1)
                        fn(sn[:, e, 0:nk], sn[:, e, 0:nk], ACT.Exp, bias=stat[:, e, 2:3],
                           accum_out=stat[:, e, 3:4]).then_inc(S.na_e, 1)

                    def highs(t, e):
                        for k, _, first, count, bank in na_batches(t, e):
                            act.wait_ge(S.na_pt, b0 + k + 1)
                            if e == 0 and first == 0 and t:
                                act.wait_ge(S.na_pv, TILES * u + t)
                            for out, src in na_copies(t, e, first, count, bank, pth):
                                x = fn(out, src, ACT.Copy)
                            x.then_inc(S.na_pth, 1)

                    exps(0, 0)
                    exps(0, 1)
                    for t in range(TILES):
                        highs(t, 0)
                        if t + 1 < TILES:
                            exps(t + 1, 0)
                        highs(t, 1)
                        if t + 1 < TILES:
                            exps(t + 1, 1)
                        filled(l, "na", p, t, 2)
                    split_to(SPLIT_NO["g", l, "", FILL * p + FILL - 1] + 3)
                barrier(act)

                for g in range(HEADS):
                    n = l * HEADS + g
                    for gg in ((0, 1) if g == 0 else (g + 1,) if g + 1 < HEADS else ()):
                        fn(by_chunk(uT[:, gg % 2, :]), projected("u", l, "fn", gg), ACT.Copy).then_inc(S.act_evac, 1)
                    for j in range(4):
                        act.wait_ge(S.u_pair, 5 * n + j + 1)
                        fn(xcs[:, j].rearrange("p a b -> p (a b)"), ps[:, 6 + j % 2, 0:256], ACT.Copy
                           ).then_inc(S.pair_copied, 1)
                    for i in range(2):
                        act.wait_ge(S.x_done, 5 * n + 2 * i + 2)
                        w = (HK + 1) if i == 0 else HK
                        if g:
                            act.wait_ge(S.q_done, 2 * (n - 1) + i + 1)
                        fn(qsb[:, i, 0:w], ps[:, 3 * (g % 2) + 1 if i == 0 else 6, 0:w], ACT.Copy).then_inc(S.q_copied, 1)
                    act.wait_ge(S.x_done, 5 * n + 5)
                    if g:
                        act.wait_ge(S.f_lo, n)
                    fn(ft[:, TL:], ps[:, 7, 0:P], ACT.Copy).then_inc(S.f_ctx, 1)
                    act.drain()
                    act.wait_ge(S.q_done, 2 * n + 2)
                    fn(fhi[:, g, :], ft[:], ACT.Copy).then_inc(S.f_hi, 1)
                for m in range(HEADS):
                    g = projected("z", l, "fn", m)
                    if m:
                        act.wait_ge(*evacuated("w", l, "fn", m - 1))
                    fn(by_chunk(fth[:]), g, ACT.Tanh, scale=0.5).then_inc(S.th_ready, 1)
                    split_to(SPLIT_NO["w", l, "fn", m] + 3)
                barrier(act)

                def head_norm(n):
                    for c in range(NC):
                        act.wait_ge(S.sso_done, NC * n + c + 1)
                        fn(rso[:, c * CH:(c + 1) * CH], ps[:, 6 + c % 2, 0:CH], ACT.Ln, bias=eps[:, 0:1],
                           scale=1.0 / P).then_inc(S.sso_read, 1)
                    act.drain()
                    fn(rso[:], rso[:], ACT.Exp, scale=-0.5).then_inc(S.rso_ready, 1)

                for h in range(HEADS):
                    n, u = 2 * HEADS * l + HEADS + h, l * HEADS + h
                    n9, g0 = u * TILES, u * (3 * LT + 1)
                    g = projected("q", l, "df", h)
                    fn(by_chunk(xi_d[:, 0:T]), g, ACT.Copy, scale=0.125).then_inc(S.act_evac, 1)
                    if h:
                        head_norm(u - 1)
                    act.wait_ge(S.rope_done, 2 * u + 1)
                    fn(xh_d[:, 0:T], xi_d[:, 0:T], ACT.Copy).then_inc(S.xh_ready, 1)
                    g = projected("k", l, "df", h)
                    act.wait_ge(S.x_split, 2 * n + 1)
                    act.wait_ge(S.q_placed, 64 * (n + 1))
                    cached_keys(n, (xi_d,))
                    keys_out(g, (xi_d,)).then_inc(S.act_evac, 1)
                    act.wait_ge(S.rope_done, 2 * u + 2)
                    fn(xh_d[:], xi_d[:], ACT.Copy).then_inc(S.xh_ready, 1)
                    gate_tanh(l, "df", h)
                    rows(n, l, "df", h, vT_d)

                    def exps(t, m):
                        nk = TC if t == LT else TL + PAST
                        e = (e1, e2)[m]
                        act.wait_ge(S.df_m, 2 * (n9 + t) + m + 1)
                        if t >= 3 and m == 0:
                            act.wait_ge(S.df_pt, g0 + 3 * (t - 2))
                        fn(e[:, t % (3 - m), 0:nk], flat[:, 1536 * m:1536 * m + nk], ACT.Exp,
                           bias=stat[:, t % 2, m:m + 1], accum_out=stat[:, t % 2, 2 + m:3 + m]).then_inc(S.df_e, 1)

                    def highs(t, g):
                        if t == LT and g:
                            return
                        if g == 0 and t % 2 == 0 and t >= 2:
                            act.wait_ge(S.df_pv, u * 5 + t // 2)
                        act.wait_ge(S.df_pt, g0 + 3 * t + g + 1)
                        w = 3 if t < LT else 1
                        fn(aTh[:, 3 * g:3 * g + w, (t % 2) * P:(t % 2 + 1) * P],
                           ps[:, 6, 0:w * P].rearrange("p (t n) -> p t n", n=P), ACT.Copy).then_inc(S.df_pth, 1)

                    exps(0, 0)
                    exps(0, 1)
                    for t in range(TILES + 1):
                        for step in range(5):
                            if step in (0, 1, 3) and t >= 1:
                                highs(t - 1, (0, 1, 0, 2)[step])
                            if step in (2, 4) and t + 1 < TILES:
                                exps(t + 1, step // 2 - 1)
                        if t < TILES:
                            filled(l, "df", h, t, 7)
                    split_to(SPLIT_NO["g", l, "", FILL * (HEADS + h) + FILL - 1] + 3)
                    act.wait_ge(S.df_o, 5 * (u + 1))
                    fn(sqo[:], obuf[:], ACT.Square).then_inc(S.sqo_ready, 1)
                head_norm((l + 1) * HEADS - 1)
                barrier(act)

                for i in range(3 * BK):
                    n = l * 3 * BK + i
                    act.wait_ge(o_load[i % 2], 16 * (n // 2 + 1))
                    fn(omh[i // BK][:, i % BK, :], oraw[:, i % 2, :], ACT.Copy).then_inc(S.o_hi, 1)

                def y_high(m):
                    act.wait_ge(S.y_added, l * 2 * KT + KT + m + 1)
                    act.wait_ge(S.w_used, SPLIT_NO["b", l, "", 2 * KT - 1] + 1)
                    fn(hhi[:, m, :], ysum[:, m, :], ACT.Copy).then_inc(S.y_hi, 1)

                for i in range(3 * KT):
                    split_to(SPLIT_NO["b", l, "", i] + 2)
                    if i > 2 * KT:
                        y_high(i - 2 * KT - 1)
                y_high(KT - 1)
                for m in range(KT):
                    split_to(SPLIT_NO["o", l, "", m] + 2)
                    if l + 1 < DEPTH:
                        act.wait_ge(*evacuated("o", l, "", m))
                        squares(l + 1, m)
                split_to(SPLIT_NO["o", l, "", KT - 1] + 3)
                barrier(act)
            for t in range(TILES):
                act.wait_ge(S.fin_tr, t + 1)
                if t >= 2:
                    act.wait_ge(S.fin_y, t - 1)
                act.drain()
                fn(junk[:], flat[:, 1024 * (t % 2):1024 * (t % 2) + D], ACT.Square, accum_out=fss[:, t % 2, 0:1])
                act.drain()
                fn(fss[:, t % 2, 1:2], fss[:, t % 2, 0:1], ACT.Ln, bias=eps[:, 0:1], scale=1.0 / D)
                act.drain()
                fn(fss[:, t % 2, 2:3], fss[:, t % 2, 1:2], ACT.Exp, scale=-0.5).then_inc(S.fin_rs, 1)

        @block.vector
        def _(dve):
            v = nc.vector
            ths = [0]
            dve.wait_ge(S.setup_load, 16 * 5)
            v.memset(ones[:], 1.0)
            v.memset(eps[:], EPS)
            v.tensor_tensor(lammul[:], lamraw[:, :, 0:4:2, :], lamraw[:, :, 1:4:2, :], ALU.mult)
            dve.drain()
            v.tensor_reduce(lprod[:], lammul[:], AX.X, ALU.add).then_inc(S.lprod_ready, 1)
            dve.wait_ge(S.cth_ready, 2)
            v.scalar_tensor_tensor(out=cth[:], in0=cth[:], scalar=1.0, in1=craw[:], op0=ALU.add, op1=ALU.mult)
            v.tensor_tensor(neglam[:], lexp[:, :, 1], lexp[:, :, 0], ALU.subtract)
            dve.drain()
            v.tensor_scalar(csil[:], cth[:], 0.5, None, ALU.mult).then_inc(S.csil_ready, 1)
            for l in range(DEPTH):
                lam_init = 0.8 - 0.6 * math.exp(-0.3 * l)
                v.tensor_scalar(neglam[:, l:l + 1], neglam[:, l:l + 1], -lam_init, None, ALU.add)
                v.tensor_scalar(subg[:, l:l + 1], subg[:, l:l + 1], 1.0 - lam_init, None, ALU.mult)
            for g in range(2 * TILES):
                t, half = divmod(g, 2)
                dve.wait_ge(S.xtok_done, g + 1)
                v.tensor_copy(xT[:, 4 * half:4 * half + 4, t * P:(t + 1) * P],
                              ps[:, g % 2, :].rearrange("p (k n) -> p k n", k=4)).then_inc(S.xtok_used, 1)
            barrier(dve)
            for l in range(DEPTH):
                dve.wait_ge(S.mod_used, (l + 1) * MODS)
                for j in range(2):
                    v.tensor_tensor(modr[:, :, j], ps[:, 7, j:2 * MODS:2], bcol[:, l, :], ALU.add)
                dve.drain()
                for j in range(2):
                    v.scalar_tensor_tensor(out=mul_a[:, :, j], in0=modr[:, KT:2 * KT, j], scalar=1.0, in1=gcol[:, l, :],
                                           op0=ALU.add, op1=ALU.mult)
                v.tensor_scalar(mul_g[:], modr[:, 2 * KT:, :], 0.25, None, ALU.mult).then_inc(S.mod_ready, 1)
                dve.drain()
                dve.wait_ge(S.rstd_ready, l + 1)

                def scaled(m):
                    for j, (a, b) in enumerate(((0, TL), (TL, T))):
                        x = v.scalar_tensor_tensor(out=tn[:, m % 2, a:b], in0=xT[:, m, a:b], scalar=mul_a[:, m, j:j + 1],
                                                   in1=rstd[:, a:b], op0=ALU.mult, op1=ALU.mult)
                    x.then_inc(S.t_ready, 1)

                def h_low(m):
                    dve.wait_ge(S.hi_ready, l * KT + m + 1)
                    for j, (a, b) in enumerate(((0, TL), (TL, T))):
                        x = v.scalar_tensor_tensor(out=hlo[:, m, a:b], in0=tn[:, m % 2, a:b], scalar=modr[:, m, j:j + 1],
                                                   in1=hhi[:, m, a:b].bitcast(F32), op0=ALU.add, op1=ALU.subtract)
                    x.then_inc(S.h_ready, 1)

                scaled(0)
                for m in range(KT):
                    if m + 1 < KT:
                        dve.drain()
                        scaled(m + 1)
                    h_low(m)

                def silu_gate(g, tanh, out):
                    ths[0] += 1
                    dve.wait_ge(S.th_ready, ths[0])
                    v.scalar_tensor_tensor(out=by_chunk(out[:]), in0=by_chunk(tanh[:]), scalar=1.0, in1=g,
                                           op0=ALU.add, op1=ALU.mult).then_inc(S.dve_evac, 1)

                def value_lows(n):
                    for i, (bank, a, b) in enumerate(((7, 0, 4), (6, 4, 8), (7, 8, 9))):
                        dve.wait_ge(S.v_hi, 3 * n + i + 1)
                        src = ps[:, bank, 0:(b - a) * P].rearrange("p (t n) -> p t n", n=P)
                        v.tensor_tensor(vlo[:, a:b, :], src, vhi[:, a:b, :].bitcast(F32), ALU.subtract
                                        ).then_inc(S.v_lo, 1)

                for p in range(HEADS):
                    n, u = 2 * HEADS * l + p, l * HEADS + p
                    u0, b0 = u * 2 * TILES, u * NA_BATCHES
                    silu_gate(group(JOB_NO["z", l, "na", p] % 2), gst, zs)
                    value_lows(n)

                    def biased(t, e):
                        st = stat[:, e]
                        c0 = 1536 * e
                        dve.wait_ge(S.na_s, u0 + 2 * t + e + 1)
                        if t:
                            dve.wait_ge(S.na_pt, b0 + na_batches(t - 1, e)[-1][0] + 1)
                        if t == LT:
                            v.tensor_copy(sn[:, e, 0:P], flat[:, c0:c0 + P])
                            v.tensor_reduce(st[:, 0:1], flat[:, c0:c0 + P], AX.X, ALU.max)
                            dve.drain()
                            v.tensor_scalar(st[:, 2:3], st[:, 0:1], -1.0, None, ALU.mult).then_inc(S.na_b, 1)
                            return
                        _, m, at = window(t)
                        nk = m * GW
                        v.tensor_tensor_reduce(out=sn[:, e, 0:nk], in0=flat[:, c0:c0 + nk],
                                               in1=bias[:, e, at:at + m, :].rearrange("p a b -> p (a b)"), scale=1.0,
                                               scalar=-3.0e38, op0=ALU.add, op1=ALU.max, accum_out=st[:, 0:1])
                        v.tensor_scalar(sn[:, e, nk:nk + PAST], flat[:, c0 + nk:c0 + nk + PAST], 1.0, None,
                                        ALU.mult, ALU.max, accum_out=st[:, 1:2])
                        dve.drain()
                        v.tensor_scalar(st[:, 2:3], st[:, 0:1], st[:, 1:2], -1.0, ALU.max, ALU.mult
                                        ).then_inc(S.na_b, 1)

                    def normed(t, e):
                        st = stat[:, e]
                        nk = P if t == LT else window(t)[1] * GW + PAST
                        dve.wait_ge(S.na_e, u0 + 2 * t + e + 1)
                        v.reciprocal(st[:, 4:5], st[:, 3:4])
                        dve.drain()
                        v.tensor_scalar(sn[:, e, 0:nk], sn[:, e, 0:nk], st[:, 4:5], None, ALU.mult
                                        ).then_inc(S.na_p, 1)

                    def lows(t, e):
                        for k, _, first, count, bank in na_batches(t, e):
                            dve.wait_ge(S.na_pth, b0 + k + 1)
                            for (out, src), (hi, _) in zip(na_copies(t, e, first, count, bank, ptl),
                                                           na_copies(t, e, first, count, bank, pth)):
                                x = v.tensor_tensor(out, src, hi.bitcast(F32), ALU.subtract)
                            x.then_inc(S.na_ptc, 1)

                    def gated(t):
                        dve.wait_ge(S.na_pv, TILES * u + t + 1)
                        if t == 0 and n:
                            dve.wait_ge(S.o_store, 16 * n)
                        for e in range(2):
                            r = slice(64 * e, 64 * e + 64)
                            x = v.tensor_tensor(obuf[r, P * t:P * t + P], ps[r, 5, P * e:P * e + P],
                                                zs[r, P * t:P * t + P], ALU.mult)
                        x.then_inc(S.na_o, 1)

                    dve.wait_ge(S.masked, u + 1)
                    biased(0, 0)
                    biased(0, 1)
                    normed(0, 0)
                    normed(0, 1)
                    for t in range(TILES):
                        if t:
                            gated(t - 1)
                        lows(t, 0)
                        if t + 1 < TILES:
                            biased(t + 1, 0)
                        lows(t, 1)
                        if t + 1 < TILES:
                            biased(t + 1, 1)
                            normed(t + 1, 0)
                            normed(t + 1, 1)
                    gated(LT)
                barrier(dve)

                for g in range(HEADS):
                    n = l * HEADS + g
                    for j in range(5):
                        if j < 4:
                            dve.wait_ge(S.pair_copied, 4 * n + j + 1)
                            hi = ps[:, 6 + j % 2, 256:512]
                            lo = xcs[:, j].rearrange("p a b -> p (a b)")
                            v.tensor_tensor(xsum[:, j].rearrange("p a b -> p (a b)"), lo, hi, ALU.add)
                            v.tensor_tensor(xdif[:, j].rearrange("p a b -> p (a b)"), lo, hi, ALU.subtract
                                            ).then_inc(S.folded, 1)
                        else:
                            dve.wait_ge(S.u_pair, 5 * n + 5)
                            v.tensor_copy(xctx[:].rearrange("p a b -> p (a b)"), ps[:, 6, 0:256]).then_inc(S.folded, 1)
                    if g:
                        dve.wait_ge(S.f_lo, n)
                    for i in range(2):
                        bank = 3 * (g % 2) + 2 * i
                        first = 1 if i == 0 else 0
                        w = (HK + 1) if i == 0 else HK
                        dve.wait_ge(S.q_copied, 2 * n + i + 1)
                        v.tensor_tensor(ft[:, i:i + 2 * w - 1:2], ps[:, bank, 0:w], qsb[:, i, 0:w], ALU.subtract)
                        v.tensor_tensor(ft[:, TL - 2 * first - i:TL // 2:-2], ps[:, bank, first:HK],
                                        qsb[:, i, first:HK], ALU.add).then_inc(S.q_done, 1)
                for m in range(HEADS):
                    silu_gate(group(JOB_NO["z", l, "fn", m] % 2), fth, fzs)
                    dve.drain()
                    dve.wait_ge(S.w_used, SPLIT_NO["w", l, "fn", m] + 1)
                    if m:
                        dve.wait_ge(S.f_store, 16 * (l * HEADS + m))
                    v.tensor_tensor(by_chunk(fout[:]), group(JOB_NO["w", l, "fn", m] % 2), by_chunk(fzs[:]), ALU.mult
                                    ).then_inc(S.dve_evac, 1)
                barrier(dve)

                def head_out(u):
                    dve.wait_ge(S.rso_ready, u + 1)
                    v.scalar_tensor_tensor(out=obuf[:], in0=obuf[:], scalar=subg[:, l:l + 1], in1=rso[:],
                                           op0=ALU.mult, op1=ALU.mult)
                    dve.drain()
                    v.tensor_tensor(obuf[:], obuf[:], zs[:], ALU.mult).then_inc(S.out_ready, 1)

                dve.wait_ge(S.rope_load, 32 * (l + 1))
                for h in range(HEADS):
                    n, u = 2 * HEADS * l + HEADS + h, l * HEADS + h
                    n9 = u * TILES
                    for r in range(2):
                        dve.wait_ge(*evacuated("qk"[r], l, "df", h))
                        v.stream_shuffle(xr[:, 0:TL], xi_d[:, 0:TL], [(i + 16) % 32 for i in range(32)])
                        dve.drain()
                        v.tensor_tensor(xr[:, 0:TL], xr[:, 0:TL], sinT[:], ALU.mult)
                        v.tensor_tensor(xc[:, 0:TL], xi_d[:, 0:TL], cosT[:], ALU.mult)
                        dve.drain()
                        v.tensor_tensor(xi_d[:, 0:TL], xc[:, 0:TL], xr[:, 0:TL], ALU.add).then_inc(S.rope_done, 1)
                        if r == 0 and h:
                            head_out(u - 1)
                    silu_gate(group(JOB_NO["z", l, "df", h] % 2), gst, zs)
                    value_lows(n)

                    def maxes(t, m):
                        nk = TC if t == LT else TL + PAST
                        dve.wait_ge(S.df_s, 2 * (n9 + t) + m + 1)
                        v.tensor_reduce(stat[:, t % 2, m:m + 1], flat[:, 1536 * m:1536 * m + nk], AX.X, ALU.max,
                                        negate=True).then_inc(S.df_m, 1)

                    def combined(t):
                        st = stat[:, t % 2]
                        nk = TC if t == LT else TL + PAST
                        dve.wait_ge(S.df_e, 2 * (n9 + t) + 2)
                        v.reciprocal(st[:, 4:6], st[:, 2:4])
                        dve.drain()
                        v.tensor_scalar(e2[:, t % 2, 0:nk], e2[:, t % 2, 0:nk], st[:, 5:6], neglam[:, l:l + 1],
                                        ALU.mult, ALU.mult)
                        dve.drain()
                        v.scalar_tensor_tensor(out=e1[:, t % 3, 0:nk], in0=e1[:, t % 3, 0:nk], scalar=st[:, 4:5],
                                               in1=e2[:, t % 2, 0:nk], op0=ALU.mult, op1=ALU.add).then_inc(S.df_p, 1)

                    def lows(t, g):
                        if t == LT and g:
                            return
                        dve.wait_ge(S.df_pth, u * (3 * LT + 1) + 3 * t + g + 1)
                        w = 3 if t < LT else 1
                        at = (slice(None), slice(3 * g, 3 * g + w), slice((t % 2) * P, (t % 2 + 1) * P))
                        v.tensor_tensor(aTl[at], ps[:, 6, 0:w * P].rearrange("p (t n) -> p t n", n=P),
                                        aTh[at].bitcast(F32), ALU.subtract).then_inc(S.df_ptc, 1)

                    def out_pair(pair):
                        w = 2 * P if pair < 4 else P
                        dve.wait_ge(S.df_pv, 5 * u + pair + 1)
                        if pair == 0:
                            dve.wait_ge(S.o_store, 16 * n)
                        v.tensor_copy(obuf[:, 2 * P * pair:2 * P * pair + w], ps[:, 7, 0:w]).then_inc(S.df_o, 1)

                    maxes(0, 0)
                    maxes(0, 1)
                    for t in range(TILES + 1):
                        for g in range(3):
                            if t >= 1:
                                lows(t - 1, g)
                            if t + 1 < TILES and g < 2:
                                maxes(t + 1, g)
                        if t < TILES:
                            combined(t)
                        if t % 2 == 0 and t >= 2:
                            out_pair(t // 2 - 1)
                    out_pair(4)
                head_out((l + 1) * HEADS - 1)
                barrier(dve)

                for i in range(3 * BK):
                    dve.wait_ge(S.o_hi, l * 3 * BK + i + 1)
                    v.tensor_tensor(oml[i // BK][:, i % BK, :], oraw[:, i % 2, :],
                                    omh[i // BK][:, i % BK, :].bitcast(F32), ALU.subtract).then_inc(S.o_lo, 1)

                def y_low(m):
                    dve.wait_ge(S.y_hi, l * KT + m + 1)
                    v.tensor_tensor(hlo[:, m, :], ysum[:, m, :], hhi[:, m, :].bitcast(F32), ALU.subtract
                                    ).then_inc(S.y_lo, 1)

                for i in range(3 * KT):
                    b, m = divmod(i, KT)
                    n = l * 3 * KT + i
                    dve.wait_ge(g_load[n % 3], 16 * (n // 3 + 1))
                    dve.wait_ge(S.w_used, SPLIT_NO["b", l, "", i] + 1)
                    out = ysum[:, m, :] if b == 0 else gth[:, i % 3, :]
                    v.scalar_tensor_tensor(out=by_chunk(out), in0=by_chunk(gth[:, i % 3, :]), scalar=1.0,
                                           in1=group(JOB_NO["b", l, "", i] % 2), op0=ALU.add, op1=ALU.mult
                                           ).then_inc(S.dve_evac, 1)
                    if i >= 2 * KT + 2:
                        y_low(i - 2 * KT - 2)
                y_low(KT - 2)
                y_low(KT - 1)
                for m in range(KT):
                    n = l * KT + m
                    dve.wait_ge(S.w_used, SPLIT_NO["o", l, "", m] + 1)
                    dve.wait_ge(x_load[m % 2], 16 * (n // 2 + 1))
                    g = group(JOB_NO["o", l, "", m] % 2)
                    for src, lo, hi, j in ((g[:, 0:2], 0, 2 * CH, 0), (g[:, 2, 0:TL - 2 * CH], 2 * CH, TL, 0),
                                           (g[:, 2, TL - 2 * CH:], TL, T, 1)):
                        o, r = xT[:, m, lo:hi], xold[:, m % 2, lo:hi]
                        if lo == 0:
                            o, r = by_chunk(o), by_chunk(r)
                        x = v.scalar_tensor_tensor(out=o, in0=src, scalar=mul_g[:, m, j:j + 1], in1=r,
                                                   op0=ALU.mult, op1=ALU.add)
                    x.then_inc(S.dve_evac, 1)
                barrier(dve)
            dve.wait_ge(S.fg_load, 16)
            for t in range(TILES):
                dve.wait_ge(S.fin_rs, t + 1)
                if t >= 2:
                    dve.wait_ge((S.fin_st0, S.fin_st1)[t % 2], 16 * (t // 2))
                v.scalar_tensor_tensor(out=yb[:, t % 2, :], in0=flat[:, 1024 * (t % 2):1024 * (t % 2) + D],
                                       scalar=fss[:, t % 2, 2:3], in1=fg[:], op0=ALU.mult, op1=ALU.mult
                                       ).then_inc(S.fin_y, 1)

        @block.gpsimd
        def _(pool):
            g_ = nc.gpsimd
            split = [0]

            def split_to(s_end):
                while split[0] < min(s_end, len(SPLIT)):
                    s = split[0]
                    n, kt = CHUNK[SPLIT[s]], chunk_k(SPLIT[s])
                    pool.wait_ge(S.w_hi, s + 1)
                    g_.tensor_tensor(wlo[:, s % 2, 0:kt, :], wraw[:, n % 2, 0:kt, :],
                                     whi[:, s % 2, 0:kt, :].bitcast(F32), ALU.subtract).then_inc(S.w_lo, 1)
                    split[0] += 1

            def add_squares(i):
                for m in range(1, KT):
                    if m >= 2:
                        pool.drain()
                    pool.wait_ge(S.sq_ready, i * KT + m + 1)
                    g_.tensor_tensor(sqs[:], sqs[:], sq[:, m % 2, :], ALU.add).then_inc(S.sq_added, 1)
                    yield m

            g_.memset(ident[:], 0.0)
            pool.drain()
            g_.affine_select(out=ident[:], in_=ident[:], compare_op=ALU.not_equal, fill=1.0, base=0,
                             pattern=[[-1, P]], channel_multiplier=1).then_inc(S.setup_done, 1)
            for _ in add_squares(0):
                pass
            split_to(2)
            barrier(pool)
            for l in range(DEPTH):
                for ph in ("na", "fn", "df"):
                    for p in range(HEADS):
                        n = 2 * HEADS * l + (HEADS if ph == "df" else 0) + p
                        if ph == "fn":
                            split_to(SPLIT_NO["u", l, ph, 0] + min(p, 2) + 3)
                            pool.wait_ge(S.f_hi, l * HEADS + p + 1)
                            g_.tensor_tensor(flo[:, p, :], ft[:], fhi[:, p, :].bitcast(F32), ALU.subtract
                                             ).then_inc(S.f_lo, 1)
                            continue
                        x0, x1, x2 = (xi, xh, xl) if ph == "na" else (xi_d, xh_d, xl_d)
                        for r in range(2):
                            split_to(SPLIT_NO["kz"[r], l, ph, p] + 2)
                            if ph == "na":
                                pool.wait_ge(*evacuated("qk"[r], l, ph, p))
                            else:
                                pool.wait_ge(S.xh_ready, 2 * (l * HEADS + p) + r + 1)
                            w = (T, TK)[r]
                            if r:
                                pool.wait_ge(S.q_placed, 64 * (n + 1))
                            g_.tensor_tensor(x2[:, 0:w], x0[:, 0:w], x1[:, 0:w].bitcast(F32), ALU.subtract
                                             ).then_inc(S.x_split, 1)
                        if ph == "na":
                            u = l * HEADS + p
                            pool.wait_ge(S.mask_load, 16 * (l + 1))
                            pool.wait_ge(S.bias_load, 128 * (u + 1))
                            for e in range(2):
                                x = g_.tensor_tensor(bias[:, e], bias[:, e], mask[:], ALU.add)
                            x.then_inc(S.masked, 1)
                        split_to(SPLIT_NO["v", l, ph, p] + 2)
                        pool.wait_ge(S.vc_hi, n + 1)
                        g_.tensor_tensor(vlo[:, TILES, :], vraw[:], vhi[:, TILES, :].bitcast(F32), ALU.subtract
                                         ).then_inc(S.vc_lo, 1)
                        for i in range(FILL):
                            split_to(SPLIT_NO["g", l, "", FILL * (p + (HEADS if ph == "df" else 0)) + i] + 2)
                        split_to(SPLIT_NO["g", l, "", FILL * (p + (HEADS if ph == "df" else 0)) + FILL - 1] + 3)
                    if ph == "fn":
                        split_to(SPLIT_NO["w", l, ph, HEADS - 1] + 3)
                    barrier(pool)
                for i in range(3 * KT):
                    split_to(SPLIT_NO["b", l, "", i] + 2)
                    if i >= KT:
                        pool.wait_ge(*evacuated("b", l, "", i))
                        g_.tensor_tensor(ysum[:, i % KT, :], ysum[:, i % KT, :], gth[:, i % 3, :], ALU.add
                                         ).then_inc(S.y_added, 1)
                adds = add_squares(l + 1)
                for m in range(KT):
                    split_to(SPLIT_NO["o", l, "", m] + 2)
                    if l + 1 < DEPTH and m:
                        next(adds)
                split_to(SPLIT_NO["o", l, "", KT - 1] + 3)
                barrier(pool)


def dft_tables():
    c = np.arange(P)
    ang = 2 * np.pi * (np.outer(c, c) % P) / P
    chan = np.stack([np.cos(ang), np.sin(ang)], 1) / np.sqrt(P)
    ctx = np.stack([np.cos(ang), -np.sin(ang)], 1) / np.sqrt(P)
    tok = np.zeros((4, P, 4, TL // 4 + 2))
    t = np.arange(TL // 2)
    for i in range(4):
        odd = i // 2
        k = 2 * np.arange(TL // 4 + 1 - odd) + odd
        ang = 2 * np.pi * (np.outer(t, k) % TL) / TL
        tok[:, :, i, :len(k)] = ((np.sin if i % 2 else np.cos)(ang) / np.sqrt(TL)).reshape(4, P, len(k))
    return [np.ascontiguousarray(a, np.float32) for a in (chan, ctx, tok.transpose(1, 0, 2, 3))]


def rope_tables():
    t = np.arange(TL)
    inv = (np.float32(10000.0) ** (-np.arange(0, 32, 2, dtype=np.float32) / np.float32(32))).astype(np.float32)
    d = np.arange(P) % 64
    where = np.where((d < 32)[:, None], (t // GW)[None], (t % GW)[None]).astype(np.float32)
    ang = where * inv[d % 16][:, None]
    sign = np.where(d % 32 < 16, -1.0, 1.0)[:, None]
    return np.stack([np.cos(ang), np.sin(ang) * sign]).astype(np.float32)


def window_mask():
    c = np.arange(GW)
    start = np.clip(c - 8, 0, GW - 16)
    out = (c[None] < start[:, None]) | (c[None] >= start[:, None] + 16)
    m = np.zeros((2, GW, NS + NI, GW), bool) | out[None, :, None, :]
    m[0, :, NS + I_MAX - I_MIN] = True
    m[1, :, NS] = True
    return np.where(m, np.float32(-1e30), np.float32(0)).reshape(P, NS + NI, GW)


def kernel(x_prompt, x_sample, cache_na_k, cache_na_v, cache_diff_k, cache_diff_v, c, c_ctx, norm_g, w_mod, b_mod,
           w_in, na_rpb, fnet_w, diff_lq1, diff_lk1, diff_lq2, diff_lk2, diff_subln_g, w_branch, w_out, final_g):
    import concourse.bacc as bacc
    from concourse.bass_utils import run_bass_kernel_spmd

    arr = np.asarray
    padded = np.zeros((DEPTH, 8, 15, PADW), np.float32)
    padded[..., GW - 16:GW + 15] = arr(na_rpb)
    rpb = np.stack([padded[..., GW - 1 - q:2 * GW - 1 - q] for q in range(GW)], 2)
    tables = dft_tables()
    ins = {
        "x_prompt": arr(x_prompt), "x_sample": arr(x_sample), "cache_na_k": arr(cache_na_k),
        "cache_na_v": arr(cache_na_v), "cache_diff_k": arr(cache_diff_k), "cache_diff_v": arr(cache_diff_v),
        "cvec": np.stack([arr(c)[0].reshape(KT, P).T, arr(c_ctx).reshape(KT, P).T], -1),
        "norm_g": arr(norm_g).reshape(DEPTH, KT, P).transpose(2, 0, 1),
        "w_mod": arr(w_mod), "b_mod": arr(b_mod).reshape(DEPTH, MODS, P).transpose(2, 0, 1), "w_in": arr(w_in),
        "rpb": rpb, "fnet_w": arr(fnet_w),
        "lams": np.stack([arr(diff_lq1), arr(diff_lk1), arr(diff_lq2), arr(diff_lk2)], 1),
        "subln_g": arr(diff_subln_g).T, "w_branch": arr(w_branch), "w_out": arr(w_out), "final_g": arr(final_g),
        "na_mask": window_mask(), "rope": rope_tables(), "dft_c": tables[0], "dft_x": tables[1], "dft_t": tables[2],
    }
    ins = {k: np.ascontiguousarray(v) for k, v in ins.items()}
    outs = {
        "y_prompt": (1, TC, D), "y_sample": (1, TL, D), "new_na_k": (1, DEPTH, 8, TC, 64),
        "new_na_v": (1, DEPTH, 8, TC, 64), "new_diff_k": (1, DEPTH, HEADS, TC, P), "new_diff_v": (1, DEPTH, HEADS, TC, P),
    }
    nc = bacc.Bacc("TRN2", target_bir_lowering=False, num_devices=1)
    args = [nc.dram_tensor(n, a.shape, F32, kind="ExternalInput").ap() for n, a in ins.items()]
    args += [nc.dram_tensor(n, s, F32, kind="ExternalOutput").ap() for n, s in outs.items()]
    args.append(nc.dram_tensor("xs_dram", (KT, P, T), F32, kind="Internal").ap())
    args.append(nc.dram_tensor("outs_dram", (3, BK, P, T), F32, kind="Internal").ap())
    args.append(nc.dram_tensor("gates_dram", (3 * KT, P, T), F32, kind="Internal").ap())
    build(nc, *args)
    r = run_bass_kernel_spmd(nc, [ins], core_ids=[0]).results[0]
    return tuple(r[n] for n in outs)
```

```python
import math
from collections import namedtuple

import numpy as np

import concourse.bass as bass
from concourse import mybir

F32 = mybir.dt.float32
F32R = mybir.dt.float32r
ALU = mybir.AluOpType
ACT = mybir.ActivationFunctionType
AX = mybir.AxisListType

P = 128
DEPTH = 2
D = 1024
KT = D // P
TL = 1024
TC = 128
T = TL + TC
TILES = T // P
LT = TL // P
CH = 384
NC = T // CH
PAST = 128
GW = 64
NA_BATCHES = 4 * LT + 2
WIN = 8
HEADS = 4
BW = 512
BK = BW // P
EPS = 1e-6

MODS = 3 * KT
ROUTE = {"z": "dve", "q": "act", "k": "act", "v": "act", "u": "act", "w": "dve", "b": "dve", "o": "dve"}
MOD_AHEAD = 6
MOD_GROUP = 4
FILL = 3


def plan():
    out = []
    for l in range(DEPTH):
        for ph in ("na", "fn", "df"):
            if ph == "fn":
                out += [("u", l, ph, g) for g in range(HEADS)]
                out += [(r, l, ph, m) for m in range(HEADS) for r in "zw"]
                continue
            for p in range(HEADS):
                out += [(r, l, ph, p) for r in "qkvz"]
                at = FILL * (p + (HEADS if ph == "df" else 0))
                out += [("g", l, "", at + i) for i in range(FILL)]
        if l + 1 < DEPTH:
            out += [("m", l + 1, "", i) for i in range(MOD_AHEAD)]
        for i in range(3 * KT):
            out.append(("b", l, "", i))
            if l + 1 < DEPTH and i + MOD_AHEAD < MODS:
                out.append(("m", l + 1, "", i + MOD_AHEAD))
        out += [("o", l, "", m) for m in range(KT)]
    return out


STREAM = plan()
CHUNK = {c: i for i, c in enumerate(STREAM)}
SPLIT = [c for c in STREAM if c[0] != "m"]
SPLIT_NO = {c: i for i, c in enumerate(SPLIT)}
JOBS = [c for c in SPLIT if c[0] != "g"]
JOB_NO = {c: i for i, c in enumerate(JOBS)}


def chunk_k(c):
    return BK if c[0] in "wb" else KT


S_MIN, S_MAX = -6, 7
I_MIN, I_MAX = -4, 4
NS = S_MAX - S_MIN + 1
NI = I_MAX - I_MIN + 1
PADW = 2 * GW - 1


def window(t):
    rows = TL // GW
    lo = min(max(2 * t - WIN // 2, 0), rows - WIN)
    hi = min(max(2 * t + 1 - WIN // 2, 0), rows - WIN) + WIN
    n = hi - lo
    e = (lo - 2 * t - S_MIN) if n == WIN else NS + (lo - 2 * t - I_MIN)
    return lo, n, e


def na_tiles(t):
    if t == LT:
        return [(0, P, LT)]
    lo, n, _ = window(t)
    nk = n * GW
    tiles = [(P * j, P * j + P, lo // 2 + j) for j in range(4)] + [(nk, nk + PAST, TILES)]
    return tiles + ([(512, nk, lo // 2 + 4)] if nk > 512 else [])


def gates_split(l, i, ahead):
    return min(SPLIT_NO["g", l, "", i] + ahead, SPLIT_NO["b", l, "", 0])


def build(nc, x_prompt, x_sample, cache_na_k, cache_na_v, cache_diff_k, cache_diff_v, cvec, norm_g, w_mod,
          b_mod, w_in, rpb, fnet_w, lams, subln_g, w_branch, w_out, final_g, na_mask, rope, dft_c, dft_x, dft_t,
          y_prompt, y_sample, new_na_k, new_na_v, new_diff_k, new_diff_v, xs_dram, outs_dram, gates_dram):
    base = (nc.sbuf_base + 31) // 32 * 32
    TB = T * 4
    TILE_B = P * 4

    class Place:

        def __init__(self, at):
            self.at = at

        def __call__(self, name, shape, dtype=F32):
            size = int(np.prod(shape[1:])) * 4
            t = nc.alloc_sbuf_tensor_at(name, shape, dtype, offset=self.at)
            self.at += (size + 31) // 32 * 32
            return t

    keep = Place(base)
    hhi = keep("hhi", [P, KT, T], F32R)
    hlo = keep("hlo", [P, KT, T], F32R)
    wraw = keep("wraw", [P, 2, KT, P])
    whi = keep("whi", [P, 2, KT, P], F32R)
    wlo = keep("wlo", [P, 2, KT, P], F32R)
    ident = keep("ident", [P, P])
    ones = keep("ones", [P, P])
    eps = keep("eps", [P, 1])
    csil = keep("csil", [P, KT, 2])
    gcol = keep("gcol", [P, DEPTH, KT])
    bcol = keep("bcol", [P, DEPTH, MODS])
    subg = keep("subg", [P, DEPTH])
    modr = keep("modr", [P, MODS, 2])
    mul_a = keep("mul_a", [P, KT, 2])
    mul_g = keep("mul_g", [P, KT, 2])
    neglam = keep("neglam", [P, DEPTH])
    lprod = keep("lprod", [P, DEPTH, 2])
    lexp = keep("lexp", [P, DEPTH, 2])
    cth = keep("cth", [P, KT, 2])
    craw = keep("craw", [P, KT, 2])
    y0 = keep.at
    arena0 = y0 + KT * TB

    TK = T + PAST
    pl = Place(y0)
    ysum = pl("ysum", [P, KT, T])
    assert pl.at == arena0
    xT = pl("xT", [P, KT, T])
    sqs = pl("sqs", [P, T])
    sq = pl("sq", [P, 2, T])
    rstd = pl("rstd", [P, T])
    tn = pl("tn", [P, 2, T])
    assert pl.at <= nc.sbuf_usable_end

    pl = Place(y0)
    xtok = pl("xtok", [P, TILES, D])

    wmod0 = nc.alloc_sbuf_tensor_at("wmod0", [P, 4, KT, MOD_GROUP * P], F32, offset=base)

    pl = Place(y0)
    qq = pl("qq", [P, 2, T], F32R)
    kkh = pl("kkh", [P, 2, TK], F32R)
    kkl = pl("kkl", [P, 2, TK], F32R)
    vhi = pl("vhi", [P, TILES + 1, P], F32R)
    vlo = pl("vlo", [P, TILES + 1, P], F32R)
    vraw = pl("vraw", [P, P])
    vout = pl("vout", [P, P])
    ck = pl("ck", [P, P])
    kout = pl("kout", [P, P])
    gst = pl("gst", [P, T])
    zs = pl("zs", [P, T])
    obuf = pl("obuf", [P, T])
    stat = pl("stat", [P, 2, 8])
    na_at = pl.at
    xi = pl("xi", [P, TK])
    xh = pl("xh", [P, TK], F32R)
    xl = pl("xl", [P, TK], F32R)
    bias = pl("bias", [P, 2, NS + NI, GW])
    mask = pl("mask", [P, NS + NI, GW])
    sn = pl("sn", [P, 2, 704])
    pth = pl("pth", [P, 6, 2, P], F32R)
    ptl = pl("ptl", [P, 6, 2, P], F32R)
    vT = pl("vT", [P, T])
    assert pl.at <= nc.sbuf_usable_end, pl.at - nc.sbuf_usable_end
    pl = Place(na_at)
    e1 = pl("e1", [P, 3, TK])
    e2 = pl("e2", [P, 2, TK])
    aTh = pl("aTh", [P, LT + 1, 2 * P], F32R)
    aTl = pl("aTl", [P, LT + 1, 2 * P], F32R)
    cosT = pl("cosT", [P, TL])
    sinT = pl("sinT", [P, TL])
    assert pl.at <= nc.sbuf_usable_end, pl.at - nc.sbuf_usable_end
    pl = Place(na_at)
    xi_d = pl("xi_d", [P, TK])
    xh_d = pl("xh_d", [P, TK], F32R)
    xl_d = pl("xl_d", [P, TK], F32R)
    xr = pl("xr", [P, TK])
    xc = pl("xc", [P, TK])
    vT_d = pl("vT_d", [P, T])
    xk_d = nc.alloc_sbuf_tensor_at("xk_d", [P, TK], F32, offset=pl.at)
    rso = nc.alloc_sbuf_tensor_at("rso", [P, T], F32, offset=pl.at + TK * 4)
    sqo = gst

    HK = TL // 4
    pl = Place(y0)
    uT = pl("uT", [P, 2, T])
    fth = pl("fth", [P, T])
    fzs = pl("fzs", [P, T])
    fout = pl("fout", [P, T])
    tab_c = pl("tab_c", [P, 2, P])
    tab_x = pl("tab_x", [P, 2, P])
    tab_t = pl("tab_t", [P, 4, 4, HK + 2])
    xcs = pl("xcs", [P, 4, 2, P])
    xsum = pl("xsum", [P, 4, 2, P])
    xdif = pl("xdif", [P, 4, 2, P])
    xctx = pl("xctx", [P, 2, P])
    qsb = pl("qsb", [P, 2, HK + 2])
    ft = pl("ft", [P, T])
    fhi = pl("fhi", [P, HEADS, T], F32R)
    flo = pl("flo", [P, HEADS, T], F32R)
    assert pl.at <= nc.sbuf_usable_end

    HB = BK * TB
    omh = [nc.alloc_sbuf_tensor_at(f"omh{b}", [P, BK, T], F32R, offset=a)
           for b, a in enumerate((base, base + 2 * HB, arena0))]
    oml = [nc.alloc_sbuf_tensor_at(f"oml{b}", [P, BK, T], F32R, offset=a + HB)
           for b, a in enumerate((base, base + 2 * HB, arena0))]
    pl = Place(arena0 + KT * TB)
    pl.at += 3 * TB
    oraw = pl("oraw", [P, 2, T])
    gth = pl("gth", [P, 3, T])
    assert pl.at <= nc.sbuf_usable_end, pl.at - nc.sbuf_usable_end
    xold = nc.alloc_sbuf_tensor_at("xold", [P, 2, T], F32, offset=arena0 + KT * TB + 3 * TB)

    pl = Place(y0)
    fg = pl("fg", [P, D])
    yb = pl("yb", [P, 2, D])
    junk = pl("junk", [P, D])
    fss = pl("fss", [P, 2, 4])
    pl = Place(y0)
    lamraw = nc.alloc_sbuf_tensor_at("lamraw", [P, DEPTH, 4, 64], F32, offset=base + 4 * KT * MOD_GROUP * TILE_B)
    lammul = nc.alloc_sbuf_tensor_at("lammul", [P, DEPTH, 2, 64], F32, offset=base + 4 * KT * MOD_GROUP * TILE_B + DEPTH * 4 * 64 * 4)

    ps = nc.alloc_psum_tensor("ps", [P, 8, 512], F32)
    flat = ps[:].rearrange("p b n -> p (b n)")

    def group(g):
        return ps[:, 3 * g:3 * g + NC, 0:CH]

    def by_chunk(ap):
        return ap.rearrange("p (c n) -> p c n", n=CH)

    names = """bar setup_load m_load0 m_load1 m_load2 m_load3 setup_done xtok_ready xtok_used w_load0 w_load1 w_hi w_lo w_used mod_used mod_ready
        sq_ready sq_added ss_done rstd_ready csil_ready cth_ready lprod_ready xtok_done t_ready hi_ready h_ready act_evac dve_evac th_ready masked kv_load mask_load bias_load tab_load rope_load fg_load v_out xh_ready
        ck_done ck_used kc_done kc_used v_done v_hi v_lo vc_hi vc_lo x_split xs_copied q_placed k_placed
        rope_done store k_store o_store fil_done fil_evac g_store
        na_s na_b na_e na_r na_p na_pt na_pth na_ptc na_pv na_o df_s df_m df_e df_p df_pt df_pth df_ptc df_pv df_o
        f_store u_pair pair_copied folded x_done q_done q_copied f_hi f_lo f_ctx
        sqo_ready sso_done sso_read rso_ready out_ready o_load0 o_load1 o_hi o_lo g_load0 g_load1 g_load2 y_added
        x_load0 x_load1 y_hi y_lo fin_tr fin_rs fin_y fin_st0 fin_st1""".split()
    S = namedtuple("Semaphores", names)(*[nc.alloc_semaphore(n) for n in names])
    w_load, o_load, x_load = (S.w_load0, S.w_load1), (S.o_load0, S.o_load1), (S.x_load0, S.x_load1)
    m_load = (S.m_load0, S.m_load1, S.m_load2, S.m_load3)
    g_load = (S.g_load0, S.g_load1, S.g_load2)
    barriers = {}

    def barrier(eng):
        barriers[eng] = barriers.get(eng, 0) + 1
        eng.drain().then_inc(S.bar, 1)
        eng.wait_ge(S.bar, 5 * barriers[eng])

    evacs = {"act": S.act_evac, "dve": S.dve_evac}

    def evacuated(*c):
        who = ROUTE[c[0]]
        return evacs[who], sum(ROUTE[x[0]] == who for x in JOBS[:JOB_NO[c] + 1])

    def gate_used(l, i):
        if i < KT:
            return evacuated("b", l, "", i)
        return S.y_added, l * 2 * KT + i - KT + 1

    def na_batches(t, e):
        if t == LT:
            return [(4 * LT + e, e, 0, 1, 6 + e)]
        count = len(na_tiles(t))
        return [(4 * t + 2 * e, e, 0, 3, 6), (4 * t + 2 * e + 1, e, 3, count - 3, 7)]

    def na_copies(t, e, first, count, bank, to):
        n = count if first + count < 6 else count - 1
        out = [(to[:, first:first + n, e, :], ps[:, bank, 0:n * P].rearrange("p (t n) -> p t n", n=P))]
        if n < count:
            out.append((to[0:64, 5, e, :], ps[0:64, bank, n * P:n * P + P]))
        return out

    def loaded_no(n):
        return w_load[n % 2], 16 * (n // 2 + 1)

    with nc.Block() as block:

        @block.sync
        def _(sp):
            issued = [0]

            def weights_to(n_end):
                while issued[0] < min(n_end, len(STREAM)):
                    n = issued[0]
                    if n >= 2:
                        before = STREAM[n - 2]
                        if before[0] == "m":
                            sp.wait_ge(S.mod_used, before[1] * MODS + before[3] + 1)
                        else:
                            sp.wait_ge(S.w_lo, SPLIT_NO[before] + 1)
                    c = STREAM[n]
                    src = weight(*c).rearrange("(k p) n -> p k n", p=P)
                    sp.dma_start(wraw[:, n % 2, 0:chunk_k(c), :], src).then_inc(w_load[n % 2], 16)
                    issued[0] += 1

            def weight(kind, l, ph, i):
                def cols(w, m):
                    return w[:, m * P:(m + 1) * P]

                if kind == "m":
                    return cols(w_mod[l], i)
                if kind == "g":
                    return cols(w_in[l], 40 + i)
                if kind == "b":
                    return cols(w_branch[l, i // KT], i % KT)
                if kind == "o":
                    return cols(w_out[l], i)
                if kind == "w":
                    return cols(fnet_w[l], i)
                first = {"na": {"q": 0, "k": 4, "v": 8, "z": 12}, "fn": {"u": 16, "z": 20},
                         "df": {"q": 24, "k": 28, "v": 32, "z": 36}}
                return cols(w_in[l], first[ph][kind] + i)

            def place(n, h, lo, l, ph, p):
                sp.wait_ge(S.x_split, 2 * n + 1)
                for e in range(2):
                    for r, x in enumerate((h, lo)):
                        sp.dma_start(qq[64 * r:64 * r + 64, e, :].bitcast(F32),
                                     x[64 * e:64 * e + 64, 0:T].bitcast(F32)).then_inc(S.q_placed, 16)
                weights_to(CHUNK["v", l, ph, p] + 3)
                sp.wait_ge(S.x_split, 2 * n + 2)
                for x, kk in ((h, kkh), (lo, kkl)):
                    for e in range(2):
                        for r in range(2):
                            sp.dma_start(kk[64 * r:64 * r + 64, e, :].bitcast(F32),
                                         x[64 * e:64 * e + 64, :].bitcast(F32)).then_inc(S.k_placed, 16)
                weights_to(CHUNK["z", l, ph, p] + 3)

            def gate_stores(l, ph, p):
                first = FILL * (p + (HEADS if ph == "df" else 0))
                for i in range(first, first + FILL):
                    weights_to(min(CHUNK["g", l, "", i] + 4, CHUNK["g", l, "", 3 * KT - 1] + 3))
                    n = l * 3 * KT + i
                    sp.wait_ge(S.fil_evac, 3 * (n + 1))
                    sp.dma_start(gates_dram[i], gst[:]).then_inc(S.g_store, 16)
                    sp.wait_ge(S.g_store, 16 * (n + 1))

            for out, src in ((craw[:], cvec), (gcol[:], norm_g), (bcol[:], b_mod), (subg[:], subln_g)):
                sp.dma_start(out, src).then_inc(S.setup_load, 16)
            sp.dma_start(lamraw[:], lams.rearrange("(o a) b c -> o a b c", o=1).broadcast_to([P, DEPTH, 4, 64])
                         ).then_inc(S.setup_load, 16)
            sp.dma_start(xtok[:, 0:LT, :], x_sample[0].rearrange("(t p) d -> p t d", p=P)).then_inc(S.xtok_ready, 16)
            sp.dma_start(xtok[:, LT, :], x_prompt[0]).then_inc(S.xtok_ready, 16)
            for g in range(MODS // MOD_GROUP):
                if g >= 4:
                    sp.wait_ge(S.mod_used, MOD_GROUP * (g - 3))
                cols = slice(g * MOD_GROUP * P, (g + 1) * MOD_GROUP * P)
                sp.dma_start(wmod0[:, g % 4], w_mod[0, :, cols].rearrange("(k p) n -> p k n", p=P)
                             ).then_inc(m_load[g % 4], 16)
            weights_to(2)
            barrier(sp)
            for l in range(DEPTH):
                sp.dma_start(xs_dram.rearrange("k p t -> p k t"), xT[:]).then_inc(S.store, 16)
                weights_to(CHUNK["q", l, "na", 0] + 2)
                sp.wait_ge(S.store, 16 * (l + 1))
                sp.wait_ge(S.h_ready, KT * (l + 1))
                for p in range(HEADS):
                    n, u = 2 * HEADS * l + p, l * HEADS + p
                    if p:
                        sp.wait_ge(S.ck_done, n)
                        sp.wait_ge(S.vc_lo, n)
                        sp.wait_ge(S.na_b, u * 2 * TILES)
                    sp.dma_start(ck[:].rearrange("p (h d) -> p h d", h=2),
                                 cache_na_k[0, l, 2 * p:2 * p + 2].rearrange("h n d -> n h d")).then_inc(S.kv_load, 16)
                    sp.dma_start(vraw[:].rearrange("p (h d) -> p h d", h=2),
                                 cache_na_v[0, l, 2 * p:2 * p + 2].rearrange("h n d -> n h d")).then_inc(S.kv_load, 16)
                    weights_to(CHUNK["k", l, "na", p] + 2)
                    if p == 0:
                        sp.dma_start(mask[:], na_mask).then_inc(S.mask_load, 16)
                    for e in range(2):
                        for r in range(2):
                            for lo, m, at in ((S_MIN, NS, 0), (I_MIN, NI, NS)):
                                r0 = lo - r + WIN - 1
                                sp.dma_start(bias[GW * r:GW * r + GW, e, at:at + m, :],
                                             rpb[l, 2 * p + e, :, r0:r0 + m, :]).then_inc(S.bias_load, 16)
                    place(n, xh, xl, l, "na", p)
                    sp.wait_ge(S.v_out, n + 1)
                    sp.dma_start(new_na_k[0, l, 2 * p:2 * p + 2].rearrange("h n d -> n h d"),
                                 kout[:].rearrange("p (h d) -> p h d", h=2)).then_inc(S.k_store, 16)
                    sp.dma_start(new_na_v[0, l, 2 * p:2 * p + 2].rearrange("h n d -> n h d"),
                                 vout[:].rearrange("p (h d) -> p h d", h=2)).then_inc(S.k_store, 16)
                    gate_stores(l, "na", p)
                    sp.wait_ge(S.na_o, TILES * (u + 1))
                    sp.dma_start(outs_dram[0, p], obuf[:]).then_inc(S.o_store, 16)
                    sp.wait_ge(S.o_store, 16 * (n + 1))
                    sp.wait_ge(S.k_store, 32 * (n + 1))
                barrier(sp)
                for out, src in ((tab_c[:], dft_c), (tab_x[:], dft_x), (tab_t[:], dft_t)):
                    sp.dma_start(out, src).then_inc(S.tab_load, 16)
                for m in range(HEADS):
                    weights_to(CHUNK["w", l, "fn", m] + 4)
                    sp.wait_ge(*evacuated("w", l, "fn", m))
                    sp.dma_start(outs_dram[1, m], fout[:]).then_inc(S.f_store, 16)
                    sp.wait_ge(S.f_store, 16 * (l * HEADS + m + 1))
                barrier(sp)
                sp.dma_start(cosT[:], rope[0]).then_inc(S.rope_load, 16)
                sp.dma_start(sinT[:], rope[1]).then_inc(S.rope_load, 16)
                for h in range(HEADS):
                    n, u = 2 * HEADS * l + HEADS + h, l * HEADS + h
                    if h:
                        sp.wait_ge(S.ck_done, n)
                        sp.wait_ge(S.vc_lo, n)
                    sp.dma_start(ck[:], cache_diff_k[0, l, h]).then_inc(S.kv_load, 16)
                    sp.dma_start(vraw[:], cache_diff_v[0, l, h]).then_inc(S.kv_load, 16)
                    weights_to(CHUNK["k", l, "df", h] + 2)
                    place(n, xh_d, xl_d, l, "df", h)
                    if h:
                        sp.wait_ge(S.out_ready, u)
                        sp.dma_start(outs_dram[2, h - 1], obuf[:]).then_inc(S.o_store, 16)
                    sp.wait_ge(S.v_out, n + 1)
                    sp.dma_start(new_diff_k[0, l, h], kout[:]).then_inc(S.k_store, 16)
                    sp.dma_start(new_diff_v[0, l, h], vout[:]).then_inc(S.k_store, 16)
                    gate_stores(l, "df", h)
                    sp.wait_ge(S.o_store, 16 * n)
                    sp.wait_ge(S.k_store, 32 * (n + 1))
                sp.wait_ge(S.out_ready, (l + 1) * HEADS)
                sp.dma_start(outs_dram[2, HEADS - 1], obuf[:]).then_inc(S.o_store, 16)
                sp.wait_ge(S.o_store, 16 * 2 * HEADS * (l + 1))
                barrier(sp)

                def gate_load(i):
                    n = l * 3 * KT + i
                    if i >= 3:
                        sp.wait_ge(*gate_used(l, i - 3))
                    sp.dma_start(gth[:, i % 3, :], gates_dram[i]).then_inc(g_load[n % 3], 16)

                def out_load(i):
                    if i >= 2:
                        sp.wait_ge(S.o_lo, l * 3 * BK + i - 1)
                    sp.dma_start(oraw[:, i % 2, :], outs_dram[i // BK, i % BK]).then_inc(o_load[i % 2], 16)

                for i in range(BK):
                    out_load(i)
                    if l + 1 < DEPTH:
                        weights_to(CHUNK["m", l + 1, "", 0] + 3 + i)
                for i in range(3):
                    gate_load(i)
                for i in range(3 * KT):
                    weights_to(CHUNK["b", l, "", i] + 4)
                    if i < 2 * BK:
                        out_load(BK + i)
                    if 1 <= i < 3 * KT - 2:
                        gate_load(i + 2)
                    if i == 2 * KT:
                        sp.wait_ge(S.o_lo, 3 * BK * (l + 1))
                        for m in range(2):
                            sp.dma_start(xold[:, m, :], xs_dram[m]).then_inc(x_load[m], 16)
                for m in range(KT):
                    weights_to(CHUNK["o", l, "", m] + 3)
                    if m >= 2:
                        sp.wait_ge(*evacuated("o", l, "", m - 2))
                        sp.dma_start(xold[:, m % 2, :], xs_dram[m]).then_inc(x_load[m % 2], 16)
                barrier(sp)
            sp.dma_start(fg[:], final_g.rearrange("(o d) -> o d", o=1).broadcast_to([P, D])).then_inc(S.fg_load, 16)
            for t in range(TILES):
                sp.wait_ge(S.fin_y, t + 1)
                out = y_sample[0, t * P:(t + 1) * P, :] if t < LT else y_prompt[0]
                sp.dma_start(out, yb[:, t % 2, :]).then_inc((S.fin_st0, S.fin_st1)[t % 2], 16)
            sp.wait_ge(S.fin_st0, 16 * ((TILES + 1) // 2))
            sp.wait_ge(S.fin_st1, 16 * (TILES // 2))

        @block.tensor
        def _(pe):
            mm = nc.tensor.matmul

            def job(c, mhi, mlo, rows_ready=None, between={}):
                s, j, kt = SPLIT_NO[c], JOB_NO[c], chunk_k(c)
                pe.wait_ge(S.w_lo, s + 1)
                if j >= 2:
                    pe.wait_ge(*evacuated(*JOBS[j - 2]))
                for k in range(kt):
                    if rows_ready is not None:
                        pe.wait_ge(rows_ready[0], rows_ready[1] + k + 1)
                    for a, b in ((whi, mhi), (whi, mlo), (wlo, mhi)):
                        for n in range(NC):
                            x = mm(ps[:, 3 * (j % 2) + n, 0:CH], a[:, s % 2, k, :], b[:, k, n * CH:(n + 1) * CH],
                                   start=(k == 0 and a is whi and b is mhi), stop=(k == kt - 1 and a is wlo))
                    if k == kt - 1:
                        x.then_inc(S.w_used, 1)
                    for step in between.get(k, ()):
                        step()

            def filler(l, ph, p, i, bank, k0=0, k1=KT):
                g, n = divmod(i, NC)
                c = ("g", l, "", FILL * (p + (HEADS if ph == "df" else 0)) + g)
                s, at = SPLIT_NO[c], 3 * (l * 3 * KT + c[3]) + n
                if n == 0 and k0 == 0:
                    pe.wait_ge(S.w_lo, s + 1)
                if at and k0 == 0:
                    pe.wait_ge(S.fil_evac, at)
                for k in range(k0, k1):
                    for a, b in ((whi, hhi), (whi, hlo), (wlo, hhi)):
                        x = mm(ps[:, bank, 0:CH], a[:, s % 2, k, :], b[:, k, n * CH:(n + 1) * CH],
                               start=(k == 0 and a is whi and b is hhi), stop=(k == KT - 1 and a is wlo))
                if k1 == KT:
                    x.then_inc(S.w_used if n == NC - 1 else S.fil_done, 1)

            def transposed(bank, srcs):
                for j, src in enumerate(srcs):
                    x = nc.tensor.transpose(ps[:, bank, j * P:(j + 1) * P], src, ident[:])
                return x

            def cached_keys(n):
                pe.wait_ge(S.kv_load, 32 * (n + 1))
                transposed(6, [ck[:]]).then_inc(S.ck_done, 1)

            def new_keys(n, x):
                pe.wait_ge(S.ck_used, n + 1)
                pe.wait_ge(S.x_split, 2 * n + 2)
                transposed(6, [x[:, TL + PAST:]]).then_inc(S.kc_done, 1)

            def values_to_rows(n, l, ph, p, vt, i):
                if i == 0:
                    pe.wait_ge(*evacuated("v", l, ph, p))
                if i == 1:
                    pe.wait_ge(S.kc_used, n + 1)
                if i == 2:
                    pe.wait_ge(S.v_lo, 3 * n + 1)
                transposed((7, 6, 7)[i], [vt[:, t * P:(t + 1) * P] for t in range(4 * i, min(4 * i + 4, TILES))]
                           ).then_inc(S.v_done, 1)

            def gate_job(n, l, ph, p, x, vt):
                def batch(i):
                    return lambda: values_to_rows(n, l, ph, p, vt, i)

                job(("z", l, ph, p), hhi, hlo,
                    between={1: (lambda: new_keys(n, x),), 2: (batch(0),), 3: (batch(1),), 5: (batch(2),)})

            def score(out, e, t, k0, k1):
                q = qq[:, e, t * P:(t + 1) * P]
                mm(out, q, kkh[:, e, k0:k1], start=True, stop=False)
                return mm(out, q, kkl[:, e, k0:k1], start=False, stop=True)

            pe.wait_ge(S.setup_done, 1)
            pe.wait_ge(S.xtok_ready, 32)
            for g in range(2 * TILES):
                t, half = divmod(g, 2)
                if g >= 2:
                    pe.wait_ge(S.xtok_used, g - 1)
                transposed(g % 2, [xtok[:, t, (4 * half + j) * P:(4 * half + j + 1) * P] for j in range(4)]
                           ).then_inc(S.xtok_done, 1)

            def modulation(l, i):
                if l:
                    n = CHUNK["m", l, "", i]
                    pe.wait_ge(*loaded_no(n))
                    w = wraw[:, n % 2]
                else:
                    g, j = divmod(i, MOD_GROUP)
                    pe.wait_ge(m_load[g % 4], 16 * (g // 4 + 1))
                    w = wmod0[:, g % 4, :, j * P:(j + 1) * P]
                for k in range(KT):
                    x = mm(ps[:, 7, 2 * i:2 * i + 2], w[:, k, :], csil[:, k, :],
                           start=(k == 0), stop=(k == KT - 1))
                x.then_inc(S.mod_used, 1)

            pe.wait_ge(S.csil_ready, 1)
            for i in range(MODS):
                modulation(0, i)
            barrier(pe)
            for l in range(DEPTH):
                pe.wait_ge(S.sq_added, (KT - 1) * (l + 1))
                for n in range(NC):
                    x = mm(ps[:, n, 0:CH], ones[:], sqs[:, n * CH:(n + 1) * CH], start=True, stop=True)
                x.then_inc(S.ss_done, 1)

                for p in range(HEADS):
                    n, u = 2 * HEADS * l + p, l * HEADS + p
                    u0, b0 = u * 2 * TILES, u * NA_BATCHES
                    if p:
                        pe.wait_ge(S.na_b, u0)
                        pe.wait_ge(S.fil_evac, 3 * (l * 3 * KT + FILL * p))
                    job(("q", l, "na", p), hhi, hlo, (S.h_ready, KT * l) if p == 0 else None)
                    if p:
                        pe.wait_ge(S.na_o, TILES * u)
                    cached_keys(n)
                    job(("k", l, "na", p), hhi, hlo)
                    job(("v", l, "na", p), hhi, hlo)
                    gate_job(n, l, "na", p, xi, vT)

                    def scores(t, e):
                        if t >= 1:
                            pe.wait_ge(S.na_b, u0 + 2 * (t - 1) + e + 1)
                        bank = 3 * e
                        if t == LT:
                            x = score(ps[:, bank, 0:P], e, t, TL + PAST, TK)
                        else:
                            lo, rows, _ = window(t)
                            k0, nk = lo * GW, rows * GW
                            score(ps[:, bank, :], e, t, k0, k0 + 512)
                            if nk > 512:
                                score(ps[:, bank + 1, 0:nk - 512], e, t, k0 + 512, k0 + nk)
                            x = score(ps[:, bank + 1, nk - 512:nk - 512 + PAST], e, t, TL, TL + PAST)
                        x.then_inc(S.na_s, 1)

                    def probs_t(t, e):
                        pe.wait_ge(S.na_p, u0 + 2 * t + e + 1)
                        for k, _, first, count, bank in na_batches(t, e):
                            if k >= 2:
                                pe.wait_ge(S.na_ptc, b0 + k - 1)
                            for j in range(count):
                                c0, c1, _ = na_tiles(t)[first + j]
                                x = nc.tensor.transpose(ps[0:c1 - c0, bank, j * P:(j + 1) * P], sn[:, e, c0:c1], ident[:])
                            x.then_inc(S.na_pt, 1)

                    def values(t):
                        pe.wait_ge(S.na_ptc, b0 + na_batches(t, 1)[-1][0] + 1)
                        if t:
                            pe.wait_ge(S.na_o, TILES * u + t)
                        tiles = na_tiles(t)
                        for j, (c0, c1, vtile) in enumerate(tiles):
                            kk = c1 - c0
                            for a, b in ((vhi, pth), (vlo, pth), (vhi, ptl)):
                                x = mm(ps[:, 5, 0:2 * P], a[0:kk, vtile, :], b[0:kk, j], start=(j == 0 and a is vhi and b is pth),
                                       stop=(j == len(tiles) - 1 and b is ptl))
                        x.then_inc(S.na_pv, 1)

                    pe.wait_ge(S.q_placed, 64 * (n + 1))
                    pe.wait_ge(S.k_placed, 128 * (n + 1))
                    pe.wait_ge(S.vc_lo, n + 1)
                    scores(0, 0)
                    filler(l, "na", p, 0, 2)
                    pe.wait_ge(*evacuated("z", l, "na", p))
                    scores(0, 1)
                    pe.wait_ge(S.v_lo, 3 * n + 3)
                    for t in range(TILES):
                        probs_t(t, 0)
                        if t + 1 < TILES:
                            scores(t + 1, 0)
                            scores(t + 1, 1)
                        probs_t(t, 1)
                        if t:
                            filler(l, "na", p, t, 2)
                        values(t)
                barrier(pe)

                job(("u", l, "fn", 0), hhi, hlo)
                pe.wait_ge(S.tab_load, 48 * (l + 1))
                for g in range(HEADS):
                    n = l * HEADS + g
                    if g >= 1:
                        pe.wait_ge(S.q_done, 2 * n)
                        pe.wait_ge(S.f_ctx, n)
                    if g + 1 < HEADS:
                        job(("u", l, "fn", g + 1), hhi, hlo)
                    pe.wait_ge(*evacuated("u", l, "fn", g))
                    for j in range(5):
                        if j >= 2:
                            pe.wait_ge(S.folded, n * 5 + j - 1)
                        for i, t in enumerate((j, j + 4) if j < 4 else (8,)):
                            x = mm(ps[:, 6 + j % 2, 256 * i:256 * i + 256], uT[:, g % 2, t * P:(t + 1) * P],
                                   tab_c[:].rearrange("p a b -> p (a b)"), start=True, stop=True)
                        x.then_inc(S.u_pair, 1)
                    pe.wait_ge(S.folded, n * 5 + 5)
                    for i, bank in enumerate((3 * (g % 2), 3 * (g % 2) + 1, 3 * (g % 2) + 2, 6)):
                        x_in, part = ((xsum, 0), (xsum, 1), (xdif, 0), (xdif, 1))[i]
                        width = (HK + 1) if i < 2 else HK
                        for j in range(4):
                            x = mm(ps[:, bank, 0:width], x_in[:, j, part, :], tab_t[:, j, i, 0:width],
                                   start=(j == 0), stop=(j == 3))
                        x.then_inc(S.x_done, 1)
                    for i in range(2):
                        x = mm(ps[:, 7, 0:P], xctx[:, i, :], tab_x[:, i, :], start=(i == 0), stop=(i == 1))
                    x.then_inc(S.x_done, 1)
                pe.wait_ge(S.q_done, 2 * (l + 1) * HEADS)
                pe.wait_ge(S.f_ctx, (l + 1) * HEADS)
                for m in range(HEADS):
                    job(("z", l, "fn", m), hhi, hlo)
                    if m == 0:
                        pe.wait_ge(S.f_lo, (l + 1) * HEADS)
                    job(("w", l, "fn", m), fhi, flo)
                barrier(pe)

                def square_sums(n, chunks):
                    pe.wait_ge(S.sqo_ready, n + 1)
                    for c in chunks:
                        if c == 2:
                            pe.wait_ge(S.sso_read, NC * n + 1)
                        mm(ps[:, 6 + c % 2, 0:CH], ones[:], sqo[:, c * CH:(c + 1) * CH], start=True, stop=True
                           ).then_inc(S.sso_done, 1)

                def values(u, pair, gates):
                    last = 3 * 2 * (pair + 1) if pair < 4 else 3 * LT + 1
                    pe.wait_ge(S.df_ptc, u * (3 * LT + 1) + last)
                    pe.wait_ge(S.fil_evac, 3 * l * 3 * KT + gates)
                    if pair:
                        pe.wait_ge(S.df_o, 5 * u + pair)
                    w = 2 * P if pair < 4 else P
                    tiles = [*range(LT), TILES] if pair < 4 else [LT]
                    for j, vtile in enumerate(tiles):
                        for a, b in ((vhi, aTh), (vlo, aTh), (vhi, aTl)):
                            x = mm(ps[:, 7, 0:w], a[:, vtile, :], b[:, j, 0:w],
                                   start=(j == 0 and a is vhi and b is aTh),
                                   stop=(j == len(tiles) - 1 and b is aTl))
                    x.then_inc(S.df_pv, 1)

                for h in range(HEADS):
                    n, u = 2 * HEADS * l + HEADS + h, l * HEADS + h
                    n9, g0, o0 = u * TILES, u * (3 * LT + 1), u * 5
                    if h:
                        pe.wait_ge(S.df_e, 2 * n9)
                        pe.wait_ge(S.fil_evac, 3 * (l * 3 * KT + FILL * (HEADS + h)))
                    job(("q", l, "df", h), hhi, hlo)
                    if h:
                        values(u - 1, 4, FILL * (HEADS + h) * 3)
                    cached_keys(n)
                    job(("k", l, "df", h), hhi, hlo)
                    if h:
                        pe.wait_ge(S.ck_used, n + 1)
                        square_sums(u - 1, (0, 1))
                    job(("v", l, "df", h), hhi, hlo)
                    if h:
                        square_sums(u - 1, (2,))
                        pe.wait_ge(S.sso_read, NC * u)
                    gate_job(n, l, "df", h, xk_d, vT_d)

                    def scores(t, m):
                        if t >= 1:
                            pe.wait_ge(S.df_e, 2 * (n9 + t - 1) + m + 1)
                        if t == LT:
                            x = score(ps[:, 3 * m, 0:P], m, t, TL + PAST, TK)
                        else:
                            for b, (k0, k1) in enumerate(((0, 512), (512, 1024), (1024, 1152))):
                                x = score(ps[:, 3 * m + b, 0:k1 - k0], m, t, k0, k1)
                        x.then_inc(S.df_s, 1)

                    def probs_t(t, g):
                        if g == 0:
                            pe.wait_ge(S.df_p, n9 + t + 1)
                        elif t == LT:
                            return
                        if t or g:
                            pe.wait_ge(S.df_ptc, g0 + 3 * t + g)
                        for j in range(3 if t < LT else 1):
                            kt = 3 * g + j
                            x = nc.tensor.transpose(ps[:, 6, j * P:(j + 1) * P],
                                                    e1[:, t % 3, kt * P:(kt + 1) * P], ident[:])
                        x.then_inc(S.df_pt, 1)

                    pe.wait_ge(S.q_placed, 64 * (n + 1))
                    pe.wait_ge(S.k_placed, 128 * (n + 1))
                    pe.wait_ge(S.vc_lo, n + 1)
                    scores(0, 0)
                    pe.wait_ge(S.v_lo, 3 * n + 3)
                    filler(l, "df", h, 0, 7, 0, 6)
                    pe.wait_ge(*evacuated("z", l, "df", h))
                    scores(0, 1)
                    filler(l, "df", h, 0, 7, 6, KT)
                    scores(1, 0)
                    scores(1, 1)
                    for t in range(1, TILES):
                        probs_t(t - 1, 0)
                        if t + 1 < TILES:
                            scores(t + 1, 0)
                        if t >= 3:
                            pe.wait_ge(S.df_o, o0 + (t - 1) // 2)
                        if t % 2:
                            scores(t + 1, 1)
                            probs_t(t - 1, 1)
                            filler(l, "df", h, t, 7, 0, 3)
                            probs_t(t - 1, 2)
                            filler(l, "df", h, t, 7, 3, KT)
                        else:
                            filler(l, "df", h, t, 7, 0, 1)
                            probs_t(t - 1, 1)
                            filler(l, "df", h, t, 7, 1, KT)
                            probs_t(t - 1, 2)
                            if t + 1 < TILES:
                                scores(t + 1, 1)
                            values(u, t // 2 - 1, 3 * FILL * (HEADS + h) + t + 1)
                    probs_t(LT, 0)
                values((l + 1) * HEADS - 1, 4, 3 * FILL * 2 * HEADS)
                square_sums((l + 1) * HEADS - 1, (0, 1, 2))
                barrier(pe)

                if l + 1 < DEPTH:
                    for i in range(MOD_AHEAD):
                        modulation(l + 1, i)
                for i in range(3 * KT):
                    b = i // KT
                    job(("b", l, "", i), omh[b], oml[b], (S.o_lo, 3 * BK * l + b * BK) if i % KT == 0 else None)
                    if l + 1 < DEPTH and i + MOD_AHEAD < MODS:
                        modulation(l + 1, i + MOD_AHEAD)
                for m in range(KT):
                    job(("o", l, "", m), hhi, hlo, (S.y_lo, KT * l) if m == 0 else None)
                barrier(pe)
            for t in range(TILES):
                if t >= 2:
                    pe.wait_ge(S.fin_y, t - 1)
                for half in range(2):
                    x = transposed(2 * (t % 2) + half, [xT[:, 4 * half + j, t * P:(t + 1) * P] for j in range(4)])
                x.then_inc(S.fin_tr, 1)

        @block.scalar
        def _(act):
            fn = nc.scalar.activation
            split = [0]

            def split_to(s_end):
                while split[0] < min(s_end, len(SPLIT)):
                    s = split[0]
                    n, kt = CHUNK[SPLIT[s]], chunk_k(SPLIT[s])
                    act.wait_ge(*loaded_no(n))
                    if s >= 2:
                        act.wait_ge(S.w_used, s - 1)
                    fn(whi[:, s % 2, 0:kt, :], wraw[:, n % 2, 0:kt, :], ACT.Copy).then_inc(S.w_hi, 1)
                    split[0] += 1

            def projected(*c):
                split_to(SPLIT_NO[c] + 2)
                act.wait_ge(S.w_used, SPLIT_NO[c] + 1)
                return group(JOB_NO[c] % 2)

            def filled(l, ph, p, i, bank):
                g, n = divmod(i, NC)
                c = ("g", l, "", FILL * (p + (HEADS if ph == "df" else 0)) + g)
                at = l * 3 * KT + c[3]
                if n == 0:
                    split_to(gates_split(l, c[3], 2))
                    if at:
                        act.wait_ge(S.g_store, 16 * at)
                    act.wait_ge(*evacuated("z", l, ph, p))
                if n == NC - 1:
                    act.wait_ge(S.w_used, SPLIT_NO[c] + 1)
                else:
                    act.wait_ge(S.fil_done, (NC - 1) * at + n + 1)
                fn(gst[:, n * CH:(n + 1) * CH], ps[:, bank, 0:CH], ACT.Tanh, scale=0.5).then_inc(S.fil_evac, 1)

            def keys_out(g, outs):
                for out in outs:
                    fn(by_chunk(out[:, 0:2 * CH]), g[:, 0:2], ACT.Copy)
                    fn(out[:, 2 * CH:TL], g[:, 2, 0:TL - 2 * CH], ACT.Copy)
                    x = fn(out[:, TL + PAST:], g[:, 2, TL - 2 * CH:], ACT.Copy)
                return x

            def cached_keys(n, outs):
                act.wait_ge(S.ck_done, n + 1)
                for out in outs:
                    x = fn(out[:, TL:TL + PAST], ps[:, 6, 0:P], ACT.Copy)
                x.then_inc(S.ck_used, 1)

            def gate_tanh(l, ph, p):
                g = projected("z", l, ph, p)
                at = l * 3 * KT + FILL * (p + (HEADS if ph == "df" else 0))
                if at:
                    act.wait_ge(S.g_store, 16 * at)
                fn(by_chunk(gst[:]), g, ACT.Tanh, scale=0.5).then_inc(S.th_ready, 1)
                split_to(SPLIT_NO["z", l, ph, p] + 3)

            def values_out(l, ph, p, vt):
                g = projected("v", l, ph, p)
                fn(by_chunk(vt[:]), g, ACT.Copy).then_inc(S.act_evac, 1)
                split_to(SPLIT_NO["v", l, ph, p] + 3)

            def rows(n, l, ph, p):
                act.wait_ge(S.kv_load, 32 * (n + 1))
                fn(vhi[:, TILES, :], vraw[:], ACT.Copy).then_inc(S.vc_hi, 1)
                act.wait_ge(S.kc_done, n + 1)
                if n:
                    act.wait_ge(S.k_store, 32 * n)
                fn(kout[:], ps[:, 6, 0:P], ACT.Copy).then_inc(S.kc_used, 1)
                for i, (bank, a, b) in enumerate(((7, 0, 4), (6, 4, 8), (7, 8, 9))):
                    act.wait_ge(S.v_done, 3 * n + i + 1)
                    src = ps[:, bank, 0:(b - a) * P].rearrange("p (t n) -> p t n", n=P)
                    if i == 2:
                        fn(vout[:], ps[:, bank, 0:P], ACT.Copy).then_inc(S.v_out, 1)
                    fn(vhi[:, a:b, :], src, ACT.Copy).then_inc(S.v_hi, 1)

            def squares(i, m):
                if m == 0:
                    fn(sqs[:], xT[:, 0, :], ACT.Square).then_inc(S.sq_ready, 1)
                    return
                if m >= 3:
                    act.wait_ge(S.sq_added, (KT - 1) * i + m - 2)
                fn(sq[:, m % 2, :], xT[:, m, :], ACT.Square).then_inc(S.sq_ready, 1)

            act.wait_ge(S.setup_load, 16 * 5)
            fn(cth[:], craw[:], ACT.Tanh, scale=0.5).then_inc(S.cth_ready, 1)
            act.wait_ge(S.lprod_ready, 1)
            fn(lexp[:], lprod[:], ACT.Exp).then_inc(S.cth_ready, 1)
            act.wait_ge(S.xtok_used, 2 * TILES)
            for m in range(KT):
                squares(0, m)
            split_to(2)
            barrier(act)
            for l in range(DEPTH):
                act.wait_ge(S.ss_done, l + 1)
                fn(by_chunk(rstd[:]), group(0), ACT.Ln, bias=eps[:, 0:1], scale=1.0 / D)
                act.drain()
                fn(rstd[:], rstd[:], ACT.Exp, scale=-0.5).then_inc(S.rstd_ready, 1)
                act.wait_ge(S.mod_ready, l + 1)
                for m in range(KT):
                    act.wait_ge(S.t_ready, l * KT + m + 1)
                    for j, (a, b) in enumerate(((0, TL), (TL, T))):
                        x = fn(hhi[:, m, a:b], tn[:, m % 2, a:b], ACT.Identity, bias=modr[:, m, j:j + 1])
                    x.then_inc(S.hi_ready, 1)
                for p in range(HEADS):
                    n, u = 2 * HEADS * l + p, l * HEADS + p
                    g = projected("q", l, "na", p)
                    if p == 0:
                        act.wait_ge(S.store, 16 * (l + 1))
                    fn(by_chunk(xi[:, 0:T]), g, ACT.Copy, scale=0.125)
                    fn(by_chunk(xh[:, 0:T]), g, ACT.Copy, scale=0.125).then_inc(S.act_evac, 1)
                    g = projected("k", l, "na", p)
                    act.wait_ge(S.x_split, 2 * n + 1)
                    act.wait_ge(S.q_placed, 64 * (n + 1))
                    cached_keys(n, (xi, xh))
                    keys_out(g, (xi, xh)).then_inc(S.act_evac, 1)
                    values_out(l, "na", p, vT)
                    rows(n, l, "na", p)
                    gate_tanh(l, "na", p)
                    u0, b0 = u * 2 * TILES, u * NA_BATCHES

                    def exps(t, e):
                        nk = P if t == LT else window(t)[1] * GW + PAST
                        act.wait_ge(S.na_b, u0 + 2 * t + e + 1)
                        fn(sn[:, e, 0:nk], sn[:, e, 0:nk], ACT.Exp, bias=stat[:, e, 2:3],
                           accum_out=stat[:, e, 3:4]).then_inc(S.na_e, 1)

                    def highs(t, e):
                        for k, _, first, count, bank in na_batches(t, e):
                            act.wait_ge(S.na_pt, b0 + k + 1)
                            if e == 0 and first == 0 and t:
                                act.wait_ge(S.na_pv, TILES * u + t)
                            for out, src in na_copies(t, e, first, count, bank, pth):
                                x = fn(out, src, ACT.Copy)
                            x.then_inc(S.na_pth, 1)

                    exps(0, 0)
                    exps(0, 1)
                    for t in range(TILES):
                        highs(t, 0)
                        if t + 1 < TILES:
                            exps(t + 1, 0)
                        highs(t, 1)
                        if t + 1 < TILES:
                            exps(t + 1, 1)
                        filled(l, "na", p, t, 2)
                    split_to(gates_split(l, FILL * p + FILL - 1, 3))
                barrier(act)

                for g in range(HEADS):
                    n = l * HEADS + g
                    for gg in ((0, 1) if g == 0 else (g + 1,) if g + 1 < HEADS else ()):
                        fn(by_chunk(uT[:, gg % 2, :]), projected("u", l, "fn", gg), ACT.Copy).then_inc(S.act_evac, 1)
                    for j in range(4):
                        act.wait_ge(S.u_pair, 5 * n + j + 1)
                        fn(xcs[:, j].rearrange("p a b -> p (a b)"), ps[:, 6 + j % 2, 0:256], ACT.Copy
                           ).then_inc(S.pair_copied, 1)
                    for i in range(2):
                        act.wait_ge(S.x_done, 5 * n + 2 * i + 2)
                        w = (HK + 1) if i == 0 else HK
                        if g:
                            act.wait_ge(S.q_done, 2 * (n - 1) + i + 1)
                        fn(qsb[:, i, 0:w], ps[:, 3 * (g % 2) + 1 if i == 0 else 6, 0:w], ACT.Copy).then_inc(S.q_copied, 1)
                    act.wait_ge(S.x_done, 5 * n + 5)
                    if g:
                        act.wait_ge(S.f_lo, n)
                    fn(ft[:, TL:], ps[:, 7, 0:P], ACT.Copy).then_inc(S.f_ctx, 1)
                    act.drain()
                    act.wait_ge(S.q_done, 2 * n + 2)
                    fn(fhi[:, g, :], ft[:], ACT.Copy).then_inc(S.f_hi, 1)
                for m in range(HEADS):
                    g = projected("z", l, "fn", m)
                    if m:
                        act.wait_ge(*evacuated("w", l, "fn", m - 1))
                    fn(by_chunk(fth[:]), g, ACT.Tanh, scale=0.5).then_inc(S.th_ready, 1)
                    split_to(SPLIT_NO["w", l, "fn", m] + 3)
                barrier(act)

                def head_norm(n, chunks):
                    for c in chunks:
                        act.wait_ge(S.sso_done, NC * n + c + 1)
                        fn(rso[:, c * CH:(c + 1) * CH], ps[:, 6 + c % 2, 0:CH], ACT.Ln, bias=eps[:, 0:1],
                           scale=1.0 / P).then_inc(S.sso_read, 1)
                    if c == NC - 1:
                        act.drain()
                        fn(rso[:], rso[:], ACT.Exp, scale=-0.5).then_inc(S.rso_ready, 1)

                def head_squares(u):
                    act.wait_ge(S.df_o, 5 * (u + 1))
                    act.wait_ge(S.g_store, 16 * (l * 3 * KT + FILL * (HEADS + u % HEADS + 1)))
                    fn(sqo[:], obuf[:], ACT.Square).then_inc(S.sqo_ready, 1)

                for h in range(HEADS):
                    n, u = 2 * HEADS * l + HEADS + h, l * HEADS + h
                    n9, g0 = u * TILES, u * (3 * LT + 1)
                    g = projected("q", l, "df", h)
                    fn(by_chunk(xi_d[:, 0:T]), g, ACT.Copy, scale=0.125).then_inc(S.act_evac, 1)
                    if h:
                        head_squares(u - 1)
                    act.wait_ge(S.rope_done, 2 * u + 1)
                    fn(xh_d[:, 0:T], xi_d[:, 0:T], ACT.Copy).then_inc(S.xh_ready, 1)
                    g = projected("k", l, "df", h)
                    if h:
                        act.wait_ge(S.kc_done, n)
                        act.wait_ge(S.x_split, 2 * n)
                    cached_keys(n, (xk_d,))
                    keys_out(g, (xk_d,)).then_inc(S.act_evac, 1)
                    if h:
                        head_norm(u - 1, (0, 1))
                    act.wait_ge(S.rope_done, 2 * u + 2)
                    act.wait_ge(S.q_placed, 64 * (n + 1))
                    act.wait_ge(S.x_split, 2 * n + 1)
                    fn(xh_d[:], xk_d[:], ACT.Copy).then_inc(S.xh_ready, 1)
                    values_out(l, "df", h, vT_d)
                    if h:
                        head_norm(u - 1, (2,))
                    rows(n, l, "df", h)
                    gate_tanh(l, "df", h)

                    def exps(t, m):
                        nk = TC if t == LT else TL + PAST
                        e = (e1, e2)[m]
                        act.wait_ge(S.df_m, 2 * (n9 + t) + m + 1)
                        if t >= 3 and m == 0:
                            act.wait_ge(S.df_pt, g0 + 3 * (t - 2))
                        fn(e[:, t % (3 - m), 0:nk], flat[:, 1536 * m:1536 * m + nk], ACT.Exp,
                           bias=stat[:, t % 2, m:m + 1], accum_out=stat[:, t % 2, 2 + m:3 + m]).then_inc(S.df_e, 1)

                    def highs(t, g):
                        if t == LT and g:
                            return
                        if g == 0 and t % 2 == 0 and t >= 2:
                            act.wait_ge(S.df_pv, u * 5 + t // 2)
                        act.wait_ge(S.df_pt, g0 + 3 * t + g + 1)
                        w = 3 if t < LT else 1
                        fn(aTh[:, 3 * g:3 * g + w, (t % 2) * P:(t % 2 + 1) * P],
                           ps[:, 6, 0:w * P].rearrange("p (t n) -> p t n", n=P), ACT.Copy).then_inc(S.df_pth, 1)

                    exps(0, 0)
                    exps(0, 1)
                    filled(l, "df", h, 0, 7)
                    exps(1, 0)
                    exps(1, 1)
                    for t in range(1, TILES):
                        highs(t - 1, 0)
                        highs(t - 1, 1)
                        if t + 1 < TILES:
                            exps(t + 1, 0)
                        if t % 2:
                            highs(t - 1, 2)
                            exps(t + 1, 1)
                            filled(l, "df", h, t, 7)
                        else:
                            filled(l, "df", h, t, 7)
                            highs(t - 1, 2)
                            if t + 1 < TILES:
                                exps(t + 1, 1)
                    highs(LT, 0)
                    split_to(gates_split(l, FILL * (HEADS + h) + FILL - 1, 3))
                head_squares((l + 1) * HEADS - 1)
                head_norm((l + 1) * HEADS - 1, (0, 1, 2))
                barrier(act)

                def out_high(i):
                    n = l * 3 * BK + i
                    act.wait_ge(o_load[i % 2], 16 * (n // 2 + 1))
                    fn(omh[i // BK][:, i % BK, :], oraw[:, i % 2, :], ACT.Copy).then_inc(S.o_hi, 1)

                for i in range(BK):
                    out_high(i)

                def y_high(m):
                    act.wait_ge(S.y_added, l * 2 * KT + KT + m + 1)
                    act.wait_ge(S.w_used, SPLIT_NO["b", l, "", 2 * KT - 1] + 1)
                    fn(hhi[:, m, :], ysum[:, m, :], ACT.Copy).then_inc(S.y_hi, 1)

                for i in range(3 * KT):
                    split_to(SPLIT_NO["b", l, "", i] + 2)
                    if i < 2 * BK:
                        out_high(BK + i)
                    if i > 2 * KT:
                        y_high(i - 2 * KT - 1)
                y_high(KT - 1)
                for m in range(KT):
                    split_to(SPLIT_NO["o", l, "", m] + 2)
                    if l + 1 < DEPTH:
                        act.wait_ge(*evacuated("o", l, "", m))
                        squares(l + 1, m)
                split_to(SPLIT_NO["o", l, "", KT - 1] + 3)
                barrier(act)
            for t in range(TILES):
                act.wait_ge(S.fin_tr, t + 1)
                if t >= 2:
                    act.wait_ge(S.fin_y, t - 1)
                act.drain()
                fn(junk[:], flat[:, 1024 * (t % 2):1024 * (t % 2) + D], ACT.Square, accum_out=fss[:, t % 2, 0:1])
                act.drain()
                fn(fss[:, t % 2, 1:2], fss[:, t % 2, 0:1], ACT.Ln, bias=eps[:, 0:1], scale=1.0 / D)
                act.drain()
                fn(fss[:, t % 2, 2:3], fss[:, t % 2, 1:2], ACT.Exp, scale=-0.5).then_inc(S.fin_rs, 1)

        @block.vector
        def _(dve):
            v = nc.vector
            ths = [0]
            dve.wait_ge(S.setup_load, 16 * 5)
            v.memset(ones[:], 1.0)
            v.memset(eps[:], EPS)
            v.tensor_tensor(lammul[:], lamraw[:, :, 0:4:2, :], lamraw[:, :, 1:4:2, :], ALU.mult)
            dve.drain()
            v.tensor_reduce(lprod[:], lammul[:], AX.X, ALU.add).then_inc(S.lprod_ready, 1)
            dve.wait_ge(S.cth_ready, 2)
            v.scalar_tensor_tensor(out=cth[:], in0=cth[:], scalar=1.0, in1=craw[:], op0=ALU.add, op1=ALU.mult)
            v.tensor_tensor(neglam[:], lexp[:, :, 1], lexp[:, :, 0], ALU.subtract)
            dve.drain()
            v.tensor_scalar(csil[:], cth[:], 0.5, None, ALU.mult).then_inc(S.csil_ready, 1)
            for l in range(DEPTH):
                lam_init = 0.8 - 0.6 * math.exp(-0.3 * l)
                v.tensor_scalar(neglam[:, l:l + 1], neglam[:, l:l + 1], -lam_init, None, ALU.add)
                v.tensor_scalar(subg[:, l:l + 1], subg[:, l:l + 1], 1.0 - lam_init, None, ALU.mult)
            for g in range(2 * TILES):
                t, half = divmod(g, 2)
                dve.wait_ge(S.xtok_done, g + 1)
                v.tensor_copy(xT[:, 4 * half:4 * half + 4, t * P:(t + 1) * P],
                              ps[:, g % 2, :].rearrange("p (k n) -> p k n", k=4)).then_inc(S.xtok_used, 1)
            barrier(dve)
            for l in range(DEPTH):
                dve.wait_ge(S.mod_used, (l + 1) * MODS)
                for j in range(2):
                    v.tensor_tensor(modr[:, :, j], ps[:, 7, j:2 * MODS:2], bcol[:, l, :], ALU.add)
                dve.drain()
                for j in range(2):
                    v.scalar_tensor_tensor(out=mul_a[:, :, j], in0=modr[:, KT:2 * KT, j], scalar=1.0, in1=gcol[:, l, :],
                                           op0=ALU.add, op1=ALU.mult)
                v.tensor_scalar(mul_g[:], modr[:, 2 * KT:, :], 0.25, None, ALU.mult).then_inc(S.mod_ready, 1)
                dve.drain()
                dve.wait_ge(S.rstd_ready, l + 1)

                def scaled(m):
                    for j, (a, b) in enumerate(((0, TL), (TL, T))):
                        x = v.scalar_tensor_tensor(out=tn[:, m % 2, a:b], in0=xT[:, m, a:b], scalar=mul_a[:, m, j:j + 1],
                                                   in1=rstd[:, a:b], op0=ALU.mult, op1=ALU.mult)
                    x.then_inc(S.t_ready, 1)

                def h_low(m):
                    dve.wait_ge(S.hi_ready, l * KT + m + 1)
                    for j, (a, b) in enumerate(((0, TL), (TL, T))):
                        x = v.scalar_tensor_tensor(out=hlo[:, m, a:b], in0=tn[:, m % 2, a:b], scalar=modr[:, m, j:j + 1],
                                                   in1=hhi[:, m, a:b].bitcast(F32), op0=ALU.add, op1=ALU.subtract)
                    x.then_inc(S.h_ready, 1)

                scaled(0)
                for m in range(KT):
                    if m + 1 < KT:
                        dve.drain()
                        scaled(m + 1)
                    h_low(m)

                def silu_gate(g, tanh, out):
                    ths[0] += 1
                    dve.wait_ge(S.th_ready, ths[0])
                    v.scalar_tensor_tensor(out=by_chunk(out[:]), in0=by_chunk(tanh[:]), scalar=1.0, in1=g,
                                           op0=ALU.add, op1=ALU.mult).then_inc(S.dve_evac, 1)

                def value_lows(n):
                    for i, (bank, a, b) in enumerate(((7, 0, 4), (6, 4, 8), (7, 8, 9))):
                        dve.wait_ge(S.v_hi, 3 * n + i + 1)
                        src = ps[:, bank, 0:(b - a) * P].rearrange("p (t n) -> p t n", n=P)
                        v.tensor_tensor(vlo[:, a:b, :], src, vhi[:, a:b, :].bitcast(F32), ALU.subtract
                                        ).then_inc(S.v_lo, 1)

                for p in range(HEADS):
                    n, u = 2 * HEADS * l + p, l * HEADS + p
                    u0, b0 = u * 2 * TILES, u * NA_BATCHES
                    value_lows(n)

                    def biased(t, e):
                        st = stat[:, e]
                        c0 = 1536 * e
                        dve.wait_ge(S.na_s, u0 + 2 * t + e + 1)
                        if t:
                            dve.wait_ge(S.na_pt, b0 + na_batches(t - 1, e)[-1][0] + 1)
                        if t == LT:
                            v.tensor_copy(sn[:, e, 0:P], flat[:, c0:c0 + P])
                            v.tensor_reduce(st[:, 0:1], flat[:, c0:c0 + P], AX.X, ALU.max)
                            dve.drain()
                            v.tensor_scalar(st[:, 2:3], st[:, 0:1], -1.0, None, ALU.mult).then_inc(S.na_b, 1)
                            return
                        _, m, at = window(t)
                        nk = m * GW
                        v.tensor_tensor_reduce(out=sn[:, e, 0:nk], in0=flat[:, c0:c0 + nk],
                                               in1=bias[:, e, at:at + m, :].rearrange("p a b -> p (a b)"), scale=1.0,
                                               scalar=-3.0e38, op0=ALU.add, op1=ALU.max, accum_out=st[:, 0:1])
                        v.tensor_scalar(sn[:, e, nk:nk + PAST], flat[:, c0 + nk:c0 + nk + PAST], 1.0, None,
                                        ALU.mult, ALU.max, accum_out=st[:, 1:2])
                        dve.drain()
                        v.tensor_scalar(st[:, 2:3], st[:, 0:1], st[:, 1:2], -1.0, ALU.max, ALU.mult
                                        ).then_inc(S.na_b, 1)

                    def normed(t, e):
                        st = stat[:, e]
                        nk = P if t == LT else window(t)[1] * GW + PAST
                        dve.wait_ge(S.na_e, u0 + 2 * t + e + 1)
                        v.reciprocal(st[:, 4:5], st[:, 3:4])
                        dve.drain()
                        v.tensor_scalar(sn[:, e, 0:nk], sn[:, e, 0:nk], st[:, 4:5], None, ALU.mult
                                        ).then_inc(S.na_p, 1)

                    def lows(t, e):
                        for k, _, first, count, bank in na_batches(t, e):
                            dve.wait_ge(S.na_pth, b0 + k + 1)
                            for (out, src), (hi, _) in zip(na_copies(t, e, first, count, bank, ptl),
                                                           na_copies(t, e, first, count, bank, pth)):
                                x = v.tensor_tensor(out, src, hi.bitcast(F32), ALU.subtract)
                            x.then_inc(S.na_ptc, 1)

                    def gated(t):
                        dve.wait_ge(S.na_pv, TILES * u + t + 1)
                        if t == 0 and n:
                            dve.wait_ge(S.o_store, 16 * n)
                        for e in range(2):
                            r = slice(64 * e, 64 * e + 64)
                            x = v.tensor_tensor(obuf[r, P * t:P * t + P], ps[r, 5, P * e:P * e + P],
                                                zs[r, P * t:P * t + P], ALU.mult)
                        x.then_inc(S.na_o, 1)

                    dve.wait_ge(S.masked, u + 1)
                    biased(0, 0)
                    silu_gate(group(JOB_NO["z", l, "na", p] % 2), gst, zs)
                    normed(0, 0)
                    biased(0, 1)
                    normed(0, 1)
                    for t in range(TILES):
                        if t:
                            gated(t - 1)
                        lows(t, 0)
                        if t + 1 < TILES:
                            biased(t + 1, 0)
                        lows(t, 1)
                        if t + 1 < TILES:
                            biased(t + 1, 1)
                            normed(t + 1, 0)
                            normed(t + 1, 1)
                    gated(LT)
                barrier(dve)

                for g in range(HEADS):
                    n = l * HEADS + g
                    for j in range(5):
                        if j < 4:
                            dve.wait_ge(S.pair_copied, 4 * n + j + 1)
                            hi = ps[:, 6 + j % 2, 256:512]
                            lo = xcs[:, j].rearrange("p a b -> p (a b)")
                            v.tensor_tensor(xsum[:, j].rearrange("p a b -> p (a b)"), lo, hi, ALU.add)
                            v.tensor_tensor(xdif[:, j].rearrange("p a b -> p (a b)"), lo, hi, ALU.subtract
                                            ).then_inc(S.folded, 1)
                        else:
                            dve.wait_ge(S.u_pair, 5 * n + 5)
                            v.tensor_copy(xctx[:].rearrange("p a b -> p (a b)"), ps[:, 6, 0:256]).then_inc(S.folded, 1)
                    if g:
                        dve.wait_ge(S.f_lo, n)
                    for i in range(2):
                        bank = 3 * (g % 2) + 2 * i
                        first = 1 if i == 0 else 0
                        w = (HK + 1) if i == 0 else HK
                        dve.wait_ge(S.q_copied, 2 * n + i + 1)
                        v.tensor_tensor(ft[:, i:i + 2 * w - 1:2], ps[:, bank, 0:w], qsb[:, i, 0:w], ALU.subtract)
                        v.tensor_tensor(ft[:, TL - 2 * first - i:TL // 2:-2], ps[:, bank, first:HK],
                                        qsb[:, i, first:HK], ALU.add).then_inc(S.q_done, 1)
                for m in range(HEADS):
                    silu_gate(group(JOB_NO["z", l, "fn", m] % 2), fth, fzs)
                    dve.drain()
                    dve.wait_ge(S.w_used, SPLIT_NO["w", l, "fn", m] + 1)
                    if m:
                        dve.wait_ge(S.f_store, 16 * (l * HEADS + m))
                    v.tensor_tensor(by_chunk(fout[:]), group(JOB_NO["w", l, "fn", m] % 2), by_chunk(fzs[:]), ALU.mult
                                    ).then_inc(S.dve_evac, 1)
                barrier(dve)

                def head_out(u):
                    dve.wait_ge(S.rso_ready, u + 1)
                    v.scalar_tensor_tensor(out=obuf[:], in0=obuf[:], scalar=subg[:, l:l + 1], in1=rso[:],
                                           op0=ALU.mult, op1=ALU.mult)
                    dve.drain()
                    v.tensor_tensor(obuf[:], obuf[:], zs[:], ALU.mult).then_inc(S.out_ready, 1)

                dve.wait_ge(S.rope_load, 32 * (l + 1))
                for h in range(HEADS):
                    n, u = 2 * HEADS * l + HEADS + h, l * HEADS + h
                    n9 = u * TILES
                    for r in range(2):
                        x = (xi_d, xk_d)[r]
                        dve.wait_ge(*evacuated("qk"[r], l, "df", h))
                        v.stream_shuffle(xr[:, 0:TL], x[:, 0:TL], [(i + 16) % 32 for i in range(32)])
                        dve.drain()
                        v.tensor_tensor(xr[:, 0:TL], xr[:, 0:TL], sinT[:], ALU.mult)
                        v.tensor_tensor(xc[:, 0:TL], x[:, 0:TL], cosT[:], ALU.mult)
                        dve.drain()
                        v.tensor_tensor(x[:, 0:TL], xc[:, 0:TL], xr[:, 0:TL], ALU.add).then_inc(S.rope_done, 1)
                    if h:
                        head_out(u - 1)
                    value_lows(n)

                    def maxes(t, m):
                        nk = TC if t == LT else TL + PAST
                        dve.wait_ge(S.df_s, 2 * (n9 + t) + m + 1)
                        v.tensor_reduce(stat[:, t % 2, m:m + 1], flat[:, 1536 * m:1536 * m + nk], AX.X, ALU.max,
                                        negate=True).then_inc(S.df_m, 1)

                    def scaled_e2(t):
                        st = stat[:, t % 2]
                        nk = TC if t == LT else TL + PAST
                        dve.wait_ge(S.df_e, 2 * (n9 + t) + 2)
                        v.reciprocal(st[:, 4:6], st[:, 2:4])
                        dve.drain()
                        v.tensor_scalar(e2[:, t % 2, 0:nk], e2[:, t % 2, 0:nk], st[:, 5:6], neglam[:, l:l + 1],
                                        ALU.mult, ALU.mult)

                    def combined(t):
                        st = stat[:, t % 2]
                        nk = TC if t == LT else TL + PAST
                        dve.drain()
                        v.scalar_tensor_tensor(out=e1[:, t % 3, 0:nk], in0=e1[:, t % 3, 0:nk], scalar=st[:, 4:5],
                                               in1=e2[:, t % 2, 0:nk], op0=ALU.mult, op1=ALU.add).then_inc(S.df_p, 1)

                    def lows(t, g):
                        if t == LT and g:
                            return
                        dve.wait_ge(S.df_pth, u * (3 * LT + 1) + 3 * t + g + 1)
                        w = 3 if t < LT else 1
                        at = (slice(None), slice(3 * g, 3 * g + w), slice((t % 2) * P, (t % 2 + 1) * P))
                        v.tensor_tensor(aTl[at], ps[:, 6, 0:w * P].rearrange("p (t n) -> p t n", n=P),
                                        aTh[at].bitcast(F32), ALU.subtract).then_inc(S.df_ptc, 1)

                    def out_pair(pair):
                        w = 2 * P if pair < 4 else P
                        dve.wait_ge(S.df_pv, 5 * u + pair + 1)
                        if pair == 0:
                            dve.wait_ge(S.o_store, 16 * n)
                        v.tensor_copy(obuf[:, 2 * P * pair:2 * P * pair + w], ps[:, 7, 0:w]).then_inc(S.df_o, 1)

                    maxes(0, 0)
                    silu_gate(group(JOB_NO["z", l, "df", h] % 2), gst, zs)
                    maxes(0, 1)
                    maxes(1, 0)
                    scaled_e2(0)
                    combined(0)
                    maxes(1, 1)
                    for t in range(1, TILES):
                        lows(t - 1, 0)
                        if t % 2:
                            maxes(t + 1, 0)
                            scaled_e2(t)
                            lows(t - 1, 1)
                            maxes(t + 1, 1)
                            lows(t - 1, 2)
                            combined(t)
                        else:
                            scaled_e2(t)
                            lows(t - 1, 1)
                            if t + 1 < TILES:
                                maxes(t + 1, 0)
                            combined(t)
                            lows(t - 1, 2)
                            if t + 1 < TILES:
                                maxes(t + 1, 1)
                            out_pair(t // 2 - 1)
                    lows(LT, 0)
                    out_pair(4)
                head_out((l + 1) * HEADS - 1)
                barrier(dve)

                def out_low(i):
                    dve.wait_ge(S.o_hi, l * 3 * BK + i + 1)
                    v.tensor_tensor(oml[i // BK][:, i % BK, :], oraw[:, i % 2, :],
                                    omh[i // BK][:, i % BK, :].bitcast(F32), ALU.subtract).then_inc(S.o_lo, 1)

                for i in range(BK):
                    out_low(i)

                def y_low(m):
                    dve.wait_ge(S.y_hi, l * KT + m + 1)
                    v.tensor_tensor(hlo[:, m, :], ysum[:, m, :], hhi[:, m, :].bitcast(F32), ALU.subtract
                                    ).then_inc(S.y_lo, 1)

                for i in range(3 * KT):
                    b, m = divmod(i, KT)
                    n = l * 3 * KT + i
                    dve.wait_ge(g_load[n % 3], 16 * (n // 3 + 1))
                    dve.wait_ge(S.w_used, SPLIT_NO["b", l, "", i] + 1)
                    out = ysum[:, m, :] if b == 0 else gth[:, i % 3, :]
                    v.scalar_tensor_tensor(out=by_chunk(out), in0=by_chunk(gth[:, i % 3, :]), scalar=1.0,
                                           in1=group(JOB_NO["b", l, "", i] % 2), op0=ALU.add, op1=ALU.mult
                                           ).then_inc(S.dve_evac, 1)
                    if i < 2 * BK:
                        out_low(BK + i)
                    if i >= 2 * KT + 2:
                        y_low(i - 2 * KT - 2)
                y_low(KT - 2)
                y_low(KT - 1)
                for m in range(KT):
                    n = l * KT + m
                    dve.wait_ge(S.w_used, SPLIT_NO["o", l, "", m] + 1)
                    dve.wait_ge(x_load[m % 2], 16 * (n // 2 + 1))
                    g = group(JOB_NO["o", l, "", m] % 2)
                    for src, lo, hi, j in ((g[:, 0:2], 0, 2 * CH, 0), (g[:, 2, 0:TL - 2 * CH], 2 * CH, TL, 0),
                                           (g[:, 2, TL - 2 * CH:], TL, T, 1)):
                        o, r = xT[:, m, lo:hi], xold[:, m % 2, lo:hi]
                        if lo == 0:
                            o, r = by_chunk(o), by_chunk(r)
                        x = v.scalar_tensor_tensor(out=o, in0=src, scalar=mul_g[:, m, j:j + 1], in1=r,
                                                   op0=ALU.mult, op1=ALU.add)
                    x.then_inc(S.dve_evac, 1)
                barrier(dve)
            dve.wait_ge(S.fg_load, 16)
            for t in range(TILES):
                dve.wait_ge(S.fin_rs, t + 1)
                if t >= 2:
                    dve.wait_ge((S.fin_st0, S.fin_st1)[t % 2], 16 * (t // 2))
                v.scalar_tensor_tensor(out=yb[:, t % 2, :], in0=flat[:, 1024 * (t % 2):1024 * (t % 2) + D],
                                       scalar=fss[:, t % 2, 2:3], in1=fg[:], op0=ALU.mult, op1=ALU.mult
                                       ).then_inc(S.fin_y, 1)

        @block.gpsimd
        def _(pool):
            g_ = nc.gpsimd
            split = [0]

            def split_to(s_end):
                while split[0] < min(s_end, len(SPLIT)):
                    s = split[0]
                    n, kt = CHUNK[SPLIT[s]], chunk_k(SPLIT[s])
                    pool.wait_ge(S.w_hi, s + 1)
                    g_.tensor_tensor(wlo[:, s % 2, 0:kt, :], wraw[:, n % 2, 0:kt, :],
                                     whi[:, s % 2, 0:kt, :].bitcast(F32), ALU.subtract).then_inc(S.w_lo, 1)
                    split[0] += 1

            def add_squares(i):
                for m in range(1, KT):
                    if m >= 2:
                        pool.drain()
                    pool.wait_ge(S.sq_ready, i * KT + m + 1)
                    g_.tensor_tensor(sqs[:], sqs[:], sq[:, m % 2, :], ALU.add).then_inc(S.sq_added, 1)
                    yield m

            g_.memset(ident[:], 0.0)
            pool.drain()
            g_.affine_select(out=ident[:], in_=ident[:], compare_op=ALU.not_equal, fill=1.0, base=0,
                             pattern=[[-1, P]], channel_multiplier=1).then_inc(S.setup_done, 1)
            for _ in add_squares(0):
                pass
            split_to(2)
            barrier(pool)
            for l in range(DEPTH):
                for ph in ("na", "fn", "df"):
                    for p in range(HEADS):
                        n = 2 * HEADS * l + (HEADS if ph == "df" else 0) + p
                        if ph == "fn":
                            split_to(SPLIT_NO["u", l, ph, 0] + min(p, 2) + 3)
                            pool.wait_ge(S.f_hi, l * HEADS + p + 1)
                            g_.tensor_tensor(flo[:, p, :], ft[:], fhi[:, p, :].bitcast(F32), ALU.subtract
                                             ).then_inc(S.f_lo, 1)
                            continue
                        for r in range(2):
                            x0, x1, x2 = (xi, xh, xl) if ph == "na" else ((xi_d, xk_d)[r], xh_d, xl_d)
                            split_to(SPLIT_NO["kv"[r], l, ph, p] + 2)
                            if ph == "na":
                                pool.wait_ge(*evacuated("qk"[r], l, ph, p))
                            else:
                                pool.wait_ge(S.xh_ready, 2 * (l * HEADS + p) + r + 1)
                            w = (T, TK)[r]
                            if r:
                                pool.wait_ge(S.q_placed, 64 * (n + 1))
                            g_.tensor_tensor(x2[:, 0:w], x0[:, 0:w], x1[:, 0:w].bitcast(F32), ALU.subtract
                                             ).then_inc(S.x_split, 1)
                        if ph == "na":
                            u = l * HEADS + p
                            pool.wait_ge(S.mask_load, 16 * (l + 1))
                            pool.wait_ge(S.bias_load, 128 * (u + 1))
                            for e in range(2):
                                x = g_.tensor_tensor(bias[:, e], bias[:, e], mask[:], ALU.add)
                            x.then_inc(S.masked, 1)
                        pool.wait_ge(S.vc_hi, n + 1)
                        g_.tensor_tensor(vlo[:, TILES, :], vraw[:], vhi[:, TILES, :].bitcast(F32), ALU.subtract
                                         ).then_inc(S.vc_lo, 1)
                        split_to(SPLIT_NO["z", l, ph, p] + 2)
                        for i in range(FILL):
                            split_to(gates_split(l, FILL * (p + (HEADS if ph == "df" else 0)) + i, 2))
                        split_to(gates_split(l, FILL * (p + (HEADS if ph == "df" else 0)) + FILL - 1, 3))
                    if ph == "fn":
                        split_to(SPLIT_NO["w", l, ph, HEADS - 1] + 3)
                    barrier(pool)
                for i in range(3 * KT):
                    split_to(SPLIT_NO["b", l, "", i] + 2)
                    if i >= KT:
                        pool.wait_ge(*evacuated("b", l, "", i))
                        g_.tensor_tensor(ysum[:, i % KT, :], ysum[:, i % KT, :], gth[:, i % 3, :], ALU.add
                                         ).then_inc(S.y_added, 1)
                adds = add_squares(l + 1)
                for m in range(KT):
                    split_to(SPLIT_NO["o", l, "", m] + 2)
                    if l + 1 < DEPTH and m:
                        next(adds)
                split_to(SPLIT_NO["o", l, "", KT - 1] + 3)
                barrier(pool)


def dft_tables():
    c = np.arange(P)
    ang = 2 * np.pi * (np.outer(c, c) % P) / P
    chan = np.stack([np.cos(ang), np.sin(ang)], 1) / np.sqrt(P)
    ctx = np.stack([np.cos(ang), -np.sin(ang)], 1) / np.sqrt(P)
    tok = np.zeros((4, P, 4, TL // 4 + 2))
    t = np.arange(TL // 2)
    for i in range(4):
        odd = i // 2
        k = 2 * np.arange(TL // 4 + 1 - odd) + odd
        ang = 2 * np.pi * (np.outer(t, k) % TL) / TL
        tok[:, :, i, :len(k)] = ((np.sin if i % 2 else np.cos)(ang) / np.sqrt(TL)).reshape(4, P, len(k))
    return [np.ascontiguousarray(a, np.float32) for a in (chan, ctx, tok.transpose(1, 0, 2, 3))]


def rope_tables():
    t = np.arange(TL)
    inv = (np.float32(10000.0) ** (-np.arange(0, 32, 2, dtype=np.float32) / np.float32(32))).astype(np.float32)
    d = np.arange(P) % 64
    where = np.where((d < 32)[:, None], (t // GW)[None], (t % GW)[None]).astype(np.float32)
    ang = where * inv[d % 16][:, None]
    sign = np.where(d % 32 < 16, -1.0, 1.0)[:, None]
    return np.stack([np.cos(ang), np.sin(ang) * sign]).astype(np.float32)


def window_mask():
    c = np.arange(GW)
    start = np.clip(c - 8, 0, GW - 16)
    out = (c[None] < start[:, None]) | (c[None] >= start[:, None] + 16)
    m = np.zeros((2, GW, NS + NI, GW), bool) | out[None, :, None, :]
    m[0, :, NS + I_MAX - I_MIN] = True
    m[1, :, NS] = True
    return np.where(m, np.float32(-1e30), np.float32(0)).reshape(P, NS + NI, GW)


def kernel(x_prompt, x_sample, cache_na_k, cache_na_v, cache_diff_k, cache_diff_v, c, c_ctx, norm_g, w_mod, b_mod,
           w_in, na_rpb, fnet_w, diff_lq1, diff_lk1, diff_lq2, diff_lk2, diff_subln_g, w_branch, w_out, final_g):
    import concourse.bacc as bacc
    from concourse.bass_utils import run_bass_kernel_spmd

    arr = np.asarray
    padded = np.zeros((DEPTH, 8, 15, PADW), np.float32)
    padded[..., GW - 16:GW + 15] = arr(na_rpb)
    rpb = np.stack([padded[..., GW - 1 - q:2 * GW - 1 - q] for q in range(GW)], 2)
    tables = dft_tables()
    ins = {
        "x_prompt": arr(x_prompt), "x_sample": arr(x_sample), "cache_na_k": arr(cache_na_k),
        "cache_na_v": arr(cache_na_v), "cache_diff_k": arr(cache_diff_k), "cache_diff_v": arr(cache_diff_v),
        "cvec": np.stack([arr(c)[0].reshape(KT, P).T, arr(c_ctx).reshape(KT, P).T], -1),
        "norm_g": arr(norm_g).reshape(DEPTH, KT, P).transpose(2, 0, 1),
        "w_mod": arr(w_mod), "b_mod": arr(b_mod).reshape(DEPTH, MODS, P).transpose(2, 0, 1), "w_in": arr(w_in),
        "rpb": rpb, "fnet_w": arr(fnet_w),
        "lams": np.stack([arr(diff_lq1), arr(diff_lk1), arr(diff_lq2), arr(diff_lk2)], 1),
        "subln_g": arr(diff_subln_g).T, "w_branch": arr(w_branch), "w_out": arr(w_out), "final_g": arr(final_g),
        "na_mask": window_mask(), "rope": rope_tables(), "dft_c": tables[0], "dft_x": tables[1], "dft_t": tables[2],
    }
    ins = {k: np.ascontiguousarray(v) for k, v in ins.items()}
    outs = {
        "y_prompt": (1, TC, D), "y_sample": (1, TL, D), "new_na_k": (1, DEPTH, 8, TC, 64),
        "new_na_v": (1, DEPTH, 8, TC, 64), "new_diff_k": (1, DEPTH, HEADS, TC, P), "new_diff_v": (1, DEPTH, HEADS, TC, P),
    }
    nc = bacc.Bacc("TRN2", target_bir_lowering=False, num_devices=1)
    args = [nc.dram_tensor(n, a.shape, F32, kind="ExternalInput").ap() for n, a in ins.items()]
    args += [nc.dram_tensor(n, s, F32, kind="ExternalOutput").ap() for n, s in outs.items()]
    args.append(nc.dram_tensor("xs_dram", (KT, P, T), F32, kind="Internal").ap())
    args.append(nc.dram_tensor("outs_dram", (3, BK, P, T), F32, kind="Internal").ap())
    args.append(nc.dram_tensor("gates_dram", (3 * KT, P, T), F32, kind="Internal").ap())
    build(nc, *args)
    r = run_bass_kernel_spmd(nc, [ins], core_ids=[0]).results[0]
    return tuple(r[n] for n in outs)
```
